# Optimizing a Trainium2 kernel written in Bass

```python
import math
import jax, jax.numpy as jnp
from jax import lax
import numpy as np

D_MODEL = 1024
BATCH = 1
SEQ = 4096
DEPTH = 1
DEC_BATCH = 8
DEC_SEQ = 16
PAST_LEN = 1024

CHUNK = 64
SSD_WIDTH = D_MODEL // 2
SSD_HEAD_DIM = 64
SSD_HEADS = SSD_WIDTH // SSD_HEAD_DIM
SSD_GROUPS = 2
SSD_HEADS_PER_GROUP = SSD_HEADS // SSD_GROUPS
SSD_STATE = 128
CONV_WIDTH = 4
CONV_DIM = SSD_WIDTH + 2 * SSD_GROUPS * SSD_STATE
GMLP_WIDTH = D_MODEL - SSD_WIDTH
GMLP_GROUPS = 8
GMLP_GROUP_DIM = GMLP_WIDTH // GMLP_GROUPS
GMLP_CHUNK = 128
IN_PROJ = SSD_WIDTH + CONV_DIM + SSD_HEADS + 2 * GMLP_WIDTH
N_EXPERT_GROUPS = 4
EXPERTS_PER_GROUP = 8
N_EXPERTS = N_EXPERT_GROUPS * EXPERTS_PER_GROUP
TOP_K_IN_GROUP = 2
D_EXPERT = 256
MOE_BLOCK = 128
EPS = 1e-6

kernel_name = "hybrid_ssd_gmlp_hmoe_stream_step"

def rms_norm(x, g):
    xf = x.astype(jnp.float32)
    y = xf * lax.rsqrt(jnp.mean(xf * xf, axis=-1, keepdims=True) + EPS)
    return (y * g.astype(jnp.float32)).astype(x.dtype)

def layer_norm(x, g, b):
    xf = x.astype(jnp.float32)
    mu = jnp.mean(xf, axis=-1, keepdims=True)
    var = jnp.mean(jnp.square(xf - mu), axis=-1, keepdims=True)
    y = (xf - mu) * lax.rsqrt(var + EPS) * g.astype(jnp.float32) + b.astype(jnp.float32)
    return y.astype(x.dtype)

def causal_conv(xbc, prev, w, b):
    l = xbc.shape[1]
    xpad = jnp.concatenate([prev.astype(xbc.dtype), xbc], axis=1)
    out = b.astype(xbc.dtype) + sum(xpad[:, k:k + l] * w[k].astype(xbc.dtype) for k in range(CONV_WIDTH))
    return jax.nn.silu(out), xpad[:, -(CONV_WIDTH - 1):]

def ssd_scan(x, dt, a, bmat, cmat, h0, chunk):
    bsz, l = x.shape[:2]
    nc = l // chunk
    G, R, P, N = SSD_GROUPS, SSD_HEADS_PER_GROUP, SSD_HEAD_DIM, SSD_STATE
    f32 = jnp.float32
    xr = x.reshape(bsz, nc, chunk, G, R, P).astype(f32)
    dtr = dt.reshape(bsz, nc, chunk, G, R).astype(f32)
    bm = bmat.reshape(bsz, nc, chunk, G, N).astype(f32)
    cm = cmat.reshape(bsz, nc, chunk, G, N).astype(f32)
    a_dt = jnp.moveaxis(dtr * a.reshape(G, R).astype(f32), 2, -1)
    a_cs = jnp.cumsum(a_dt, axis=-1)
    xdt = xr * dtr[..., None]
    mask = jnp.tril(jnp.ones((chunk, chunk), dtype=bool))
    seg = a_cs[..., :, None] - a_cs[..., None, :]
    decay = jnp.where(mask, jnp.exp(jnp.where(mask, seg, 0.0)), 0.0)
    cb = jnp.einsum("bclgn,bcsgn->bcgls", cm, bm)
    y_diag = jnp.einsum("bcgls,bcgrls,bcsgrp->bclgrp", cb, decay, xdt)
    decay_to_end = jnp.exp(a_cs[..., -1:] - a_cs)
    chunk_states = jnp.einsum("bcsgn,bcgrs,bcsgrp->bcgrpn", bm, decay_to_end, xdt)
    chunk_decay = jnp.exp(a_cs[..., -1])

    def step(h, inp):
        st, dec = inp
        return h * dec[..., None, None] + st, h

    h_final, h_prev = lax.scan(step, h0.astype(f32),
                               (jnp.moveaxis(chunk_states, 1, 0), jnp.moveaxis(chunk_decay, 1, 0)))
    h_prev = jnp.moveaxis(h_prev, 0, 1)
    y_off = jnp.einsum("bclgn,bcgrpn,bcgrl->bclgrp", cm, h_prev, jnp.exp(a_cs))
    y = (y_diag + y_off).reshape(bsz, l, SSD_HEADS, P)
    return y, h_final

def hier_moe(h, w_rg, b_rg, w_re, b_re, w_gate, w_up, w_down):
    T = h.shape[0]
    f32 = jnp.float32
    hf = h.astype(f32)
    g_logits = hf @ w_rg.astype(f32) + b_rg.astype(f32)
    g_prob = jax.nn.softmax(g_logits, axis=-1)
    g_sel = jnp.argmax(g_logits, axis=-1)
    p_group = jnp.take_along_axis(g_prob, g_sel[:, None], axis=1)
    e_logits = (hf @ w_re.astype(f32) + b_re.astype(f32)).reshape(T, N_EXPERT_GROUPS, EXPERTS_PER_GROUP)
    e_sel_logits = jnp.take_along_axis(e_logits, g_sel[:, None, None], axis=1)[:, 0]
    top_val, top_idx = lax.top_k(e_sel_logits, TOP_K_IN_GROUP)
    weights = p_group * jax.nn.softmax(top_val, axis=-1)
    expert_idx = (g_sel[:, None] * EXPERTS_PER_GROUP + top_idx).astype(jnp.int32)

    S = T * TOP_K_IN_GROUP
    flat_e = expert_idx.reshape(S)
    flat_w = weights.reshape(S)
    order = jnp.argsort(flat_e)
    sorted_e = flat_e[order]
    counts = jnp.bincount(flat_e, length=N_EXPERTS)
    padded = (counts + MOE_BLOCK - 1) // MOE_BLOCK * MOE_BLOCK
    start = jnp.cumsum(counts) - counts
    pend = jnp.cumsum(padded)
    pstart = pend - padded
    dest = pstart[sorted_e] + jnp.arange(S, dtype=jnp.int32) - start[sorted_e]
    n_blocks = (S + MOE_BLOCK - 1) // MOE_BLOCK + N_EXPERTS
    n_slots = n_blocks * MOE_BLOCK
    slot_tok = jnp.full((n_slots,), T, jnp.int32).at[dest].set((order // TOP_K_IN_GROUP).astype(jnp.int32))
    slot_w = jnp.zeros((n_slots,), f32).at[dest].set(flat_w[order])
    block_e = jnp.minimum(jnp.searchsorted(pend, jnp.arange(n_blocks) * MOE_BLOCK, side="right"), N_EXPERTS - 1)
    h_pad = jnp.concatenate([h, jnp.zeros((1, h.shape[1]), h.dtype)], axis=0)

    def run_block(args):
        toks, e = args
        xb = h_pad[toks]
        return (jax.nn.silu(xb @ w_gate[e]) * (xb @ w_up[e])) @ w_down[e]

    ys = lax.map(run_block, (slot_tok.reshape(n_blocks, MOE_BLOCK), block_e))
    ys = ys.reshape(n_slots, -1) * slot_w[:, None].astype(ys.dtype)
    out = jnp.zeros((T + 1, ys.shape[1]), ys.dtype).at[slot_tok].add(ys)[:T]
    return out.astype(h.dtype)

def layer_forward(x, conv_prev, ssm_prev, norm1_g, w_in, conv_w, conv_b, dt_bias, a_log, d_skip,
                  ssm_norm_g, ln_v_g, ln_v_b, w_spatial, b_spatial, w_out, norm2_g,
                  w_rg, b_rg, w_re, b_re, w_gate, w_up, w_down):
    bsz, l = x.shape[:2]
    h = rms_norm(x, norm1_g)
    proj = h @ w_in.astype(h.dtype)
    z, xbc, dt_raw, gu, gv = jnp.split(
        proj, [SSD_WIDTH, SSD_WIDTH + CONV_DIM, SSD_WIDTH + CONV_DIM + SSD_HEADS,
               SSD_WIDTH + CONV_DIM + SSD_HEADS + GMLP_WIDTH], axis=-1)
    xbc_act, conv_new = causal_conv(xbc, conv_prev, conv_w, conv_b)
    xs, bm, cm = jnp.split(xbc_act, [SSD_WIDTH, SSD_WIDTH + SSD_GROUPS * SSD_STATE], axis=-1)
    dt = jax.nn.softplus(dt_raw.astype(jnp.float32) + dt_bias.astype(jnp.float32))
    a = -jnp.exp(a_log.astype(jnp.float32))
    h0 = ssm_prev.reshape(bsz, SSD_GROUPS, SSD_HEADS_PER_GROUP, SSD_HEAD_DIM, SSD_STATE)
    xh = xs.reshape(bsz, l, SSD_HEADS, SSD_HEAD_DIM)
    y, h_final = ssd_scan(xh, dt, a, bm.reshape(bsz, l, SSD_GROUPS, SSD_STATE),
                          cm.reshape(bsz, l, SSD_GROUPS, SSD_STATE), h0, min(CHUNK, l))
    y = y + xh.astype(jnp.float32) * d_skip.astype(jnp.float32)[:, None]
    gated = (y.reshape(bsz, l, SSD_WIDTH) * jax.nn.silu(z.astype(jnp.float32)))
    gated = gated.reshape(bsz, l, SSD_GROUPS, SSD_WIDTH // SSD_GROUPS)
    gated = gated * lax.rsqrt(jnp.mean(gated * gated, axis=-1, keepdims=True) + EPS)
    ssd_out = (gated.reshape(bsz, l, SSD_WIDTH) * ssm_norm_g.astype(jnp.float32)).astype(x.dtype)
    gu = jax.nn.gelu(gu)
    gv = layer_norm(jax.nn.gelu(gv), ln_v_g, ln_v_b)
    span = min(GMLP_CHUNK, l)
    nc = l // span
    w_s = jnp.tril(w_spatial[:, :span, :span]).astype(gv.dtype)
    v = gv.reshape(bsz, nc, span, GMLP_GROUPS, GMLP_GROUP_DIM)
    mixed = jnp.einsum("hts,bcshd->bcthd", w_s, v) + b_spatial[:, :span].T.astype(gv.dtype)[None, None, :, :, None]
    gmlp_out = (gu * mixed.reshape(bsz, l, GMLP_WIDTH)).astype(x.dtype)
    x = x + jnp.concatenate([ssd_out, gmlp_out], axis=-1) @ w_out.astype(x.dtype)
    h2 = rms_norm(x, norm2_g).reshape(bsz * l, D_MODEL)
    x = x + hier_moe(h2, w_rg, b_rg, w_re, b_re, w_gate, w_up, w_down).reshape(bsz, l, D_MODEL)
    ssm_new = h_final.reshape(bsz, SSD_HEADS, SSD_HEAD_DIM, SSD_STATE)
    return x, conv_new, ssm_new, gv

def setup_inputs(seed: int = 0) -> dict:
    key = jax.random.key(seed)
    ks = jax.random.split(key, 32)
    f32 = jnp.float32

    def nrm(k, shape, scale):
        return jax.random.normal(k, shape, f32) * scale

    dt0 = jnp.exp(jax.random.uniform(ks[6], (DEPTH, SSD_HEADS), f32, math.log(1e-3), math.log(1e-1)))
    return {
        "x_prompt": nrm(ks[0], (BATCH, SEQ, D_MODEL), 1.0),
        "x_sample": nrm(ks[1], (DEC_BATCH, DEC_SEQ, D_MODEL), 1.0),
        "cache_conv": nrm(ks[2], (DEPTH, DEC_BATCH, CONV_WIDTH - 1, CONV_DIM), 1.0),
        "state_ssm": nrm(ks[3], (DEPTH, DEC_BATCH, SSD_HEADS, SSD_HEAD_DIM, SSD_STATE), 0.5),
        "norm1_g": 1.0 + nrm(ks[4], (DEPTH, D_MODEL), 0.05),
        "w_in": nrm(ks[5], (DEPTH, D_MODEL, IN_PROJ), D_MODEL ** -0.5),
        "conv_w": nrm(ks[7], (DEPTH, CONV_WIDTH, CONV_DIM), CONV_WIDTH ** -0.5),
        "conv_b": nrm(ks[8], (DEPTH, CONV_DIM), 0.02),
        "dt_bias": dt0 + jnp.log(-jnp.expm1(-dt0)),
        "a_log": jnp.log(jax.random.uniform(ks[9], (DEPTH, SSD_HEADS), f32, 1.0, 16.0)),
        "d_skip": 1.0 + nrm(ks[10], (DEPTH, SSD_HEADS), 0.1),
        "ssm_norm_g": 1.0 + nrm(ks[11], (DEPTH, SSD_WIDTH), 0.05),
        "ln_v_g": 1.0 + nrm(ks[12], (DEPTH, GMLP_WIDTH), 0.05),
        "ln_v_b": nrm(ks[13], (DEPTH, GMLP_WIDTH), 0.02),
        "w_spatial": nrm(ks[14], (DEPTH, GMLP_GROUPS, GMLP_CHUNK, GMLP_CHUNK), GMLP_CHUNK ** -0.5),
        "b_spatial": 1.0 + nrm(ks[15], (DEPTH, GMLP_GROUPS, GMLP_CHUNK), 0.1),
        "w_out": nrm(ks[16], (DEPTH, D_MODEL, D_MODEL), D_MODEL ** -0.5),
        "norm2_g": 1.0 + nrm(ks[17], (DEPTH, D_MODEL), 0.05),
        "w_router_group": nrm(ks[18], (DEPTH, D_MODEL, N_EXPERT_GROUPS), D_MODEL ** -0.5),
        "b_router_group": nrm(ks[19], (DEPTH, N_EXPERT_GROUPS), 0.01),
        "w_router_expert": nrm(ks[20], (DEPTH, D_MODEL, N_EXPERTS), D_MODEL ** -0.5),
        "b_router_expert": nrm(ks[21], (DEPTH, N_EXPERTS), 0.01),
        "w_gate": nrm(ks[22], (DEPTH, N_EXPERTS, D_MODEL, D_EXPERT), D_MODEL ** -0.5),
        "w_up": nrm(ks[23], (DEPTH, N_EXPERTS, D_MODEL, D_EXPERT), D_MODEL ** -0.5),
        "w_down": nrm(ks[24], (DEPTH, N_EXPERTS, D_EXPERT, D_MODEL), D_EXPERT ** -0.5),
        "final_norm_g": 1.0 + nrm(ks[25], (D_MODEL,), 0.05),
    }

def reference(x_prompt, x_sample, cache_conv, state_ssm, norm1_g, w_in, conv_w, conv_b, dt_bias, a_log,
              d_skip, ssm_norm_g, ln_v_g, ln_v_b, w_spatial, b_spatial, w_out, norm2_g,
              w_router_group, b_router_group, w_router_expert, b_router_expert,
              w_gate, w_up, w_down, final_norm_g):
    yp, ys = x_prompt, x_sample
    conv_p, ssm_p, conv_s, ssm_s, v_s = [], [], [], [], []
    for i in range(DEPTH):
        lw = (norm1_g[i], w_in[i], conv_w[i], conv_b[i], dt_bias[i], a_log[i], d_skip[i], ssm_norm_g[i],
              ln_v_g[i], ln_v_b[i], w_spatial[i], b_spatial[i], w_out[i], norm2_g[i],
              w_router_group[i], b_router_group[i], w_router_expert[i], b_router_expert[i],
              w_gate[i], w_up[i], w_down[i])
        conv0 = jnp.zeros((yp.shape[0], CONV_WIDTH - 1, CONV_DIM), yp.dtype)
        ssm0 = jnp.zeros((yp.shape[0], SSD_HEADS, SSD_HEAD_DIM, SSD_STATE), jnp.float32)
        yp, cp, hp, _ = layer_forward(yp, conv0, ssm0, *lw)
        ys, cs, hs, vs = layer_forward(ys, cache_conv[i], state_ssm[i], *lw)
        conv_p.append(cp)
        ssm_p.append(hp)
        conv_s.append(cs)
        ssm_s.append(hs)
        v_s.append(vs)
    y_prompt = rms_norm(yp, final_norm_g)
    y_sample = rms_norm(ys, final_norm_g)
    conv_prompt = jnp.stack(conv_p)
    ssm_prompt = jnp.stack(ssm_p)
    conv_sample = jnp.stack(conv_s)
    ssm_sample = jnp.stack(ssm_s)
    gmlp_v_sample = jnp.stack(v_s)
    return (y_prompt, y_sample, conv_prompt, ssm_prompt, conv_sample, ssm_sample, gmlp_v_sample)


_drawn_inputs = setup_inputs


def setup_inputs(seed=0):
    import zlib

    import numpy as np

    out = dict(_drawn_inputs(seed))
    spreads = {}
    factors = {'ln_v_b': 2.873, 'b_router_group': 5.424, 'b_router_expert': 6.399}
    for name, (base, spread) in spreads.items():
        noise = np.random.default_rng([zlib.crc32(name.encode()), seed]).standard_normal(out[name].shape)
        drawn = base * np.exp(spread * noise) if base else spread * noise
        out[name] = __import__('jax').numpy.asarray(drawn.astype(out[name].dtype))
    for name, factor in factors.items():
        out[name] = (out[name] * factor).astype(out[name].dtype)
    return out
```

```python
from contextlib import ExitStack

import concourse.bass as bass
from concourse import mybir

F32 = mybir.dt.float32
I32 = mybir.dt.int32
U32 = mybir.dt.uint32
ALU = mybir.AluOpType
ACT = mybir.ActivationFunctionType
AX = mybir.AxisListType

P = 128
D = 1024
KD = D // P
SEQ = 4096
NP = SEQ // P
NT = NP + 1
T = NT * P
SB, SL = 8, 16
H, HD = 8, 64
G, N = 2, 128
W = H * HD
CD = W + 2 * G * N
CB = CD // P
CW = 4
INP = W + CD + H + 2 * W
COL_Z, COL_X, COL_DT, COL_GU, COL_GV = 0, W, W + CD, W + CD + H, W + CD + H + W
NG, EG = 4, 8
NE = NG * EG
DE = 256
NR = NG + NE
R_G1, R_CBIAS, R_CW = 0, KD, KD + CB
R_BSP = R_CW + CW * CB
R_SG = R_BSP + H
R_BSS = R_SG + W // P
NROW = R_BSS + H
N_CONST = 5 + SB + 3 + 2 + 3 + 2
NBLK = 2 * T // P + NE
EPS = 1e-6
ARTANH = (2.000000007681758, 0.6666632164140268, 0.40024595229739224, 0.27965157758356346, 0.28157778304302755)
BIG = 1e30


class Steps:

    def __init__(self, eng, sem, fence=lambda n, k: None):
        self.eng, self.sem, self.base, self.n, self.fence = eng, sem, 0, 0, fence

    def inc(self, ins):
        self.n += 1
        ins.then_inc(self.sem, 1)

    def wait(self):
        self.eng.wait_ge(self.sem, self.base + self.n)
        self.fence(self.base, 0)

    def link(self, ins):
        self.inc(ins)
        self.wait()

    def loop_begin(self, per_turn):
        self.before, self.per_turn = self.base + self.n, per_turn

    def loop_at(self, turn):
        self.base, self.n = turn * self.per_turn + self.before, 0

    def loop_end(self, turns):
        assert self.n == self.per_turn, (self.n, self.per_turn)
        self.base, self.n = self.before + turns * self.per_turn, 0


def after(eng, sem, n):
    if isinstance(n, int) and n <= 0:
        return
    eng.wait_ge(sem, n)


DVE_TURN, POOL_TURN = 102, 32


def build(nc, x_prompt, x_sample, cache_conv, state_ssm, norm1_g, w_in, conv_w, conv_b, dt_bias, a_log,
          d_skip, ssm_norm_g, ln_v_g, ln_v_b, w_spatial, b_spatial, w_out, norm2_g,
          w_rg, b_rg, w_re, b_re, w_gate, w_up, w_down, final_norm_g,
          y_prompt, y_sample, conv_prompt, ssm_prompt, conv_sample, ssm_sample, gmlp_v_sample):
    ctx = ExitStack()
    with ctx:
        def sb(name, shape, dt=F32):
            return ctx.enter_context(nc.sbuf_tensor(name, shape, dt))

        def ps(name, shape):
            return ctx.enter_context(nc.psum_tensor(name, shape, F32))

        def sem(name):
            return ctx.enter_context(nc.semaphore(name))

        x2_d = nc.dram_tensor("x2_rows", [T, D], F32).ap()
        h2_d = nc.dram_tensor("h2_rows", [T, D], F32).ap()
        ys_d = nc.dram_tensor("expert_rows", [NBLK * P, D], F32).ap()
        slot_d = nc.dram_tensor("slot_tokens", [NE * T, 1], I32).ap()

        ARENA = KD * INP
        arena = sb("arena", [P, ARENA])
        w_in_sb = arena[:, :].rearrange("p (k n) -> p k n", k=KD)
        w_out_sb = sb("w_out_sb", [P, KD, D])

        ident = sb("ident", [P, P])
        tri = sb("tri", [P, P])
        stri = sb("stri", [P, P])
        tri_s = sb("tri_s", [P, P])
        blk_s = sb("blk_s", [P, P])
        ones = sb("ones", [P, P])
        row_s = sb("row_s", [P, SB])
        iota_g = sb("iota_g", [P, NG])
        iota_e = sb("iota_e", [P, NE])
        neg_half = sb("neg_half", [P, 2])
        tok_id = sb("tok_id", [P, 1])
        g2_b = sb("g2_b", [P, D])
        lng_b = sb("lng_b", [P, W])
        lnb_b = sb("lnb_b", [P, W])
        small_b = sb("small_b", [P, 3 * H])
        dtb_b, alog_b, dsk_b = (small_b[:, k * H:(k + 1) * H] for k in range(3))
        aneg_b = sb("aneg_b", [P, H])
        rb_b = sb("rb_b", [P, NR])
        wr_sb = sb("wr_sb", [P, KD, NR])
        wsT = sb("wsT", [P, H, P])
        slot_zero = sb("slot_zero", [P, NE * T // P // 8], I32)
        iota_b = sb("iota_b", [P, NBLK])
        cols = sb("cols", [P, NROW])

        x_in = [sb(f"x_in{u}", [P, D]) for u in range(2)]
        x_res = [sb(f"x_res{u}", [P, D]) for u in range(2)]
        hT = [sb(f"hT{u}", [P, KD, P]) for u in range(2)]
        xbc = sb("xbc", [P, CD])
        xT = sb("xT", [P, CB, P + CW - 1])
        xc = sb("xc", [P, CB, P])
        xtok = sb("xtok", [P, W])
        btok = sb("btok", [P, G * N])
        gu = [sb("gu", [P, W])] * 2
        zz = [sb("zz", [P, W])] * 2
        gv = sb("gv", [P, W])
        dec = sb("dec", [P, H, P])
        cbm = sb("cbm", [P, G, P])
        xdt = sb("xdt", [P, W])
        xw = sb("xw", [P, W])
        state = sb("state", [P, W])
        yb = sb("yb", [P, W])
        tmp = sb("tmp", [P, W])
        ycat = sb("ycat", [P, D])
        tT = sb("tT", [P, KD, P])
        h2 = sb("h2", [P, D])
        rows = h2[0:NROW, 0:P]
        iota_i = ycat[:, 0:NR + 1 + NBLK].bitcast(I32)
        dt_t = sb("dt_t", [P, H])
        adt = sb("adt", [P, H])
        dtw = sb("dtw", [P, 8, H])
        e_in = sb("e_in", [P, 3 * H])
        e_out = sb("e_out", [P, 3 * H])
        bn6 = sb("bn6", [P, 6])
        mv = sb("mv", [P, 2])
        sq = sb("sq", [P, 4])
        rs = sb("rs", [P, 8])
        lgs = sb("lgs", [P, NR])
        rt = sb("rt", [P, 16])
        gex = sb("gex", [P, NG + 1])
        gexo = sb("gexo", [P, NG + 1])
        eqt = sb("eqt", [P, NE])
        em = sb("em", [P, NE])
        oh = sb("oh", [P, 3, NE])
        rk = sb("rk", [P, NE])
        carry = sb("carry", [P, NE])
        slots = sb("slots", [P, 3], I32)
        spare = sb("spare", [P, 4])
        picks = sb("picks", [P, NT, 6])

        pend_i = sb("pend_i", [P, NE], I32)
        tab = sb("tab", [P, 3, NBLK], I32)
        rowpos = sb("rowpos", [P, NT, 2], I32)
        idx = [sb(f"idx{u}", [P, 1], I32) for u in range(2)]
        fidx = [sb(f"fidx{u}", [P, 2], I32) for u in range(2)]
        wts = sb("wts", [P, 2])
        hb2 = [gv[:, 0:DE], gv[:, DE:2 * DE]]

        PB = [ps(f"PB{u}", [P, 512]) for u in range(2)]
        TB = [ps(f"TB{u}", [P, 4, P]) for u in range(2)]
        SS = ps("SS", [P, 2, 512])
        YB = ps("YB", [P, 512])
        MB = ps("MB", [P, 512])
        dt_p, acs_p, tot_p = MB[:, 0:H], MB[:, H:2 * H], MB[:, 2 * H:3 * H]
        cb_p = MB[:, 32:32 + G * P]
        lg_p, rk_p, cnt_p = MB[:, 288:288 + NR], MB[:, 324:324 + NE], MB[:, 356:356 + NE]
        sd_p = MB[:, 400:400 + 4 * SB]


        names = """started consts w_scaled eout_a cols_full cols_out ws_full ws_out states_zero
            xsq_ready xr_ready x_scaled xT_full xT_out
            proj0 proj1 proj_gv proj_gu proj_z xbc0_out xbc1_out gv_out gu_out z_out
            xbcT_full xbcT_out halo_saved conv_done zs_ready xc_ready cb_done xb_full xb_out
            dt_done dt_read lg_read cb_read rank_read dtneg_ready dtexp_ready dtrec_ready dt_ready trid_ready acs_done bcast_done
            ein_ready eout_ready seg_done decay_ready dec_ready xw_ready
            mixed_done bn_ready vr_ready v_ready ycat_hi
            ydiag_done yoff_done states_done state_ready gated_ready ysq_ready yr_ready ycat_ready
            ycT_full ycT_out out0 out1 x2_half x2_ready x2sq_ready x2r_ready h2_ready
            h2T_full h2T_out logits_done gexin_ready gexout_ready pick_ready rank_done slots_ready
            smp_zero smp_cache_T smp_cache_out smp_ws_T smp_ws_out smp_st_T smp_st_out smp_masks smp_dec_full
            smp_dec_out smp_new stateT_full stateT_out
            fenced tables gx_T gx_out0 gx_out1 gu_full silu_out hb_ready hbT_full hbT_out dn_full dn_out0 dn_out1
            idx_free fin_idx fin_sq fin_r fin_out""".split()
        s = {n: sem(n) for n in names}
        x_loaded = [sem(f"x_loaded{u}") for u in range(2)]
        res_loaded = [sem(f"res_loaded{u}") for u in range(2)]
        win_loaded = [sem(f"win_loaded{k}") for k in range(2)]
        const_loaded, ws_loaded, wout_loaded = sem("const_loaded"), sem("ws_loaded"), sem("wout_loaded")
        slots_zeroed, scattered = sem("slots_zeroed"), sem("scattered")
        x2_stored, h2_stored = sem("x2_stored"), sem("h2_stored")
        convp_stored, convs_stored, vs_stored, ssm_stored = (sem(n) for n in ("convp_stored", "convs_stored", "vs_stored", "ssm_stored"))
        smp_cache_loaded, smp_st_loaded, smp_ws_loaded = sem("smp_cache_loaded"), sem("smp_st_loaded"), sem("smp_ws_loaded")
        w_loaded = sem("w_loaded")
        idx_loaded = [sem(f"idx_loaded{u}") for u in range(2)]
        gathered = [sem(f"gathered{u}") for u in range(2)]
        ys_stored = [sem(f"ys_stored{u}") for u in range(2)]
        fx_loaded = [sem(f"fx_loaded{u}") for u in range(2)]
        fy_gathered = [sem(f"fy_gathered{u}") for u in range(2)]
        fy_stored = [sem(f"fy_stored{u}") for u in range(2)]
        gf_loaded, fin_w, fin_one, fin_add, pool_fin = (sem(n) for n in ("gf_loaded", "fin_w", "fin_one", "fin_add", "pool_fin"))
        dve_step, pool_step = sem("dve_step"), sem("pool_step")

        x_tiles = x_prompt.rearrange("a (t p) d -> (a t) p d", p=P)
        y_tiles = y_prompt.rearrange("a (t p) d -> (a t) p d", p=P)
        x2_tiles = x2_d.rearrange("(t p) d -> t p d", p=P)
        h2_tiles = h2_d.rearrange("(t p) d -> t p d", p=P)
        ys_tiles = ys_d.rearrange("(t p) d -> t p d", p=P)

        def at_tile(tiles, t):
            if isinstance(t, int):
                return tiles[t, :, :]
            return tiles[bass.ds(t, 1), :, :].rearrange("a p d -> (a p) d")

        def input_tile(t):
            if isinstance(t, int) and t == NP:
                return x_sample.rearrange("b l d -> (b l) d")
            return at_tile(x_tiles, t)

        used = [0]

        def take(n):
            used[0] += n
            assert used[0] <= ARENA, used[0]
            return arena[:, used[0] - n:used[0]]

        CMW = SB * (P + SL)
        st_old = take(SB * W).rearrange("p (q b n) -> p q b n", q=SB, b=4)
        st_T = take(SB * W).rearrange("p (q w) -> p q w", q=SB)
        cmask = take(G * CMW).rearrange("p (g w) -> p g w", g=G)
        bmask = take(G * SB * N).rearrange("p (g q n) -> p g q n", g=G, q=SB)
        wsT_s = take(H * P).rearrange("p (h t) -> p h t", h=H)
        ws_nat = take(H * P).rearrange("p (h t) -> p h t", h=H)
        xT_s = take(CB * SB * (SL + CW - 1)).rearrange("p (b q l) -> p b q l", b=CB, q=SB)
        cache_sb = take(CD)
        adt_e = take(W)
        st_dec = take(4 * SB)
        used[0] = 0
        WSLOT = KD * 2 * DE + 2 * D
        SLOT = [take(WSLOT) for _ in range(2)]
        cmp_t = take(NBLK * NE).rearrange("p (b e) -> p b e", e=NE)
        tab_i = take(2 * NE).bitcast(I32)
        tab_f = take(2 * NBLK).rearrange("p (a b) -> p a b", a=2)
        tab_b = take(NBLK).bitcast(I32)
        pickk = take(2 * NT).rearrange("p (t a) -> p t a", a=2)
        pos_t = take(2 * NT * NE).rearrange("p (t e) -> p t e", e=NE)
        used[0] = 0
        y_row = [[take(D) for _ in range(2)] for _ in range(2)]
        fin_o = [take(D) for _ in range(2)]
        gf_b = take(D)
        fin_s = take(D)

        def half(b):
            return slice(4 * b, 4 * b + 4)

        def flat(ap):
            return ap.rearrange("p a b -> p (a b)")

        class Turn:

            def __init__(self, j, u):
                self.j, self.u = j, u
                self.i = 2 * j + u
                n = self.i if isinstance(self.i, int) else None
                self.first, self.sample, self.end = n == 0, n == NP, n == NT
                self.prev = not self.first
                self.next, self.next2, self.next3 = (n is None or n + k <= NP for k in (1, 2, 3))

        def over_tiles(eng, turn, steps=None, per_turn=0):
            turn(Turn(0, 0))
            turn(Turn(0, 1))
            last = NP // 2 - 2
            if steps:
                steps.loop_begin(per_turn)
            with eng.Fori(1, last) as j:
                if steps:
                    steps.loop_at(j - 1)
                turn(Turn(j, 0))
                turn(Turn(j, 1))
            if steps:
                steps.loop_end(last - 1)
            for i in range(2 * last, NT + 1):
                turn(Turn(i // 2, i % 2))

        def transpose8(pe, src, waits, done):
            for b in range(2):
                for sm, n in waits(b):
                    after(pe, s[sm], n)
                for k in range(4):
                    mm = nc.tensor.transpose(TB[b][:, k, :], src(4 * b + k), ident[:])
                mm.then_inc(s[done], 1)

        def block_of(t):
            return lambda c: t[:, c * P:(c + 1) * P]

        def project(pe, u, out, col, n, done, waits):
            for sm, v in waits:
                pe.wait_ge(s[sm], v)
            for k in range(KD):
                mm = nc.tensor.matmul(out, hT[u][:, k, :], w_in_sb[:, k, col:col + n], start=k == 0, stop=k == KD - 1)
            mm.then_inc(s[done], 1)

        def pe_turn(pe, tn):
            i, j, u = tn.i, tn.j, tn.u
            v = 1 - u
            if tn.end:
                pe_end(pe, tn)
                return
            if tn.sample:
                pe_sample_setup(pe)
            before = (lambda b: [("xT_out", 3 + b)]) if tn.first else \
                (lambda b: [("smp_st_out", SB - 1 + b)]) if tn.sample else (lambda b: [("ycT_out", 2 * i - 1 + b)])
            transpose8(pe, block_of(xbc), lambda b: [(f"xbc{b}_out", i + 1)] + before(b), "xbcT_full")
            cum, tot = (tri_s, blk_s) if tn.sample else (tri, ones)
            pe.wait_ge(s["dt_ready"], i + 1)
            pe.wait_ge(s["dt_read"], i + 1)
            nc.tensor.matmul(acs_p, cum[:], adt[:], start=True, stop=True)
            nc.tensor.matmul(tot_p, tot[:], adt[:], start=True, stop=True).then_inc(s["acs_done"], 1)
            pe.wait_ge(s["trid_ready"], i + 1)
            pe.wait_ge(s["state_ready"], i + 1)
            if tn.sample:
                pe.wait_ge(s["smp_cache_out"], 2)
            for b in range(2):
                mm = nc.tensor.matmul(SS[:, b, :], tot[:], flat(dec[:, half(b), :]), start=True, stop=True)
            mm.then_inc(s["bcast_done"], 1)
            if tn.next:
                project(pe, v, PB[0][:, :], COL_X, 512, "proj0",
                        [("xT_out", 2 * (i + 2)), ("gu_out", 1) if tn.first else ("x2_half", 2 * i - 1)])
            if tn.prev:
                pe.wait_ge(s["h2_ready"], i)
                transpose8(pe, block_of(h2), lambda b: [("xbcT_out", 2 * i + 1 + b)], "h2T_full")
            if tn.next:
                project(pe, v, PB[1][:, :], COL_X + 512, 512, "proj1",
                        [("z_out", 1) if tn.first else ("x2_half", 2 * i)])
            pe.wait_ge(s["xc_ready"], i + 1)
            after(pe, s["dec_ready"], i)
            pe.wait_ge(s["ein_ready"], i + 1)
            for g in range(G):
                mm = nc.tensor.matmul(cb_p[:, g * P:(g + 1) * P], xc[:, 4 + g, :], xc[:, 6 + g, :], start=True, stop=True)
            mm.then_inc(s["cb_done"], 1)
            for b in range(2):
                pe.wait_ge(*((s["xbcT_out"], 1 + b) if tn.first else (s["h2T_out"], 2 * i - 1 + b)))
                for k in range(4 - 2 * b):
                    mm = nc.tensor.transpose(TB[b][:, k, :], xc[:, 4 * b + k, :], ident[:])
                mm.then_inc(s["xb_full"], 1)
            if tn.prev:
                pe_router(pe, i)
            pe.wait_ge(s["v_ready"], i + 1)
            pe.wait_ge(*((s["xbc0_out"], i + 2) if tn.next else (s["x2_half"], 2 * i - 1)))
            if tn.first:
                pe.wait_ge(s["ws_out"], 2)
            ws = wsT_s if tn.sample else wsT
            for h in range(H):
                c = slice(h * HD, (h + 1) * HD)
                mm = nc.tensor.matmul(PB[0][:, c], ws[:, h, :], gv[:, c], start=True, stop=True)
            mm.then_inc(s["mixed_done"], 1)
            pe.wait_ge(s["dec_ready"], i + 1)
            pe.wait_ge(s["xw_ready"], i + 1)
            after(pe, s["gated_ready"], i)
            for h in range(H):
                c = slice(h * HD, (h + 1) * HD)
                mm = nc.tensor.matmul(YB[:, c], dec[:, h, :], xdt[:, c], start=True, stop=True)
            mm.then_inc(s["ydiag_done"], 1)
            if tn.sample:
                pe_sample_states(pe)
            else:
                for g in range(G):
                    c = slice(g * 256, (g + 1) * 256)
                    mm = nc.tensor.matmul(SS[:, 0, c], xc[:, 6 + g, :], state[:, c], start=True, stop=True)
                mm.then_inc(s["yoff_done"], 1)
                for g in range(G):
                    c = slice(g * 256, (g + 1) * 256)
                    mm = nc.tensor.matmul(SS[:, 1, c], btok[:, g * N:(g + 1) * N], xw[:, c], start=True, stop=True)
                mm.then_inc(s["states_done"], 1)
            if tn.next:
                project(pe, v, PB[1][:, :], COL_GV, 512, "proj_gv", [("xbc1_out", i + 2)])
            if tn.prev:
                pe_rank(pe, i, tn.sample)
            if tn.next:
                project(pe, v, PB[0][:, :], COL_GU, 512, "proj_gu", [("ycat_hi", i + 1)])
            if tn.next2:
                pe.wait_ge(s["x_scaled"], i + 3)
                transpose8(pe, block_of(x_in[u]), lambda b: [("xb_out", 2 * i + 1 + b)], "xT_full")
            if tn.next:
                project(pe, v, PB[1][:, :], COL_Z, 512, "proj_z", [("gv_out", i + 2)])
            pe.wait_ge(s["ycat_ready"], i + 1)
            transpose8(pe, block_of(ycat),
                       lambda b: [("xT_out", 2 * i + 5 + b) if tn.next2 else ("xb_out", 2 * i + 1 + b)], "ycT_full")
            if tn.next:
                project(pe, v, dt_p, COL_DT, H, "dt_done", [("cb_read", 1) if tn.first else ("rank_read", i)])
            pe.wait_ge(s["ycT_out"], 2 * (i + 1))
            if tn.first:
                pe.wait_ge(s["w_scaled"], 2)
            for b in range(2):
                if tn.next:
                    pe.wait_ge(s[("gu_out", "z_out")[b]], i + 2)
                else:
                    pe.wait_ge(*((s["ycat_hi"], i + 1) if b == 0 else (s["x2_half"], 2 * i)))
                for k in range(KD):
                    mm = nc.tensor.matmul(PB[b][:, :], tT[:, k, :], w_out_sb[:, k, b * 512:(b + 1) * 512],
                                          start=k == 0, stop=k == KD - 1)
                mm.then_inc(s[f"out{b}"], 1)

        def pe_router(pe, i):
            pe.wait_ge(s["h2T_out"], 2 * i)
            pe.wait_ge(*((s["rank_read"], NP) if isinstance(i, int) and i == NT else (s["cb_read"], i + 1)))
            for k in range(KD):
                mm = nc.tensor.matmul(lg_p, tT[:, k, :], wr_sb[:, k, :], start=k == 0, stop=k == KD - 1)
            mm.then_inc(s["logits_done"], 1)

        def pe_rank(pe, i, after_decay=False):
            pe.wait_ge(s["pick_ready"], i)
            if after_decay:
                pe.wait_ge(s["smp_dec_out"], 1)
            nc.tensor.matmul(rk_p, stri[:], oh[:, 2, :], start=True, stop=True)
            nc.tensor.matmul(cnt_p, ones[:], oh[:, 2, :], start=True, stop=True).then_inc(s["rank_done"], 1)

        def pe_sample_setup(pe):
            pe.wait_ge(smp_cache_loaded, 16)
            pe.wait_ge(s["state_ready"], NP + 1)
            R = SB * (CW - 1)
            for c in range(CB):
                mm = nc.tensor.transpose(SS[:, c // 4, (c % 4) * R:(c % 4 + 1) * R], cache_sb[0:R, c * P:(c + 1) * P],
                                         ident[0:R, 0:R])
            mm.then_inc(s["smp_cache_T"], 1)
            pe.wait_ge(smp_ws_loaded, 16 * SB)
            transpose8(pe, lambda c: ws_nat[:, c, :], lambda b: [("ycT_out", 2 * NP - 1 + b)], "smp_ws_T")
            pe.wait_ge(smp_st_loaded, 16)
            for q in range(SB):
                pe.wait_ge(*((s["smp_ws_out"], q + 1) if q < 2 else (s["smp_st_out"], q - 1)))
                for k in range(4):
                    mm = nc.tensor.transpose(TB[q % 2][:, k, :], st_old[:, q, k, :], ident[:])
                mm.then_inc(s["smp_st_T"], 1)

        def pe_sample_states(pe):
            pe.wait_ge(s["smp_masks"], 3)
            pe.wait_ge(s["smp_st_out"], SB)
            pe.wait_ge(s["seg_done"], NP + 1)
            for g in range(G):
                for q in range(SB):
                    mm = nc.tensor.matmul(SS[:, 0, g * 256:(g + 1) * 256], cmask[:, g, q * P:(q + 1) * P],
                                          st_T[:, q, g * 256:(g + 1) * 256], start=q == 0, stop=q == SB - 1)
            mm.then_inc(s["yoff_done"], 1)
            pe.wait_ge(s["lg_read"], NP)
            for b in range(4):
                mm = nc.tensor.matmul(sd_p[:, b * SB:(b + 1) * SB], adt_e[:, b * P:(b + 1) * P], row_s[:], start=True, stop=True)
            mm.then_inc(s["smp_dec_full"], 1)
            for n in range(8):
                after(pe, s["smp_new"], n)
                nc.tensor.matmul(SS[:, 1, :], xw[:, (n // 2) * P:(n // 2 + 1) * P],
                                 flat(bmask[:, n // 4, half(n % 2), :]), start=True, stop=True).then_inc(s["states_done"], 1)

        def pe_end(pe, tn):
            pe.wait_ge(s["h2_ready"], NT)
            transpose8(pe, block_of(h2), lambda b: [("ycT_out", 2 * NT - 1 + b)], "h2T_full")
            pe_router(pe, NT)
            pe_rank(pe, NT)
            for k in range(4):
                mm = nc.tensor.transpose(YB[:, k * P:(k + 1) * P], state[:, k * P:(k + 1) * P], ident[:])
                if k == 0:
                    mm.then_inc(s["dn_full"], 1)
            mm.then_inc(s["stateT_full"], 1)

        def pe_phase1(pe):
            pe.wait_ge(s["consts"], 1)
            pe.wait_ge(s["x_scaled"], 1)
            transpose8(pe, block_of(x_in[0]), lambda b: [], "xT_full")
            pe.wait_ge(const_loaded, 16 * N_CONST)
            nc.tensor.transpose(MB[:, 0:NROW], rows[0:NROW, :], ident[0:NROW, 0:NROW]).then_inc(s["cols_full"], 1)
            pe.wait_ge(ws_loaded, 16)
            for b in range(2):
                for k in range(4):
                    mm = nc.tensor.transpose(SS[:, b, k * P:(k + 1) * P], xc[:, 4 * b + k, :], ident[:])
            mm.then_inc(s["ws_full"], 1)
            pe.wait_ge(s["x_scaled"], 2)
            transpose8(pe, block_of(x_in[1]), lambda b: [("xT_out", 1 + b)], "xT_full")
            pe.wait_ge(s["w_scaled"], 1)
            project(pe, 0, PB[0][:, :], COL_X, 512, "proj0", [("xT_out", 2)])
            project(pe, 0, PB[1][:, :], COL_X + 512, 512, "proj1", [])
            project(pe, 0, PB[0][:, :], COL_GU, 512, "proj_gu", [("xbc0_out", 1)])
            project(pe, 0, PB[1][:, :], COL_GV, 512, "proj_gv", [("xbc1_out", 1)])
            project(pe, 0, dt_p, COL_DT, H, "dt_done", [("cols_out", 1)])
            project(pe, 0, PB[1][:, :], COL_Z, 512, "proj_z", [("gv_out", 1)])
            pe.wait_ge(s["ws_out"], 2)
            over_tiles(pe, lambda tn: pe_turn(pe, tn))

        def act_turn(act, tn):
            i, j, u = tn.i, tn.j, tn.u
            v = 1 - u
            if tn.end:
                act_end(act)
                return
            if tn.sample:
                act_sample_setup(act)
            for b in range(2):
                act.wait_ge(s["xbcT_full"], 2 * i + 1 + b)
                if tn.sample:
                    for k in range(4):
                        ins = nc.scalar.activation(xT_s[:, 4 * b + k, :, CW - 1:],
                                                   TB[b][:, k, :].rearrange("p (q l) -> p q l", q=SB), ACT.Copy)
                else:
                    act.wait_ge(s["halo_saved"], i + 1)
                    ins = nc.scalar.activation(xT[:, half(b), CW - 1:], TB[b][:, :, :], ACT.Copy)
                ins.then_inc(s["xbcT_out"], 1)
            if tn.prev:
                act_x2sq(act, i - 1, j - 1 + u, v)
            act.wait_ge(s["z_out"], i + 1)
            nc.scalar.activation(zz[u][:, :], zz[u][:, :], ACT.Silu).then_inc(s["zs_ready"], 1)
            if tn.next:
                act.wait_ge(s["proj0"], i + 2)
                if isinstance(i, int) and i == NP - 1:
                    act.wait_ge(convp_stored, 16)
                nc.scalar.activation(xbc[:, 0:512], PB[0][:, :], ACT.Copy).then_inc(s["xbc0_out"], 1)
            act.wait_ge(s["conv_done"], i + 1)
            nc.scalar.activation(xc[:, :, :], xc[:, :, :], ACT.Silu).then_inc(s["xc_ready"], 1)
            act.wait_ge(s["ein_ready"], i + 1)
            act.wait_ge(s["state_ready"], i + 1)
            nc.scalar.activation(e_out[:, :], e_in[:, :], ACT.Exp).then_inc(s["eout_ready"], 1)
            act.wait_ge(s["seg_done"], i + 1)
            nc.scalar.activation(dec[:, :, :], dec[:, :, :], ACT.Exp).then_inc(s["decay_ready"], 1)
            if tn.prev:
                act_h2T(act, i)
            act.wait_ge(s["xb_full"], 2 * i + 1)
            after(act, s["gated_ready"], i)
            nc.scalar.activation(xtok[:, :], flat(TB[0][:, :, :]), ACT.Copy).then_inc(s["xb_out"], 1)
            act.wait_ge(s["xb_full"], 2 * i + 2)
            after(act, s["states_done"], i)
            nc.scalar.activation(btok[:, :], flat(TB[1][:, 0:2, :]), ACT.Copy).then_inc(s["xb_out"], 1)
            if tn.next:
                act.wait_ge(s["proj1"], i + 2)
                nc.scalar.activation(xbc[:, 512:], PB[1][:, :], ACT.Copy).then_inc(s["xbc1_out"], 1)
            if tn.prev:
                act.wait_ge(s["gexin_ready"], i)
                nc.scalar.activation(gexo[:, :], gex[:, :], ACT.Exp).then_inc(s["gexout_ready"], 1)
            if tn.next2:
                act_xsq(act, j + 1, u)
            if tn.sample:
                act.wait_ge(s["smp_dec_full"], 1)
                nc.scalar.activation(st_dec, sd_p, ACT.Exp).then_inc(s["smp_dec_out"], 1)
            act.wait_ge(s["gated_ready"], i + 1)
            for g in range(G):
                c = slice(g * 256, (g + 1) * 256)
                ins = nc.scalar.activation(tmp[:, c], yb[:, c], ACT.Square, accum_out=sq[:, 2 + g:3 + g])
            ins.then_inc(s["ysq_ready"], 1)
            if tn.next:
                act.wait_ge(s["proj_gv"], i + 2)
                act.wait_ge(s["mixed_done"], i + 1)
                nc.scalar.activation(gv[:, :], PB[1][:, :], ACT.Gelu_apprx_tanh).then_inc(s["gv_out"], 1)
                act.wait_ge(s["proj_gu"], i + 2)
                nc.scalar.activation(gu[v][:, :], PB[0][:, :], ACT.Gelu_apprx_tanh).then_inc(s["gu_out"], 1)
            if tn.next2:
                act_xT(act, i + 2, u)
            if tn.next:
                act.wait_ge(s["proj_z"], i + 2)
                nc.scalar.activation(zz[v][:, :], PB[1][:, :], ACT.Copy).then_inc(s["z_out"], 1)
            for b in range(2):
                act.wait_ge(s["ycT_full"], 2 * i + 1 + b)
                after(act, s["logits_done"], i)
                nc.scalar.activation(tT[:, half(b), :], TB[b][:, :, :], ACT.Copy).then_inc(s["ycT_out"], 1)
            if tn.next:
                act.wait_ge(s["dtneg_ready"], i + 2)
                nc.scalar.activation(dtw[:, 2, :], dtw[:, 1, :], ACT.Exp).then_inc(s["dtexp_ready"], 1)
        def act_x2sq(act, i, j, u):
            act.wait_ge(s["x2_half"], 2 * (i + 1))
            after(act, h2_stored, 16 * i)
            after(act, s["h2T_full"], 2 * i)
            nc.scalar.activation(h2[:, :], x_res[u][:, :], ACT.Square, accum_out=sq[:, 1:2]).then_inc(s["x2sq_ready"], 1)

        def act_xsq(act, j, u):
            act.wait_ge(x_loaded[u], 16 * (j + 1))
            nc.scalar.activation(flat(hT[u][:, :, :]), x_in[u][:, :], ACT.Square, accum_out=sq[:, 0:1]).then_inc(s["xsq_ready"], 1)

        def act_xT(act, t, u):
            for b in range(2):
                act.wait_ge(s["xT_full"], 2 * t + 1 + b)
                nc.scalar.activation(hT[u][:, half(b), :], TB[b][:, :, :], ACT.Copy).then_inc(s["xT_out"], 1)

        def act_h2T(act, i):
            for b in range(2):
                act.wait_ge(s["h2T_full"], 2 * i - 1 + b)
                nc.scalar.activation(tT[:, half(b), :], TB[b][:, :, :], ACT.Copy).then_inc(s["h2T_out"], 1)

        def act_sample_setup(act):
            R = SB * (CW - 1)
            act.wait_ge(s["smp_cache_T"], 1)
            for b in range(2):
                for k in range(4):
                    ins = nc.scalar.activation(xT_s[:, 4 * b + k, :, 0:CW - 1],
                                               SS[:, b, k * R:(k + 1) * R].rearrange("p (q l) -> p q l", q=SB), ACT.Copy)
                ins.then_inc(s["smp_cache_out"], 1)
            for q in range(SB):
                act.wait_ge(s["smp_st_T"], q + 1)
                nc.scalar.activation(st_T[:, q, :], flat(TB[q % 2][:, :, :]), ACT.Copy).then_inc(s["smp_st_out"], 1)

        def act_end(act):
            act_x2sq(act, NP, NP // 2, NP % 2)
            act_h2T(act, NT)
            act.wait_ge(s["gexin_ready"], NT)
            nc.scalar.activation(gexo[:, :], gex[:, :], ACT.Exp).then_inc(s["gexout_ready"], 1)
            act.wait_ge(s["stateT_full"], 1)
            nc.scalar.activation(tmp[:, :], YB[:, :], ACT.Copy).then_inc(s["stateT_out"], 1)

        def act_phase1(act):
            act.wait_ge(const_loaded, 16 * N_CONST)
            nc.scalar.activation(aneg_b[:, :], alog_b, ACT.Exp).then_inc(s["eout_a"], 1)
            for u in range(2):
                if u == 1:
                    act.wait_ge(s["xr_ready"], 1)
                act_xsq(act, 0, u)
                act_xT(act, u, u)
            act.wait_ge(s["proj0"], 1)
            nc.scalar.activation(xbc[:, 0:512], PB[0][:, :], ACT.Copy).then_inc(s["xbc0_out"], 1)
            act.wait_ge(s["proj1"], 1)
            nc.scalar.activation(xbc[:, 512:], PB[1][:, :], ACT.Copy).then_inc(s["xbc1_out"], 1)
            act.wait_ge(s["proj_gu"], 1)
            nc.scalar.activation(gu[0][:, :], PB[0][:, :], ACT.Gelu_apprx_tanh).then_inc(s["gu_out"], 1)
            act.wait_ge(s["proj_gv"], 1)
            nc.scalar.activation(gv[:, :], PB[1][:, :], ACT.Gelu_apprx_tanh).then_inc(s["gv_out"], 1)
            act.wait_ge(s["dtneg_ready"], 1)
            nc.scalar.activation(dtw[:, 2, :], dtw[:, 1, :], ACT.Exp).then_inc(s["dtexp_ready"], 1)
            act.wait_ge(s["proj_z"], 1)
            nc.scalar.activation(zz[0][:, :], PB[1][:, :], ACT.Copy).then_inc(s["z_out"], 1)
            over_tiles(act, lambda tn: act_turn(act, tn))

        V = nc.vector

        def per_head(ap):
            return ap.rearrange("p (h a) -> p h a", a=1).broadcast_to([P, H, HD])

        def heads(ap):
            return ap.rearrange("p (h d) -> p h d", h=H)

        def dve_turn(dve, st, tn):
            i, j, u = tn.i, tn.j, tn.u
            v = 1 - u
            if tn.end:
                dve_h2(dve, NP, NP % 2)
                dve_route(dve, st, NT)
                dve_slots(dve, st, NT)
                return
            if tn.sample:
                for b in range(2):
                    dve.wait_ge(s["smp_ws_T"], b + 1)
                    V.tensor_tensor(wsT_s[:, half(b), :], TB[b][:, :, :], over(tri_s, 4), ALU.mult).then_inc(s["smp_ws_out"], 1)
            dve.wait_ge(s["xbcT_out"], 2 * (i + 1))
            tap = cols[:, R_CW:R_CW + CW * CB].rearrange("p (w b) -> p w b", w=CW)
            for w in range(CW - 1, -1, -1):
                for c in range(CB):
                    if tn.sample:
                        src, dst = xT_s[:, c, :, w:w + SL], xc[:, c, :].rearrange("p (q l) -> p q l", q=SB)
                    else:
                        src, dst = xT[:, c, w:w + P], xc[:, c, :]
                    if w == CW - 1:
                        ins = V.tensor_scalar(dst, src, tap[:, w, c:c + 1], cols[:, R_CBIAS + c:R_CBIAS + c + 1], ALU.mult, ALU.add)
                    else:
                        ins = V.scalar_tensor_tensor(out=dst, in0=src, scalar=tap[:, w, c:c + 1], in1=dst, op0=ALU.mult, op1=ALU.add)
                if w > 0:
                    st.link(ins)
                if w == CW - 1 and tn.prev:
                    dve_h2(dve, i - 1, v)
            ins.then_inc(s["conv_done"], 1)
            dve.wait_ge(s["conv_done"], i + 1)
            V.tensor_copy(xT[:, :, 0:CW - 1], xT[:, :, P:]).then_inc(s["halo_saved"], 1)
            dve.wait_ge(s["acs_done"], i + 1)
            st.link(V.tensor_copy(e_in[:, 0:2 * H], MB[:, H:3 * H]))
            V.tensor_tensor(e_in[:, 2 * H:], e_in[:, H:2 * H], e_in[:, 0:H], ALU.subtract).then_inc(s["ein_ready"], 1)
            dve.wait_ge(s["bcast_done"], i + 1)
            for h in range(H):
                a = e_in[:, h:h + 1]
                ins = V.tensor_scalar(dec[:, h, :], SS[:, h // 4, (h % 4) * P:(h % 4 + 1) * P], a, a, ALU.min, ALU.subtract)
            ins.then_inc(s["seg_done"], 1)
            dve.wait_ge(s["cb_done"], i + 1)
            V.tensor_tensor(cbm[:, :, :], cb_p.rearrange("p (g t) -> p g t", g=G),
                            over(tri_s if tn.sample else tri, G), ALU.mult).then_inc(s["cb_read"], 1)
            dve.wait_ge(s["cb_read"], i + 1)
            dve.wait_ge(s["decay_ready"], i + 1)
            for g in range(G):
                ins = V.tensor_tensor(dec[:, half(g), :], dec[:, half(g), :],
                                      cbm[:, g:g + 1, :].broadcast_to([P, 4, P]), ALU.mult)
            ins.then_inc(s["dec_ready"], 1)
            dve.wait_ge(s["xb_out"], 2 * (i + 1))
            dve.wait_ge(s["eout_ready"], i + 1)
            st.link(V.tensor_tensor(heads(xdt[:, :]), heads(xtok[:, :]), per_head(dt_t[:, :]), ALU.mult))
            V.tensor_tensor(heads(xw[:, :]), heads(xdt[:, :]), per_head(e_out[:, 2 * H:]), ALU.mult).then_inc(s["xw_ready"], 1)
            st.inc(V.tensor_tensor(heads(yb[:, :]), heads(xtok[:, :]), per_head(dsk_b), ALU.mult))
            if tn.sample:
                dve_sample_masks(dve, st)
            if tn.prev:
                dve_route(dve, st, i)
            if tn.next2:
                dve_scale_x(dve, i + 2, u)
            dve.wait_ge(s["mixed_done"], i + 1)
            b0 = R_BSS if tn.sample else R_BSP
            st.link(V.tensor_tensor(heads(tmp[:, :]), heads(PB[0][:, :]), per_head(cols[:, b0:b0 + H]), ALU.add))
            V.tensor_tensor(ycat[:, W:], tmp[:, :], gu[u][:, :], ALU.mult).then_inc(s["ycat_hi"], 1)
            dve.wait_ge(s["ydiag_done"], i + 1)
            dve.wait_ge(s["ycat_hi"], i + 1)
            st.inc(V.tensor_tensor(yb[:, :], yb[:, :], YB[:, :], ALU.add))
            dve.wait_ge(s["yoff_done"], i + 1)
            st.link(V.tensor_tensor(heads(tmp[:, :]), heads(SS[:, 0, :]), per_head(e_out[:, 0:H]), ALU.mult))
            st.link(V.tensor_tensor(yb[:, :], yb[:, :], tmp[:, :], ALU.add))
            dve.wait_ge(s["zs_ready"], i + 1)
            V.tensor_tensor(yb[:, :], yb[:, :], zz[u][:, :], ALU.mult).then_inc(s["gated_ready"], 1)
            if tn.sample:
                dve_sample_states(dve, st)
            else:
                dve.wait_ge(s["states_done"], i + 1)
                st.link(V.tensor_tensor(heads(state[:, :]), heads(state[:, :]), per_head(e_out[:, H:2 * H]), ALU.mult))
                V.tensor_tensor(state[:, :], state[:, :], SS[:, 1, :], ALU.add).then_inc(s["state_ready"], 1)
            if tn.prev:
                dve_slots(dve, st, i)
            dve.wait_ge(s["yr_ready"], i + 1)
            for g in range(G):
                c = slice(g * 256, (g + 1) * 256)
                ins = V.tensor_scalar(ycat[:, c], yb[:, c], rs[:, 2 + g:3 + g], None, ALU.mult)
            ins.then_inc(s["ycat_ready"], 1)
            if tn.next:
                dve_v(dve, st, i + 1)
                dve_dt(dve, st, i + 1)
            dve.wait_ge(res_loaded[u], 16 * (j + 1))
            for b in range(2):
                c = slice(b * 512, (b + 1) * 512)
                dve.wait_ge(s[f"out{b}"], i + 1)
                V.tensor_tensor(x_res[u][:, c], x_res[u][:, c], PB[b][:, :], ALU.add).then_inc(s["x2_half"], 1)
        def dve_h2(dve, i, u):
            dve.wait_ge(s["x2_half"], 2 * (i + 1))
            dve.wait_ge(s["x2r_ready"], i + 1)
            V.scalar_tensor_tensor(out=h2[:, :], in0=x_res[u][:, :], scalar=rs[:, 1:2], in1=g2_b[:, :],
                                   op0=ALU.mult, op1=ALU.mult).then_inc(s["h2_ready"], 1)

        def over(mask, n):
            return mask[:, :].rearrange("p (a t) -> p a t", a=1).broadcast_to([P, n, P])

        def dve_scale_x(dve, t, u):
            dve.wait_ge(s["xr_ready"], t + 1)
            V.tensor_scalar(x_in[u][:, :], x_in[u][:, :], rs[:, 0:1], None, ALU.mult).then_inc(s["x_scaled"], 1)

        def dve_v(dve, st, t):
            dve.wait_ge(s["gv_out"], t + 1)
            st.inc(V.bn_stats(bn6[:, :], gv[:, :]))
            st.wait()
            if not isinstance(t, int):
                V.memset(spare[:, 3:4], 0.0)
            V.bn_aggr(mv[:, :], bn6[:, :]).then_inc(s["bn_ready"], 1)
            dve.wait_ge(s["vr_ready"], t + 1)
            st.link(V.tensor_scalar(gv[:, :], gv[:, :], mv[:, 0:1], rs[:, 4:5], ALU.subtract, ALU.mult))
            st.link(V.tensor_tensor(gv[:, :], gv[:, :], lng_b[:, :], ALU.mult))
            V.tensor_tensor(gv[:, :], gv[:, :], lnb_b[:, :], ALU.add).then_inc(s["v_ready"], 1)

        def dve_dt(dve, st, t):
            dve.wait_ge(s["dt_done"], t + 1)
            V.tensor_tensor(dtw[:, 0, :], dt_p, dtb_b, ALU.add).then_inc(s["dt_read"], 1)
            dve.wait_ge(s["dt_read"], t + 1)
            V.scalar_tensor_tensor(out=dtw[:, 1, :], in0=dtw[:, 0, :], scalar=-1.0, in1=dtw[:, 0, :],
                                   op0=ALU.mult, op1=ALU.min).then_inc(s["dtneg_ready"], 1)
            dve.wait_ge(s["dtexp_ready"], t + 1)
            st.link(V.tensor_scalar(dtw[:, 3, :], dtw[:, 2, :], 2.0, None, ALU.add))
            V.reciprocal(dtw[:, 4, :], dtw[:, 3, :]).then_inc(s["dtrec_ready"], 1)

        def first_max(st, src, n, iota, best, key, work, onehot):
            st.link(V.tensor_reduce(best, src, AX.X, ALU.max))
            st.link(V.tensor_scalar(work, src, best, None, ALU.is_equal))
            st.link(V.tensor_tensor(work, work, iota, ALU.mult))
            st.link(V.tensor_reduce(key, work, AX.X, ALU.min))
            st.link(V.tensor_scalar(onehot, iota, key, None, ALU.is_equal))

        def dve_route(dve, st, i):
            dve.wait_ge(s["logits_done"], i)
            V.tensor_tensor(lgs[:, :], lg_p, rb_b[:, :], ALU.add).then_inc(s["lg_read"], 1)
            dve.wait_ge(s["lg_read"], i)
            gbest, gkey, b1, k1, b2, k2 = (rt[:, c:c + 1] for c in range(6))
            gone = rt[:, 12:16]
            first_max(st, lgs[:, 0:NG], NG, iota_g[:, :], gbest, gkey, eqt[:, 0:NG], gone)
            st.inc(V.tensor_scalar(gex[:, 0:NG], lgs[:, 0:NG], gbest, None, ALU.subtract))
            st.link(V.tensor_scalar(gone, gone, -1.0, BIG, ALU.add, ALU.mult))
            st.link(V.tensor_tensor(em[:, :].rearrange("p (g e) -> p g e", g=NG), lgs[:, NG:].rearrange("p (g e) -> p g e", g=NG),
                                    gone.rearrange("p (g a) -> p g a", a=1).broadcast_to([P, NG, EG]), ALU.add))
            first_max(st, em[:, :], NE, iota_e[:, :], b1, k1, eqt[:, :], oh[:, 0, :])
            st.link(V.scalar_tensor_tensor(out=em[:, :], in0=oh[:, 0, :], scalar=-4.0 * BIG, in1=em[:, :], op0=ALU.mult, op1=ALU.add))
            first_max(st, em[:, :], NE, iota_e[:, :], b2, k2, eqt[:, :], oh[:, 1, :])
            V.tensor_tensor(gex[:, NG:], b2, b1, ALU.subtract).then_inc(s["gexin_ready"], 1)
            V.tensor_tensor(oh[:, 2, :], oh[:, 0, :], oh[:, 1, :], ALU.add).then_inc(s["pick_ready"], 1)

        def dve_slots(dve, st, i):
            k1, k2 = rt[:, 3:4], rt[:, 5:6]
            ssum, den, w1, w2, p1, p2 = (rt[:, c:c + 1] for c in range(6, 12))
            dve.wait_ge(s["gexout_ready"], i)
            st.link(V.tensor_reduce(ssum, gexo[:, 0:NG], AX.X, ALU.add))
            st.link(V.tensor_scalar(den, gexo[:, NG:], 1.0, ssum, ALU.add, ALU.mult))
            st.link(V.reciprocal(w1, den))
            st.inc(V.tensor_tensor(w2, w1, gexo[:, NG:], ALU.mult))
            dve.wait_ge(s["rank_done"], i)
            st.link(V.tensor_tensor(rk[:, :], rk_p, carry[:, :], ALU.add))
            V.tensor_tensor(carry[:, :], carry[:, :], cnt_p, ALU.add).then_inc(s["rank_read"], 1)
            for k, p in ((0, p1), (1, p2)):
                st.link(V.tensor_tensor(eqt[:, :], oh[:, k, :], rk[:, :], ALU.mult))
                st.link(V.tensor_reduce(p, eqt[:, :], AX.X, ALU.add))
            sl = rt[:, 0:3]
            st.inc(V.scalar_tensor_tensor(out=rt[:, 0:1], in0=k1, scalar=float(T), in1=p1, op0=ALU.mult, op1=ALU.add))
            st.link(V.scalar_tensor_tensor(out=rt[:, 1:2], in0=k2, scalar=float(T), in1=p2, op0=ALU.mult, op1=ALU.add))
            after(dve, scattered, 32 * (i - 1))
            st.inc(V.tensor_scalar(slots[:, 0:2], rt[:, 0:2], float(NE * T), None, ALU.add))
            st.inc(V.tensor_copy(slots[:, 2:3], tok_id[:, :]))
            pk = picks[:, bass.ds(i - 1, 1), :].rearrange("p a c -> p (a c)") if not isinstance(i, int) else picks[:, i - 1, :]
            st.inc(V.tensor_copy(pk[:, 0:1], k1))
            st.inc(V.tensor_copy(pk[:, 1:2], k2))
            st.inc(V.tensor_copy(pk[:, 2:4], rt[:, 10:12]))
            st.inc(V.tensor_copy(pk[:, 4:6], rt[:, 8:10]))
            st.wait()
            V.tensor_scalar(tok_id[:, :], tok_id[:, :], float(P), None, ALU.add).then_inc(s["slots_ready"], 1)
            dve.wait_ge(s["slots_ready"], i)

        def dve_sample_masks(dve, st):
            dve.wait_ge(s["smp_zero"], 2)
            dve.wait_ge(s["xc_ready"], NT)
            for g in range(G):
                ins = V.tensor_copy(cmask[:, g, :].rearrange("p (q w) -> p q w", q=SB)[:, :, 0:SL],
                                    xc[:, 6 + g, :].rearrange("p (q l) -> p q l", q=SB))
            ins.then_inc(s["smp_masks"], 1)
            for g in range(G):
                ins = V.tensor_tensor(bmask[:, g, :, :],
                                      btok[:, g * N:(g + 1) * N].rearrange("p (a n) -> p a n", a=1).broadcast_to([P, SB, N]),
                                      row_s[:, :].rearrange("p (q a) -> p q a", a=1).broadcast_to([P, SB, N]), ALU.mult)
            ins.then_inc(s["smp_masks"], 1)
            V.tensor_copy(heads(adt_e), per_head(adt[:, :])).then_inc(s["smp_masks"], 1)

        def dve_sample_states(dve, st):
            dve.wait_ge(s["smp_dec_out"], 1)
            for n in range(8):
                b, w = n // 2, n % 2
                o = st_old[:, half(w), b, :]
                d = st_dec[:, b * SB + 4 * w:b * SB + 4 * w + 4].rearrange("p (q a) -> p q a", a=1).broadcast_to([P, 4, N])
                dve.wait_ge(s["states_done"], NP + 1 + n)
                st.link(V.tensor_tensor(o, o, d, ALU.mult))
                V.tensor_tensor(o, o, SS[:, 1, :].rearrange("p (q n) -> p q n", q=4), ALU.add).then_inc(s["smp_new"], 1)

        def dve_phase1(dve):
            st = Steps(dve, dve_step)
            V.memset(xT[:, :, 0:CW - 1], 0.0).then_inc(s["halo_saved"], 1)
            st.inc(V.memset(carry[:, :], 0.0))
            V.memset(state[:, :], 0.0).then_inc(s["state_ready"], 1)
            dve_scale_x(dve, 0, 0)
            dve_scale_x(dve, 1, 1)
            dve.wait_ge(s["eout_a"], 1)
            st.link(V.tensor_scalar(aneg_b[:, :], aneg_b[:, :], -1.0, None, ALU.mult))
            dve.wait_ge(s["cols_full"], 1)
            V.tensor_copy(cols[:, :], MB[:, 0:NROW]).then_inc(s["cols_out"], 1)
            dve.wait_ge(s["ws_full"], 1)
            for b in range(2):
                V.tensor_tensor(wsT[:, half(b), :], SS[:, b, :].rearrange("p (h t) -> p h t", h=4), over(tri, 4),
                                ALU.mult).then_inc(s["ws_out"], 1)
            dve.wait_ge(s["cols_out"], 1)
            for k in range(KD):
                if k % 4 == 0:
                    dve.wait_ge(win_loaded[k // 4], 16)
                ins = V.tensor_scalar(w_in_sb[:, k, :], w_in_sb[:, k, :], cols[:, R_G1 + k:R_G1 + k + 1], None, ALU.mult)
            ins.then_inc(s["w_scaled"], 1)
            dve.wait_ge(wout_loaded, 16)
            for k in range(W // P):
                ins = V.tensor_scalar(w_out_sb[:, k, :], w_out_sb[:, k, :], cols[:, R_SG + k:R_SG + k + 1], None, ALU.mult)
            ins.then_inc(s["w_scaled"], 1)
            dve_dt(dve, st, 0)
            dve_v(dve, st, 0)
            over_tiles(dve, lambda tn: dve_turn(dve, st, tn), st, DVE_TURN)
            return st

        def fence(n, k):
            if not isinstance(n, int):
                nc.gpsimd.tensor_tensor(spare[:, k:k + 1], neg_half[:, 0:1], neg_half[:, 0:1], ALU.mult)

        def root(pool, st, out, in_, scale, n):
            st.link(nc.gpsimd.tensor_scalar(out, in_, scale, EPS, ALU.mult, ALU.add))
            return nc.gpsimd.tensor_tensor(out, out, neg_half[:, 0:n], ALU.pow)

        def pool_turn(pool, st, tn):
            i, j, u = tn.i, tn.j, tn.u
            if tn.end:
                pool_scatter(pool, NT)
                return
            if tn.sample:
                pool.wait_ge(s["dt_done"], NT)
                nc.gpsimd.memset(cmask[:, :, :], 0.0).then_inc(s["smp_zero"], 1)
            if tn.next2:
                pool.wait_ge(s["xsq_ready"], i + 3)
                fence(i, 1)
                root(pool, st, rs[:, 0:1], sq[:, 0:1], 1.0 / D, 1).then_inc(s["xr_ready"], 1)
            pool.wait_ge(s["ysq_ready"], i + 1)
            fence(i, 1)
            root(pool, st, rs[:, 2:4], sq[:, 2:4], 1.0 / 256, 2).then_inc(s["yr_ready"], 1)
            if tn.prev:
                pool_scatter(pool, i)
            if tn.next:
                pool_v(pool, st, i + 1)
                pool_dt(pool, st, i + 1)
            if isinstance(i, int) and i == NP - 1:
                pool.wait_ge(s["dt_done"], NT)
                nc.gpsimd.memset(ws_nat[:, :, :], 0.0).then_inc(s["smp_zero"], 1)
            pool.wait_ge(s["x2sq_ready"], i + 1)
            fence(i, 1)
            root(pool, st, rs[:, 1:2], sq[:, 1:2], 1.0 / D, 1).then_inc(s["x2r_ready"], 1)

        def pool_v(pool, st, t):
            pool.wait_ge(s["bn_ready"], t + 1)
            fence(t, 1)
            root(pool, st, rs[:, 4:5], mv[:, 1:2], 1.0, 1).then_inc(s["vr_ready"], 1)

        def pool_dt(pool, st, t):
            g = nc.gpsimd
            pool.wait_ge(s["dtrec_ready"], t + 1)
            after(pool, s["xw_ready"], t)
            r, r2, a = dtw[:, 5, :], dtw[:, 6, :], dtw[:, 7, :]
            st.link(g.tensor_tensor(r, dtw[:, 2, :], dtw[:, 4, :], ALU.mult))
            st.link(g.tensor_tensor(r2, r, r, ALU.mult))
            st.link(g.tensor_scalar(a, r2, ARTANH[4], ARTANH[3], ALU.mult, ALU.add))
            for k in (2, 1, 0):
                st.link(g.tensor_tensor(a, a, r2, ALU.mult))
                st.link(g.tensor_scalar(a, a, ARTANH[k], None, ALU.add))
            st.inc(g.tensor_scalar(dtw[:, 3, :], dtw[:, 0, :], 0.0, None, ALU.max))
            st.link(g.tensor_tensor(a, a, r, ALU.mult))
            st.link(g.tensor_tensor(dt_t[:, :], a, dtw[:, 3, :], ALU.add))
            g.tensor_tensor(adt[:, :], dt_t[:, :], aneg_b[:, :], ALU.mult).then_inc(s["dt_ready"], 1)
            pool.wait_ge(s["dt_ready"], t + 1)
            after(pool, s["ydiag_done"], t)
            mask = tri_s if isinstance(t, int) and t == NP else tri
            g.tensor_tensor(dec[:, :, :], over(mask, H), adt[:, :].rearrange("p (h a) -> p h a", a=1).broadcast_to([P, H, P]),
                            ALU.mult).then_inc(s["trid_ready"], 1)

        def pool_scatter(pool, i):
            pool.wait_ge(s["slots_ready"], i)
            fence(i, 2)
            if isinstance(i, int) and i == 1:
                pool.wait_ge(slots_zeroed, 16 * 8)
            for k in range(2):
                nc.gpsimd.indirect_dma_start(out=slot_d[:, :], out_offset=bass.IndirectOffsetOnAxis(ap=slots[:, k:k + 1], axis=0),
                                             in_=slots[:, 2:3], in_offset=None).then_inc(scattered, 16)

        def pool_phase1(pool):
            g = nc.gpsimd
            st = Steps(pool, pool_step, fence)

            def select(out, in_, op, fill, base, pattern, mult):
                st.link(g.affine_select(out=out, in_=in_, compare_op=op, fill=fill, base=base, pattern=pattern,
                                        channel_multiplier=mult))
            g.memset(neg_half[:], -0.5).then_inc(s["started"], 1)
            st.inc(g.memset(ident[:], 0.0))
            st.inc(g.memset(ones[:], 1.0))
            st.inc(g.memset(row_s[:], 1.0))
            st.link(g.memset(slot_zero[:], 0))
            select(ident[:], ident[:], ALU.not_equal, 1.0, 0, [[-1, P]], 1)
            select(tri[:], ones[:], ALU.is_ge, 0.0, 0, [[1, P]], -1)
            select(stri[:], ones[:], ALU.is_gt, 0.0, 0, [[1, P]], -1)
            q_of = blk_s[:].rearrange("p (q l) -> p q l", q=SB)
            select(row_s[:], row_s[:], ALU.is_ge, 0.0, 0, [[-SL, SB]], 1)
            select(row_s[:], row_s[:], ALU.is_ge, 0.0, SL - 1, [[SL, SB]], -1)
            select(q_of, ones[:].rearrange("p (q l) -> p q l", q=SB), ALU.is_ge, 0.0, 0, [[-SL, SB], [0, SL]], 1)
            select(q_of, q_of, ALU.is_ge, 0.0, SL - 1, [[SL, SB], [0, SL]], -1)
            st.link(g.tensor_tensor(tri_s[:], tri[:], blk_s[:], ALU.mult))
            st.inc(g.iota(iota_i[:, 0:NG], pattern=[[1, NG]], base=-NG, channel_multiplier=0))
            st.inc(g.iota(iota_i[:, NG:NR], pattern=[[1, NE]], base=-NE, channel_multiplier=0))
            st.inc(g.iota(iota_i[:, NR:NR + 1], pattern=[[1, 1]], base=0, channel_multiplier=1))
            st.link(g.iota(iota_i[:, NR + 1:], pattern=[[1, NBLK]], base=0, channel_multiplier=0))
            st.inc(g.tensor_copy(iota_g[:], iota_i[:, 0:NG]))
            st.inc(g.tensor_copy(iota_e[:], iota_i[:, NG:NR]))
            st.inc(g.tensor_copy(iota_b[:], iota_i[:, NR + 1:]))
            g.tensor_copy(tok_id[:], iota_i[:, NR:NR + 1]).then_inc(s["consts"], 1)
            for t in range(2):
                pool.wait_ge(s["xsq_ready"], t + 1)
                if t == 1:
                    pool.wait_ge(s["x_scaled"], 1)
                root(pool, st, rs[:, 0:1], sq[:, 0:1], 1.0 / D, 1).then_inc(s["xr_ready"], 1)
            pool_dt(pool, st, 0)
            pool_v(pool, st, 0)
            over_tiles(pool, lambda tn: pool_turn(pool, st, tn), st, POOL_TURN)
            return st

        def sp_turn(sp, tn):
            i, j, u = tn.i, tn.j, tn.u
            v = 1 - u
            if tn.next3:
                sp.wait_ge(s["xT_full"], 2 * (i + 2))
                sp.dma_start(x_in[v][:, :], input_tile(i + 3)).then_inc(x_loaded[v], 16)
            if tn.prev:
                sp.wait_ge(s["h2_ready"], i)
                sp.dma_start(at_tile(x2_tiles, i - 1), x_res[v][:, :]).then_inc(x2_stored, 16)
                sp.dma_start(at_tile(h2_tiles, i - 1), h2[:, :]).then_inc(h2_stored, 16)
            if tn.next:
                after(sp, x2_stored, 16 * i)
                sp.dma_start(x_res[v][:, :], input_tile(i + 1)).then_inc(res_loaded[v], 16)
            if isinstance(i, int) and i == NP - 1:
                sp.wait_ge(s["xbc1_out"], NP)
                sp.dma_start(conv_prompt[0, 0, :, :], xbc[P - CW + 1:, :]).then_inc(convp_stored, 16)
                sp.wait_ge(s["dt_done"], NT)
                sp.dma_start(cache_sb[0:SB * (CW - 1), :], cache_conv.rearrange("a q l c -> (a q l) c")).then_inc(smp_cache_loaded, 16)
                sp.dma_start(st_old, state_ssm.rearrange("a q (b h) d n -> (h d) (a q) b n", b=4)).then_inc(smp_st_loaded, 16)
                sp.wait_ge(s["smp_zero"], 1)
                for q in range(SB):
                    c = slice(q * SL, (q + 1) * SL)
                    sp.dma_start(ws_nat[c, :, c], w_spatial[0, :, 0:SL, 0:SL].rearrange("h t s -> t h s")).then_inc(smp_ws_loaded, 16)
            if tn.sample:
                sp.wait_ge(s["xbc1_out"], NT)
                for k in range(CW - 1):
                    sp.dma_start(conv_sample[0, :, k, :], xbc[SL - CW + 1 + k::SL, :]).then_inc(convs_stored, 16)
                sp.wait_ge(s["v_ready"], NT)
                sp.dma_start(gmlp_v_sample.rearrange("a q l c -> (a q l) c"), gv[:, :]).then_inc(vs_stored, 16)
            if tn.end:
                sp.wait_ge(s["smp_new"], 8)
                sp.dma_start(ssm_sample.rearrange("a q (b h) d n -> (h d) (a q) b n", b=4), st_old).then_inc(ssm_stored, 16)
                sp.wait_ge(s["stateT_out"], 1)
                sp.dma_start(ssm_prompt.rearrange("a q (b h) d n -> (h d) (a q b) n", b=4),
                             tmp[:, :].rearrange("p (b n) -> p b n", b=4)).then_inc(ssm_stored, 16)

        def sp_phase1(sp):
            for u in range(2):
                sp.dma_start(x_in[u][:, :], input_tile(u)).then_inc(x_loaded[u], 16)

            def row(dst, src):
                sp.dma_start(dst, src).then_inc(const_loaded, 16)
                count[0] += 1
            count = [0]
            row(rows[R_G1:R_G1 + KD, :], norm1_g.rearrange("a (k p) -> (a k) p", p=P))
            row(rows[R_CBIAS:R_CBIAS + CB, :], conv_b.rearrange("a (k p) -> (a k) p", p=P))
            row(rows[R_CW:R_BSP, :], conv_w.rearrange("a w (k p) -> (a w k) p", p=P))
            row(rows[R_BSP:R_SG, :], b_spatial[0, :, :])
            row(rows[R_SG:R_BSS, :], ssm_norm_g.rearrange("a (k p) -> (a k) p", p=P))
            for q in range(SB):
                row(rows[R_BSS:NROW, q * SL:(q + 1) * SL], b_spatial[0, :, 0:SL])
            for k, w in enumerate((dt_bias, a_log, d_skip)):
                row(small_b[:, k * H:(k + 1) * H], w.broadcast_to([P, H]))
            row(rb_b[:, 0:NG], b_rg.broadcast_to([P, NG]))
            row(rb_b[:, NG:], b_re.broadcast_to([P, NE]))
            row(g2_b[:, :], norm2_g.broadcast_to([P, D]))
            row(lng_b[:, :], ln_v_g.broadcast_to([P, W]))
            row(lnb_b[:, :], ln_v_b.broadcast_to([P, W]))
            row(wr_sb[:, :, 0:NG], w_rg[0, :, :].rearrange("(k p) n -> p k n", p=P))
            row(wr_sb[:, :, NG:], w_re[0, :, :].rearrange("(k p) n -> p k n", p=P))
            assert count[0] == N_CONST, count
            sp.dma_start(xc[:, :, :], w_spatial[0, :, :, :].rearrange("h t s -> t h s")).then_inc(ws_loaded, 16)
            w_rows = w_in[0, :, :].rearrange("(k p) n -> p k n", p=P)
            for k in range(2):
                sp.dma_start(w_in_sb[:, half(k), :], w_rows[:, half(k), :]).then_inc(win_loaded[k], 16)
            sp.dma_start(x_res[0][:, :], input_tile(0)).then_inc(res_loaded[0], 16)
            sp.dma_start(w_out_sb[:, :, :], w_out[0, :, :].rearrange("(k p) n -> p k n", p=P)).then_inc(wout_loaded, 16)
            sp.wait_ge(s["xT_full"], 2)
            sp.dma_start(x_in[0][:, :], input_tile(2)).then_inc(x_loaded[0], 16)
            sp.wait_ge(s["consts"], 1)
            for k in range(8):
                sp.dma_start(slot_d.rearrange("(c p n) a -> c p (n a)", c=8, p=P)[k, :, :], slot_zero[:, :]).then_inc(slots_zeroed, 16)
            over_tiles(sp, lambda tn: sp_turn(sp, tn))

        TAB_OFF, TAB_SLOT, TAB_WAIT = 0, 1, 2
        hTb = xdt[:, 0:2 * P].rearrange("p (k t) -> p k t", k=2)
        silu_g = [ycat[:, 0:DE], ycat[:, DE:2 * DE]]
        YBv = YB[:, 0:2 * P].rearrange("p (k t) -> p k t", k=2)

        def over_blocks(eng, turn):
            turn(0, 0, False)
            turn(0, 1, False)
            last = NBLK // 2 - 1
            with eng.Fori(1, last) as j:
                turn(j, 0, False)
                turn(j, 1, False)
            turn(last, 0, False)
            turn(last, 1, True)

        def dve_tables(dve, st):
            cnt, nb, pend, pstart = eqt[:, :], em[:, :], oh[:, 0, :], oh[:, 1, :]
            st.link(V.tensor_scalar(tab_i[:, 0:NE], carry[:, :], float(P - 1), None, ALU.add))
            st.link(V.tensor_scalar(tab_i[:, NE:2 * NE], tab_i[:, 0:NE], 7, None, ALU.logical_shift_right))
            st.link(V.tensor_copy(nb, tab_i[:, NE:2 * NE]))
            st.link(V.tensor_tensor_scan(out=pend, data0=ones[:, 0:NE], data1=nb, initial=0.0, op0=ALU.mult, op1=ALU.add))
            st.inc(V.tensor_tensor(pstart, pend, nb, ALU.subtract))
            st.link(V.tensor_scalar(pend_i[:, :], pend, 1.0, None, ALU.add))
            shape = [P, NBLK, NE]

            def over_b(x):
                return x.rearrange("p (a e) -> p a e", a=1).broadcast_to(shape)

            def over_e(x):
                return x.rearrange("p (b a) -> p b a", a=1).broadcast_to(shape)
            st.link(V.tensor_tensor(cmp_t, over_b(pend), over_e(iota_b[:, :]), ALU.is_le))
            st.link(V.tensor_reduce(tab_f[:, 0, :], cmp_t, AX.X, ALU.add))
            st.link(V.tensor_scalar(tab_f[:, 0, :], tab_f[:, 0, :], float(NE - 1), float(-NE), ALU.min, ALU.add))
            st.link(V.tensor_tensor(cmp_t, over_b(iota_e[:, :]), over_e(tab_f[:, 0, :]), ALU.is_equal))
            st.link(V.tensor_tensor(cmp_t, cmp_t, over_b(pstart), ALU.mult))
            st.link(V.tensor_reduce(tab_f[:, 1, :], cmp_t, AX.X, ALU.add))
            st.link(V.tensor_tensor(tab_f[:, 1, :], iota_b[:, :], tab_f[:, 1, :], ALU.subtract))
            st.link(V.tensor_scalar(tab_f[:, 1, :], tab_f[:, 1, :], float(T // P - 1), float(P), ALU.min, ALU.mult))
            st.link(V.scalar_tensor_tensor(out=tab_f[:, 1, :], in0=tab_f[:, 0, :], scalar=float(T), in1=tab_f[:, 1, :],
                                           op0=ALU.mult, op1=ALU.add))
            st.inc(V.tensor_scalar(tab[:, TAB_OFF, :], tab_f[:, 1, :], float(NE * T), None, ALU.add))
            st.inc(V.tensor_scalar(tab[:, TAB_WAIT, :], tab_f[:, 0, :], float(NE + 1), 48.0, ALU.add, ALU.mult))
            st.link(V.tensor_scalar(tab_b[:, :], tab_f[:, 0, :], float(NE), None, ALU.add))
            st.link(V.tensor_scalar(tab_b[:, :], tab_b[:, :], 1, None, ALU.bitwise_and))
            V.tensor_scalar(tab[:, TAB_SLOT, :], tab_b[:, :], float(WSLOT), None, ALU.mult).then_inc(s["tables"], 1)
            shape2 = [P, 2 * NT, NE]

            def over_t(x):
                return x.rearrange("p (a e) -> p a e", a=1).broadcast_to(shape2)
            pk = flat(pickk[:, :, :])
            st.link(V.tensor_copy(pickk[:, :, :], picks[:, :, 0:2]))
            st.link(V.tensor_tensor(pos_t, over_t(iota_e[:, :]), pk.rearrange("p (t a) -> p t a", a=1).broadcast_to(shape2), ALU.is_equal))
            st.link(V.tensor_tensor(pos_t, pos_t, over_t(pstart), ALU.mult))
            st.link(V.tensor_reduce(pk, pos_t, AX.X, ALU.add))
            st.link(V.scalar_tensor_tensor(out=rowpos[:, :, :], in0=pickk[:, :, :], scalar=float(P), in1=picks[:, :, 2:4],
                                           op0=ALU.mult, op1=ALU.add))

        def sp_phase2(sp):
            def load(e, slot):
                w = SLOT[slot]
                gup = w[:, 0:KD * 2 * DE].rearrange("p (k n) -> p k n", k=KD)
                dn = w[:, KD * 2 * DE:].rearrange("p (k n) -> p k n", k=2)

                def of(x):
                    return x[0, e, :, :] if isinstance(e, int) else x[0, bass.ds(e, 1), :, :].rearrange("a k n -> (a k) n")
                sp.dma_start(gup[:, :, 0:DE], of(w_gate).rearrange("(k p) n -> p k n", p=P)).then_inc(w_loaded, 16)
                sp.dma_start(gup[:, :, DE:], of(w_up).rearrange("(k p) n -> p k n", p=P)).then_inc(w_loaded, 16)
                sp.dma_start(dn, of(w_down).rearrange("(k p) n -> p k n", p=P)).then_inc(w_loaded, 16)

            sp.wait_ge(ssm_stored, 32)
            sp.wait_ge(s["smp_new"], 8)
            load(0, 0)
            sp.wait_ge(w_loaded, 48)
            load(1, 1)
            sp.wait_ge(s["tables"], 1)
            with sp.Fori(1, NE // 2) as m:
                for c in range(2):
                    e = 2 * m + c
                    before = sp.value_load(pend_i[0:1, bass.ds(e - 2, 1)], min_val=1, max_val=NBLK + 1)
                    sp.wait_ge(w_loaded, 48 * e)
                    sp.wait_ge(s["dn_full"], before)
                    load(e, c)

        def pool_phase2(pool):
            pool.wait_ge(scattered, 32 * NT)
            pool.wait_ge(h2_stored, 16 * NT)
            pool.wait_ge(s["tables"], 1)

            def numbers(b, u, j):
                off = pool.value_load(tab[0:1, TAB_OFF, bass.ds(b, 1)], min_val=0, max_val=(NE - 1) * T + T - P)
                pool.dma_start(idx[u][:, :], slot_d[bass.ds(off, P), :]).then_inc(idx_loaded[u], 16)

            def turn(j, u, last):
                b = 2 * j + u
                if not last:
                    numbers(b + 1, 1 - u, j)
                pool.wait_ge(idx_loaded[u], 16 * (j + 1))
                after(pool, s["gx_T"], 2 * (b - 1))
                after(pool, s["fenced"], b)
                nc.gpsimd.tensor_tensor(spare[:, 1:2], neg_half[:, 0:1], neg_half[:, 0:1], ALU.mult).then_inc(s["fenced"], 1)
                nc.gpsimd.indirect_dma_start(out=x_in[u][:, :], out_offset=None, in_=h2_d[:, :],
                                             in_offset=bass.IndirectOffsetOnAxis(ap=idx[u][:, 0:1], axis=0)).then_inc(gathered[u], 16)
                pool.wait_ge(gathered[u], 16 * (j + 1))
            numbers(0, 0, 0)
            over_blocks(pool, turn)

        def pe_rows(pe, u, j):
            b = 2 * j + u
            pe.wait_ge(gathered[u], 16 * (j + 1))
            for k in range(2):
                after(pe, s[f"gx_out{k}"], b)
                for c in range(4):
                    x = x_in[u][:, (4 * k + c) * P:(4 * k + c + 1) * P]
                    mm = nc.tensor.transpose(TB[k][:, c, :], x, ident[:])
                mm.then_inc(s["gx_T"], 1)

        def pe_gate_up(pe, u, j):
            b = 2 * j + u
            slot = pe.value_load(tab[0:1, TAB_SLOT, bass.ds(b, 1)], min_val=0, max_val=WSLOT)
            ready = pe.value_load(tab[0:1, TAB_WAIT, bass.ds(b, 1)], min_val=48, max_val=48 * NE)
            pe.wait_ge(w_loaded, ready)
            for k in range(2):
                pe.wait_ge(s[f"gx_out{k}"], b + 1)
            after(pe, s["hb_ready"], b - 1)
            for k in range(KD):
                mm = nc.tensor.matmul(PB[u][:, :], hT[u][:, k, :], arena[:, bass.ds(slot + k * 2 * DE, 2 * DE)],
                                      start=k == 0, stop=k == KD - 1)
            mm.then_inc(s["gu_full"], 1)

        def pe_phase2(pe):
            pe.wait_ge(s["tables"], 1)
            pe.wait_ge(s["stateT_out"], 1)
            pe.wait_ge(s["h2T_out"], 2 * NT)
            pe.wait_ge(s["h2_ready"], NT)
            pe.wait_ge(s["smp_new"], 8)

            def turn(j, u, last):
                b = 2 * j + u
                nj, nu = (j, 1) if u == 0 else (j + 1, 0)
                if not last:
                    pe_rows(pe, nu, nj)
                    pe_gate_up(pe, nu, nj)
                pe.wait_ge(s["hb_ready"], b + 1)
                after(pe, s["hbT_out"], b)
                for k in range(2):
                    mm = nc.tensor.transpose(YBv[:, k, :], hb2[u][:, k * P:(k + 1) * P], ident[:])
                mm.then_inc(s["hbT_full"], 1)
                slot = pe.value_load(tab[0:1, TAB_SLOT, bass.ds(b, 1)], min_val=0, max_val=WSLOT)
                pe.wait_ge(s["hbT_out"], b + 1)
                for n in range(2):
                    after(pe, s[f"dn_out{n}"], b)
                    for k in range(2):
                        mm = nc.tensor.matmul(SS[:, n, :], hTb[:, k, :],
                                              arena[:, bass.ds(slot + KD * 2 * DE + k * D + n * 512, 512)],
                                              start=k == 0, stop=k == 1)
                mm.then_inc(s["dn_full"], 1)
            pe_rows(pe, 0, 0)
            pe_gate_up(pe, 0, 0)
            over_blocks(pe, turn)

        def act_phase2(act):
            act.wait_ge(x2_stored, 16 * NT)

            def rows0(b, u):
                act.wait_ge(s["gx_T"], 2 * b + 1)
                after(act, s["gu_full"], b - 1)
                nc.scalar.activation(hT[u][:, half(0), :], TB[0][:, :, :], ACT.Copy).then_inc(s["gx_out0"], 1)

            def turn(j, u, last):
                b = 2 * j + u
                if not last:
                    rows0(b + 1, 1 - u)
                act.wait_ge(s["gu_full"], b + 1)
                after(act, s["hb_ready"], b - 1)
                nc.scalar.activation(silu_g[u], PB[u][:, 0:DE], ACT.Silu).then_inc(s["silu_out"], 1)
                act.wait_ge(s["hbT_full"], b + 1)
                after(act, s["dn_full"], b + 1)
                nc.scalar.activation(hTb, YBv, ACT.Copy).then_inc(s["hbT_out"], 1)
                act.wait_ge(s["dn_full"], b + 2)
                after(act, ys_stored[u], 16 * j)
                nc.scalar.activation(x_res[u][:, 0:512], SS[:, 0, :], ACT.Copy).then_inc(s["dn_out0"], 1)
                act.wait_ge(s["dn_out1"], b + 1)
                act.wait_ge(s["dn_out0"], b + 1)
                act.dma_start(at_tile(ys_tiles, b), x_res[u][:, :]).then_inc(ys_stored[u], 16)
            rows0(0, 0)
            over_blocks(act, turn)

        def dve_phase2(dve):
            def rows1(b, u):
                dve.wait_ge(s["gx_T"], 2 * b + 2)
                after(dve, s["gu_full"], b - 1)
                V.tensor_copy(hT[u][:, half(1), :], TB[1][:, :, :]).then_inc(s["gx_out1"], 1)

            def turn(j, u, last):
                b = 2 * j + u
                if not last:
                    rows1(b + 1, 1 - u)
                dve.wait_ge(s["silu_out"], b + 1)
                after(dve, s["hbT_full"], b - 1)
                V.tensor_tensor(hb2[u], silu_g[u], PB[u][:, DE:], ALU.mult).then_inc(s["hb_ready"], 1)
                dve.wait_ge(s["dn_full"], b + 2)
                after(dve, ys_stored[u], 16 * j)
                V.tensor_copy(x_res[u][:, 512:], SS[:, 1, :]).then_inc(s["dn_out1"], 1)
            dve.wait_ge(x2_stored, 16 * NT)
            rows1(0, 0)
            over_blocks(dve, turn)

        def over_out(eng, turn):
            turn(0, 0)
            turn(0, 1)
            with eng.Fori(1, NP // 2) as j:
                turn(j, 0)
                turn(j, 1)
            turn(NP // 2, 0)

        def sp_phase3(sp):
            sp.wait_ge(s["dn_full"], NBLK + 1)
            sp.dma_start(gf_b, final_norm_g.rearrange("(a n) -> a n", a=1).broadcast_to([P, D])).then_inc(gf_loaded, 16)
            for u in range(2):
                sp.wait_ge(s["gx_T"], 2 * NBLK)
                sp.dma_start(x_in[u][:, :], x2_tiles[u, :, :]).then_inc(fx_loaded[u], 16)

            def turn(j, u):
                t = 2 * j + u
                sp.wait_ge(s["fin_out"], t + 1)
                known = isinstance(t, int)
                out = y_sample.rearrange("b l d -> (b l) d") if known and t == NP else at_tile(y_tiles, t)
                sp.dma_start(out, fin_o[u]).then_inc(fy_stored[u], 16)
                if not known or t + 2 <= NP:
                    sp.dma_start(x_in[u][:, :], at_tile(x2_tiles, t + 2)).then_inc(fx_loaded[u], 16)
            turn(0, 0)
            turn(0, 1)
            with sp.Fori(1, NP // 2 - 1) as j:
                turn(j, 0)
                turn(j, 1)
            for t in range(NP - 2, NT):
                turn(t // 2, t % 2)
            for u in range(2):
                sp.wait_ge(fy_stored[u], 16 * (NP // 2 + 1 - u))
            for sm, n in ((convp_stored, 1), (convs_stored, CW - 1), (vs_stored, 1), (ssm_stored, 2), (x2_stored, NT), (h2_stored, NT)):
                sp.wait_ge(sm, 16 * n)

        def pool_phase3(pool, st):
            for u in range(2):
                pool.wait_ge(ys_stored[u], 16 * (NBLK // 2))

            def turn(j, u):
                t = 2 * j + u
                pool.wait_ge(s["fin_idx"], t + 1)
                after(pool, s["fin_out"], t - 1)
                fence(t, 2)
                for k in range(2):
                    nc.gpsimd.indirect_dma_start(out=y_row[u][k], out_offset=None, in_=ys_d[:, :],
                                                 in_offset=bass.IndirectOffsetOnAxis(ap=fidx[u][:, k:k + 1], axis=0)).then_inc(fy_gathered[u], 16)
                if isinstance(t, int) and t == 0:
                    return
                pool_r(t - 1)

            def pool_r(t):
                pool.wait_ge(s["fin_sq"], t + 1)
                fence(t, 1)
                nc.gpsimd.tensor_scalar(rs[:, 0:1], sq[:, 0:1], 1.0 / D, EPS, ALU.mult, ALU.add).then_inc(pool_fin, 1)
                pool.wait_ge(pool_fin, t + 1)
                nc.gpsimd.tensor_tensor(rs[:, 0:1], rs[:, 0:1], neg_half[:, 0:1], ALU.pow).then_inc(s["fin_r"], 1)
            over_out(pool, turn)
            pool_r(NP)

        def act_phase3(act):
            def turn(j, u):
                t = 2 * j + u
                act.wait_ge(fin_add, t + 1)
                nc.scalar.activation(fin_s, x_in[u][:, :], ACT.Square, accum_out=sq[:, 0:1]).then_inc(s["fin_sq"], 1)
                act.wait_ge(s["fin_sq"], t + 1)
            over_out(act, turn)

        def dve_phase3(dve):
            def turn(j, u):
                t = 2 * j + u
                known = isinstance(t, int)
                dve.wait_ge(fx_loaded[u], 16 * (j + 1))
                dve.wait_ge(fy_gathered[u], 32 * (j + 1))
                if not known or t + 2 <= NP:
                    src = rowpos[:, t + 2, :] if known else rowpos[:, bass.ds(t + 2, 1), :].rearrange("p a c -> p (a c)")
                    V.tensor_copy(fidx[u][:, :], src).then_inc(s["fin_idx"], 1)
                w = picks[:, t, 4:6] if known else picks[:, bass.ds(t, 1), 4:6].rearrange("p a c -> p (a c)")
                after(dve, s["fin_out"], t)
                V.tensor_copy(wts[:, :], w).then_inc(fin_w, 1)
                dve.wait_ge(fin_w, t + 1)
                V.scalar_tensor_tensor(out=x_in[u][:, :], in0=y_row[u][0], scalar=wts[:, 0:1], in1=x_in[u][:, :],
                                       op0=ALU.mult, op1=ALU.add).then_inc(fin_one, 1)
                dve.wait_ge(fin_one, t + 1)
                V.scalar_tensor_tensor(out=x_in[u][:, :], in0=y_row[u][1], scalar=wts[:, 1:2], in1=x_in[u][:, :],
                                       op0=ALU.mult, op1=ALU.add).then_inc(fin_add, 1)
                dve.wait_ge(s["fin_r"], t + 1)
                after(dve, fy_stored[u], 16 * j)
                V.scalar_tensor_tensor(out=fin_o[u], in0=x_in[u][:, :], scalar=rs[:, 0:1], in1=gf_b,
                                       op0=ALU.mult, op1=ALU.mult).then_inc(s["fin_out"], 1)
            dve.wait_ge(gf_loaded, 16)
            for u in range(2):
                V.tensor_copy(fidx[u][:, :], rowpos[:, u, :]).then_inc(s["fin_idx"], 1)
            turn(0, 0)
            turn(0, 1)
            with dve.Fori(1, NP // 2 - 1) as j:
                turn(j, 0)
                turn(j, 1)
            for t in range(NP - 2, NT):
                turn(t // 2, t % 2)

        block = ctx.enter_context(nc.Block())

        @block.tensor
        def _(pe):
            pe_phase1(pe)
            pe_phase2(pe)

        @block.scalar
        def _(act):
            act_phase1(act)
            act_phase2(act)
            act_phase3(act)

        @block.vector
        def _(dve):
            st = dve_phase1(dve)
            dve_tables(dve, st)
            dve_phase2(dve)
            dve_phase3(dve)

        @block.gpsimd
        def _(pool):
            st = pool_phase1(pool)
            pool_phase2(pool)
            pool_phase3(pool, st)

        @block.sync
        def _(sp):
            sp_phase1(sp)
            sp_phase2(sp)
            sp_phase3(sp)


_INS = ["x_prompt", "x_sample", "cache_conv", "state_ssm", "norm1_g", "w_in", "conv_w", "conv_b", "dt_bias", "a_log",
        "d_skip", "ssm_norm_g", "ln_v_g", "ln_v_b", "w_spatial", "b_spatial", "w_out", "norm2_g",
        "w_router_group", "b_router_group", "w_router_expert", "b_router_expert", "w_gate", "w_up", "w_down",
        "final_norm_g"]
_OUTS = [(1, SEQ, D), (SB, SL, D), (1, 1, CW - 1, CD), (1, 1, H, HD, N), (1, SB, CW - 1, CD), (1, SB, H, HD, N),
         (1, SB, SL, W)]


def kernel(**inputs):
    import numpy as _np
    import concourse.bacc as _bacc
    from concourse.bass_utils import run_bass_kernel_spmd as _run

    nc = _bacc.Bacc("TRN2", target_bir_lowering=False, num_devices=1)
    arrays, args = {}, []
    for name in _INS:
        a = _np.ascontiguousarray(inputs[name])
        arrays[f"in_{name}"] = a
        args.append(nc.dram_tensor(f"in_{name}", a.shape, mybir.dt.from_np(a.dtype), kind="ExternalInput").ap())
    for i, shape in enumerate(_OUTS):
        args.append(nc.dram_tensor(f"out_{i}", shape, F32, kind="ExternalOutput").ap())
    build(nc, *args)
    r = _run(nc, [arrays], core_ids=[0])
    return tuple(r.results[0][f"out_{i}"] for i in range(len(_OUTS)))
```

```python
from contextlib import ExitStack

import concourse.bass as bass
from concourse import mybir

F32 = mybir.dt.float32
I32 = mybir.dt.int32
U32 = mybir.dt.uint32
ALU = mybir.AluOpType
ACT = mybir.ActivationFunctionType
AX = mybir.AxisListType

P = 128
D = 1024
KD = D // P
SEQ = 4096
NP = SEQ // P
NT = NP + 1
T = NT * P
SB, SL = 8, 16
H, HD = 8, 64
G, N = 2, 128
W = H * HD
CD = W + 2 * G * N
CB = CD // P
CW = 4
INP = W + CD + H + 2 * W
COL_Z, COL_X, COL_DT, COL_GU, COL_GV = 0, W, W + CD, W + CD + H, W + CD + H + W
NG, EG = 4, 8
NE = NG * EG
DE = 256
NR = NG + NE
R_G1, R_CBIAS, R_CW = 0, KD, KD + CB
R_BSP = R_CW + CW * CB
R_SG = R_BSP + H
R_BSS = R_SG + W // P
NROW = R_BSS + H
N_CONST = 5 + SB + 3 + 2 + 3 + 2
NBLK = 2 * T // P + NE
EPS = 1e-6
ARTANH = (2.000000007681758, 0.6666632164140268, 0.40024595229739224, 0.27965157758356346, 0.28157778304302755)
BIG = 1e30


class Steps:

    def __init__(self, eng, sem, fence=lambda n, k: None):
        self.eng, self.sem, self.base, self.n, self.fence = eng, sem, 0, 0, fence

    def inc(self, ins):
        self.n += 1
        ins.then_inc(self.sem, 1)

    def wait(self):
        self.eng.wait_ge(self.sem, self.base + self.n)
        self.fence(self.base, 0)

    def link(self, ins):
        self.inc(ins)
        self.wait()

    def loop_begin(self, per_turn):
        self.before, self.per_turn = self.base + self.n, per_turn

    def loop_at(self, turn):
        self.base, self.n = turn * self.per_turn + self.before, 0

    def loop_end(self, turns):
        assert self.n == self.per_turn, (self.n, self.per_turn)
        self.base, self.n = self.before + turns * self.per_turn, 0


def after(eng, sem, n):
    if isinstance(n, int) and n <= 0:
        return
    eng.wait_ge(sem, n)


DVE_TURN, POOL_TURN = 102, 32


def build(nc, x_prompt, x_sample, cache_conv, state_ssm, norm1_g, w_in, conv_w, conv_b, dt_bias, a_log,
          d_skip, ssm_norm_g, ln_v_g, ln_v_b, w_spatial, b_spatial, w_out, norm2_g,
          w_rg, b_rg, w_re, b_re, w_gate, w_up, w_down, final_norm_g,
          y_prompt, y_sample, conv_prompt, ssm_prompt, conv_sample, ssm_sample, gmlp_v_sample):
    ctx = ExitStack()
    with ctx:
        def sb(name, shape, dt=F32):
            return ctx.enter_context(nc.sbuf_tensor(name, shape, dt))

        def ps(name, shape):
            return ctx.enter_context(nc.psum_tensor(name, shape, F32))

        def sem(name):
            return ctx.enter_context(nc.semaphore(name))

        x2_d = nc.dram_tensor("x2_rows", [T, D], F32).ap()
        h2_d = nc.dram_tensor("h2_rows", [T, D], F32).ap()
        ys_d = nc.dram_tensor("expert_rows", [NBLK * P, D], F32).ap()
        slot_d = nc.dram_tensor("slot_tokens", [NE * T, 1], I32).ap()

        ARENA = KD * INP
        arena = sb("arena", [P, ARENA])
        w_in_sb = arena[:, :].rearrange("p (k n) -> p k n", k=KD)
        w_out_sb = sb("w_out_sb", [P, KD, D])

        ident = sb("ident", [P, P])
        tri = sb("tri", [P, P])
        stri = sb("stri", [P, P])
        tri_s = sb("tri_s", [P, P])
        blk_s = sb("blk_s", [P, P])
        ones = sb("ones", [P, P])
        row_s = sb("row_s", [P, SB])
        iota_g = sb("iota_g", [P, NG])
        iota_e = sb("iota_e", [P, NE])
        neg_half = sb("neg_half", [P, 2])
        tok_id = sb("tok_id", [P, 1])
        g2_b = sb("g2_b", [P, D])
        lng_b = sb("lng_b", [P, W])
        lnb_b = sb("lnb_b", [P, W])
        small_b = sb("small_b", [P, 3 * H])
        dtb_b, alog_b, dsk_b = (small_b[:, k * H:(k + 1) * H] for k in range(3))
        aneg_b = sb("aneg_b", [P, H])
        rb_b = sb("rb_b", [P, NR])
        wr_sb = sb("wr_sb", [P, KD, NR])
        wsT = sb("wsT", [P, H, P])
        slot_zero = sb("slot_zero", [P, NE * T // P // 8], I32)
        cols = sb("cols", [P, NROW])

        x_in = [sb(f"x_in{u}", [P, D]) for u in range(2)]
        x_res = [sb(f"x_res{u}", [P, D]) for u in range(2)]
        hT = [sb(f"hT{u}", [P, KD, P]) for u in range(2)]
        xbc = sb("xbc", [P, CD])
        xT = sb("xT", [P, CB, P + CW - 1])
        xc = sb("xc", [P, CB, P])
        xtok = sb("xtok", [P, W])
        btok = sb("btok", [P, G * N])
        gu = [sb("gu", [P, W])] * 2
        zz = [sb("zz", [P, W])] * 2
        gv = sb("gv", [P, W])
        dec = sb("dec", [P, H, P])
        cbm = sb("cbm", [P, G, P])
        xdt = sb("xdt", [P, W])
        xw = sb("xw", [P, W])
        state = sb("state", [P, W])
        yb = sb("yb", [P, W])
        tmp = sb("tmp", [P, W])
        ycat = sb("ycat", [P, D])
        tT = sb("tT", [P, KD, P])
        h2 = sb("h2", [P, D])
        rows = h2[0:NROW, 0:P]
        iota_i = ycat[:, 0:NR + 1].bitcast(I32)
        slots32 = ycat[:, 0:NE].bitcast(I32)
        dt_t = sb("dt_t", [P, H])
        adt = sb("adt", [P, H])
        dtw = sb("dtw", [P, 8, H])
        e_in = sb("e_in", [P, 3 * H])
        e_out = sb("e_out", [P, 3 * H])
        bn6 = sb("bn6", [P, 6])
        mv = sb("mv", [P, 2])
        sq = sb("sq", [P, 4])
        rs = sb("rs", [P, 8])
        lgs = sb("lgs", [P, NR])
        rt = sb("rt", [P, 16])
        gex = sb("gex", [P, NG + 1])
        gexo = sb("gexo", [P, NG + 1])
        eqt = sb("eqt", [P, NE])
        em = sb("em", [P, NE])
        oh = sb("oh", [P, 3, NE])
        rk = sb("rk", [P, NE])
        carry = sb("carry", [P, NE])
        slots = sb("slots", [P, 3], I32)
        spare = sb("spare", [P, 4])
        picks = sb("picks", [P, NT, 6])

        pend_i = sb("pend_i", [P, P], I32)
        tab = sb("tab", [P, 4, P], I32)
        misc = sb("misc", [P, 2], I32)
        tcol = sb("tcol", [P, 5])
        tok0 = sb("tok0", [P, 1])
        rowpos = sb("rowpos", [P, NT, 2], I32)
        idx = [sb(f"idx{u}", [P, 1], I32) for u in range(2)]
        hb2 = [gv[:, 0:DE], gv[:, DE:2 * DE]]

        PB = [ps(f"PB{u}", [P, 512]) for u in range(2)]
        TB = [ps(f"TB{u}", [P, 4, P]) for u in range(2)]
        SS = ps("SS", [P, 2, 512])
        YB = ps("YB", [P, 512])
        MB = ps("MB", [P, 512])
        dt_p, acs_p, tot_p = MB[:, 0:H], MB[:, H:2 * H], MB[:, 2 * H:3 * H]
        cb_p = MB[:, 32:32 + G * P]
        lg_p, rk_p, cnt_p = MB[:, 288:288 + NR], MB[:, 324:324 + NE], MB[:, 356:356 + NE]
        sd_p = MB[:, 400:400 + 4 * SB]


        names = """consts w_scaled eout_a cols_full cols_out ws_full ws_out
            xsq_ready xr_ready x_scaled xT_full xT_out
            proj0 proj1 proj_gv proj_gu proj_z xbc0_out xbc1_out gv_out gu_out z_out
            xbcT_full xbcT_out halo_saved conv_done zs_ready xc_ready cb_done xb_full xb_out
            dt_done dt_read lg_read cb_read rank_read dtneg_ready dtexp_ready dtrec_ready dt_ready trid_ready acs_done bcast_done
            ein_ready eout_ready seg_done decay_ready dec_ready xw_ready
            mixed_done bn_ready vr_ready v_ready ycat_hi
            ydiag_done yoff_done states_done state_ready gated_ready ysq_ready yr_ready ycat_ready
            ycT_full ycT_out out0 out1 x2_half x2sq_ready x2r_ready h2_ready
            h2T_full h2T_out logits_done gexin_ready gexout_ready pick_ready rank_done slots_ready
            smp_zero smp_cache_T smp_cache_out smp_ws_T smp_ws_out smp_st_T smp_st_out smp_masks smp_dec_full
            smp_dec_out smp_new stateT_full stateT_out
            tab_cols tab_rows tab_half fenced tables gx_T gx_out0 gx_out1 gu_full silu_out hb_ready hbT_full hbT_out dn_full dn_out0 dn_out1
            fin_add fin_idx fin_sq fin_r fin_out""".split()
        s = {n: sem(n) for n in names}
        x_loaded = [sem(f"x_loaded{u}") for u in range(2)]
        res_loaded = [sem(f"res_loaded{u}") for u in range(2)]
        win_loaded = [sem(f"win_loaded{k}") for k in range(2)]
        const_loaded, ws_loaded, wout_loaded = sem("const_loaded"), sem("ws_loaded"), sem("wout_loaded")
        slots_zeroed, scattered = sem("slots_zeroed"), sem("scattered")
        x2_stored, h2_stored = sem("x2_stored"), sem("h2_stored")
        convp_stored, convs_stored, vs_stored, ssm_stored = (sem(n) for n in ("convp_stored", "convs_stored", "vs_stored", "ssm_stored"))
        smp_cache_loaded, smp_st_loaded, smp_ws_loaded = sem("smp_cache_loaded"), sem("smp_st_loaded"), sem("smp_ws_loaded")
        w_loaded, ys_filled = sem("w_loaded"), sem("ys_filled")
        idx_loaded = [sem(f"idx_loaded{u}") for u in range(2)]
        gathered = [sem(f"gathered{u}") for u in range(2)]
        ys_stored = [sem(f"ys_stored{u}") for u in range(2)]
        fx_loaded = [sem(f"fx_loaded{r}") for r in range(4)]
        fy_gathered = [sem(f"fy_gathered{r}") for r in range(4)]
        fy_stored = [sem(f"fy_stored{u}") for u in range(2)]
        gf_loaded, fin_w, fin_one, pool_fin = (sem(n) for n in ("gf_loaded", "fin_w", "fin_one", "pool_fin"))
        dve_step, pool_step = sem("dve_step"), sem("pool_step")

        x_tiles = x_prompt.rearrange("a (t p) d -> (a t) p d", p=P)
        y_tiles = y_prompt.rearrange("a (t p) d -> (a t) p d", p=P)
        x2_tiles = x2_d.rearrange("(t p) d -> t p d", p=P)
        h2_tiles = h2_d.rearrange("(t p) d -> t p d", p=P)
        ys_tiles = ys_d.rearrange("(t p) d -> t p d", p=P)

        def at_tile(tiles, t):
            if isinstance(t, int):
                return tiles[t, :, :]
            return tiles[bass.ds(t, 1), :, :].rearrange("a p d -> (a p) d")

        def input_tile(t):
            if isinstance(t, int) and t == NP:
                return x_sample.rearrange("b l d -> (b l) d")
            return at_tile(x_tiles, t)

        used = [0]

        def take(n):
            used[0] += n
            assert used[0] <= ARENA, used[0]
            return arena[:, used[0] - n:used[0]]

        CMW = SB * (P + SL)
        st_old = take(SB * W).rearrange("p (q b n) -> p q b n", q=SB, b=4)
        st_T = take(SB * W).rearrange("p (q w) -> p q w", q=SB)
        cmask = take(G * CMW).rearrange("p (g w) -> p g w", g=G)
        bmask = take(G * SB * N).rearrange("p (g q n) -> p g q n", g=G, q=SB)
        wsT_s = take(H * P).rearrange("p (h t) -> p h t", h=H)
        ws_nat = take(H * P).rearrange("p (h t) -> p h t", h=H)
        xT_s = take(CB * SB * (SL + CW - 1)).rearrange("p (b q l) -> p b q l", b=CB, q=SB)
        cache_sb = take(CD)
        adt_e = take(W)
        st_dec = take(4 * SB)
        used[0] = 0
        WSLOT = KD * 2 * DE + 2 * D
        SLOT = [take(WSLOT) for _ in range(2)]
        pickk = take(2 * NT).rearrange("p (t a) -> p t a", a=2)
        pos_t = take(2 * NT * NE).rearrange("p (t e) -> p t e", e=NE)
        used[0] = 0
        FB = 4
        y_row = [[take(D) for _ in range(2)] for _ in range(FB)]
        x_row = [take(D) for _ in range(FB)]
        fin_o = [take(D) for _ in range(2)]
        gf_b = take(D)
        fin_s = take(D)
        fidx = [take(2).bitcast(I32) for _ in range(FB)]
        wts = [take(2) for _ in range(FB)]

        def half(b):
            return slice(4 * b, 4 * b + 4)

        def flat(ap):
            return ap.rearrange("p a b -> p (a b)")

        class Turn:

            def __init__(self, j, u):
                self.j, self.u = j, u
                self.i = 2 * j + u
                n = self.i if isinstance(self.i, int) else None
                self.first, self.sample, self.end = n == 0, n == NP, n == NT
                self.prev = not self.first
                self.next, self.next2, self.next3 = (n is None or n + k <= NP for k in (1, 2, 3))

        def over_tiles(eng, turn, steps=None, per_turn=0):
            turn(Turn(0, 0))
            turn(Turn(0, 1))
            last = NP // 2 - 2
            if steps:
                steps.loop_begin(per_turn)
            with eng.Fori(1, last) as j:
                if steps:
                    steps.loop_at(j - 1)
                turn(Turn(j, 0))
                turn(Turn(j, 1))
            if steps:
                steps.loop_end(last - 1)
            for i in range(2 * last, NT + 1):
                turn(Turn(i // 2, i % 2))

        def transpose8(pe, src, waits, done):
            for b in range(2):
                for sm, n in waits(b):
                    after(pe, s[sm], n)
                for k in range(4):
                    mm = nc.tensor.transpose(TB[b][:, k, :], src(4 * b + k), ident[:])
                mm.then_inc(s[done], 1)

        def block_of(t):
            return lambda c: t[:, c * P:(c + 1) * P]

        def project(pe, u, out, col, n, done, waits):
            for sm, v in waits:
                pe.wait_ge(s[sm], v)
            for k in range(KD):
                mm = nc.tensor.matmul(out, hT[u][:, k, :], w_in_sb[:, k, col:col + n], start=k == 0, stop=k == KD - 1)
            mm.then_inc(s[done], 1)

        def pe_turn(pe, tn):
            i, j, u = tn.i, tn.j, tn.u
            v = 1 - u
            if tn.end:
                pe_end(pe, tn)
                return
            if tn.sample:
                pe_sample_setup(pe)
            before = (lambda b: [("xT_out", 3 + b)]) if tn.first else \
                (lambda b: [("smp_st_out", SB - 1 + b)]) if tn.sample else (lambda b: [("ycT_out", 2 * i - 1 + b)])
            transpose8(pe, block_of(xbc), lambda b: [(f"xbc{b}_out", i + 1)] + before(b), "xbcT_full")
            cum, tot = (tri_s, blk_s) if tn.sample else (tri, ones)
            pe.wait_ge(s["dt_ready"], i + 1)
            pe.wait_ge(s["dt_read"], i + 1)
            nc.tensor.matmul(acs_p, cum[:], adt[:], start=True, stop=True)
            nc.tensor.matmul(tot_p, tot[:], adt[:], start=True, stop=True).then_inc(s["acs_done"], 1)
            pe.wait_ge(s["trid_ready"], i + 1)
            pe.wait_ge(s["state_ready"], i + 1)
            if tn.sample:
                pe.wait_ge(s["smp_cache_out"], 2)
            for b in range(2):
                mm = nc.tensor.matmul(SS[:, b, :], tot[:], flat(dec[:, half(b), :]), start=True, stop=True)
            mm.then_inc(s["bcast_done"], 1)
            if tn.next:
                project(pe, v, PB[0][:, :], COL_X, 512, "proj0",
                        [("xT_out", 2 * (i + 2)), ("gu_out", 1) if tn.first else ("x2_half", 2 * i - 1)])
            if tn.prev:
                pe.wait_ge(s["h2_ready"], i)
                transpose8(pe, block_of(h2), lambda b: [("xbcT_out", 2 * i + 1 + b)], "h2T_full")
            if tn.next:
                project(pe, v, PB[1][:, :], COL_X + 512, 512, "proj1",
                        [("z_out", 1) if tn.first else ("x2_half", 2 * i)])
            pe.wait_ge(s["xc_ready"], i + 1)
            after(pe, s["dec_ready"], i)
            pe.wait_ge(s["ein_ready"], i + 1)
            for g in range(G):
                mm = nc.tensor.matmul(cb_p[:, g * P:(g + 1) * P], xc[:, 4 + g, :], xc[:, 6 + g, :], start=True, stop=True)
            mm.then_inc(s["cb_done"], 1)
            for b in range(2):
                pe.wait_ge(*((s["xbcT_out"], 1 + b) if tn.first else (s["h2T_out"], 2 * i - 1 + b)))
                for k in range(4 - 2 * b):
                    mm = nc.tensor.transpose(TB[b][:, k, :], xc[:, 4 * b + k, :], ident[:])
                mm.then_inc(s["xb_full"], 1)
            if tn.prev:
                pe_router(pe, i)
            pe.wait_ge(s["v_ready"], i + 1)
            pe.wait_ge(*((s["xbc0_out"], i + 2) if tn.next else (s["x2_half"], 2 * i - 1)))
            if tn.first:
                pe.wait_ge(s["ws_out"], 2)
            ws = wsT_s if tn.sample else wsT
            for h in range(H):
                c = slice(h * HD, (h + 1) * HD)
                mm = nc.tensor.matmul(PB[0][:, c], ws[:, h, :], gv[:, c], start=True, stop=True)
            mm.then_inc(s["mixed_done"], 1)
            pe.wait_ge(s["dec_ready"], i + 1)
            pe.wait_ge(s["xw_ready"], i + 1)
            after(pe, s["gated_ready"], i)
            for h in range(H):
                c = slice(h * HD, (h + 1) * HD)
                mm = nc.tensor.matmul(YB[:, c], dec[:, h, :], xdt[:, c], start=True, stop=True)
            mm.then_inc(s["ydiag_done"], 1)
            if tn.sample:
                pe_sample_states(pe)
            else:
                for g in range(G):
                    c = slice(g * 256, (g + 1) * 256)
                    mm = nc.tensor.matmul(SS[:, 0, c], xc[:, 6 + g, :], state[:, c], start=True, stop=True)
                mm.then_inc(s["yoff_done"], 1)
                for g in range(G):
                    c = slice(g * 256, (g + 1) * 256)
                    mm = nc.tensor.matmul(SS[:, 1, c], btok[:, g * N:(g + 1) * N], xw[:, c], start=True, stop=True)
                mm.then_inc(s["states_done"], 1)
            if tn.next:
                project(pe, v, PB[1][:, :], COL_GV, 512, "proj_gv", [("xbc1_out", i + 2)])
            if tn.prev:
                pe_rank(pe, i, tn.sample)
            if tn.next:
                project(pe, v, PB[0][:, :], COL_GU, 512, "proj_gu", [("ycat_hi", i + 1)])
            if tn.next2:
                pe.wait_ge(s["x_scaled"], i + 3)
                transpose8(pe, block_of(x_in[u]), lambda b: [("xb_out", 2 * i + 1 + b)], "xT_full")
            if tn.next:
                project(pe, v, PB[1][:, :], COL_Z, 512, "proj_z", [("gv_out", i + 2)])
            pe.wait_ge(s["ycat_ready"], i + 1)
            transpose8(pe, block_of(ycat),
                       lambda b: [("xT_out", 2 * i + 5 + b) if tn.next2 else ("xb_out", 2 * i + 1 + b)], "ycT_full")
            if tn.next:
                project(pe, v, dt_p, COL_DT, H, "dt_done", [("cb_read", 1) if tn.first else ("rank_read", i)])
            pe.wait_ge(s["ycT_out"], 2 * (i + 1))
            if tn.first:
                pe.wait_ge(s["w_scaled"], 2)
            for b in range(2):
                if tn.next:
                    pe.wait_ge(s[("gu_out", "z_out")[b]], i + 2)
                else:
                    pe.wait_ge(*((s["ycat_hi"], i + 1) if b == 0 else (s["x2_half"], 2 * i)))
                for k in range(KD):
                    mm = nc.tensor.matmul(PB[b][:, :], tT[:, k, :], w_out_sb[:, k, b * 512:(b + 1) * 512],
                                          start=k == 0, stop=k == KD - 1)
                mm.then_inc(s[f"out{b}"], 1)

        def pe_router(pe, i):
            pe.wait_ge(s["h2T_out"], 2 * i)
            pe.wait_ge(*((s["rank_read"], NP) if isinstance(i, int) and i == NT else (s["cb_read"], i + 1)))
            for k in range(KD):
                mm = nc.tensor.matmul(lg_p, tT[:, k, :], wr_sb[:, k, :], start=k == 0, stop=k == KD - 1)
            mm.then_inc(s["logits_done"], 1)

        def pe_rank(pe, i, after_decay=False):
            pe.wait_ge(s["pick_ready"], i)
            if after_decay:
                pe.wait_ge(s["smp_dec_out"], 1)
            nc.tensor.matmul(rk_p, stri[:], oh[:, 2, :], start=True, stop=True)
            nc.tensor.matmul(cnt_p, ones[:], oh[:, 2, :], start=True, stop=True).then_inc(s["rank_done"], 1)

        def pe_sample_setup(pe):
            pe.wait_ge(smp_cache_loaded, 16)
            pe.wait_ge(s["state_ready"], NP + 1)
            R = SB * (CW - 1)
            for c in range(CB):
                mm = nc.tensor.transpose(SS[:, c // 4, (c % 4) * R:(c % 4 + 1) * R], cache_sb[0:R, c * P:(c + 1) * P],
                                         ident[0:R, 0:R])
            mm.then_inc(s["smp_cache_T"], 1)
            pe.wait_ge(smp_ws_loaded, 16 * SB)
            transpose8(pe, lambda c: ws_nat[:, c, :], lambda b: [("ycT_out", 2 * NP - 1 + b)], "smp_ws_T")
            pe.wait_ge(smp_st_loaded, 16)
            for q in range(SB):
                pe.wait_ge(*((s["smp_ws_out"], q + 1) if q < 2 else (s["smp_st_out"], q - 1)))
                for k in range(4):
                    mm = nc.tensor.transpose(TB[q % 2][:, k, :], st_old[:, q, k, :], ident[:])
                mm.then_inc(s["smp_st_T"], 1)

        def pe_sample_states(pe):
            pe.wait_ge(s["smp_masks"], 3)
            pe.wait_ge(s["smp_st_out"], SB)
            pe.wait_ge(s["seg_done"], NP + 1)
            for g in range(G):
                for q in range(SB):
                    mm = nc.tensor.matmul(SS[:, 0, g * 256:(g + 1) * 256], cmask[:, g, q * P:(q + 1) * P],
                                          st_T[:, q, g * 256:(g + 1) * 256], start=q == 0, stop=q == SB - 1)
            mm.then_inc(s["yoff_done"], 1)
            pe.wait_ge(s["lg_read"], NP)
            for b in range(4):
                mm = nc.tensor.matmul(sd_p[:, b * SB:(b + 1) * SB], adt_e[:, b * P:(b + 1) * P], row_s[:], start=True, stop=True)
            mm.then_inc(s["smp_dec_full"], 1)
            for n in range(8):
                after(pe, s["smp_new"], n)
                nc.tensor.matmul(SS[:, 1, :], xw[:, (n // 2) * P:(n // 2 + 1) * P],
                                 flat(bmask[:, n // 4, half(n % 2), :]), start=True, stop=True).then_inc(s["states_done"], 1)

        def pe_end(pe, tn):
            pe.wait_ge(s["h2_ready"], NT)
            transpose8(pe, block_of(h2), lambda b: [("ycT_out", 2 * NT - 1 + b)], "h2T_full")
            pe_router(pe, NT)
            pe_rank(pe, NT)
            for k in range(4):
                mm = nc.tensor.transpose(YB[:, k * P:(k + 1) * P], state[:, k * P:(k + 1) * P], ident[:])
                if k == 0:
                    mm.then_inc(s["dn_full"], 1)
            mm.then_inc(s["stateT_full"], 1)

        def pe_phase1(pe):
            pe.wait_ge(s["consts"], 1)
            pe.wait_ge(s["x_scaled"], 1)
            transpose8(pe, block_of(x_in[0]), lambda b: [], "xT_full")
            pe.wait_ge(const_loaded, 16 * N_CONST)
            nc.tensor.transpose(MB[:, 0:NROW], rows[0:NROW, :], ident[0:NROW, 0:NROW]).then_inc(s["cols_full"], 1)
            pe.wait_ge(ws_loaded, 16)
            for b in range(2):
                for k in range(4):
                    mm = nc.tensor.transpose(SS[:, b, k * P:(k + 1) * P], xc[:, 4 * b + k, :], ident[:])
            mm.then_inc(s["ws_full"], 1)
            pe.wait_ge(s["x_scaled"], 2)
            transpose8(pe, block_of(x_in[1]), lambda b: [("xT_out", 1 + b)], "xT_full")
            pe.wait_ge(s["w_scaled"], 1)
            project(pe, 0, PB[0][:, :], COL_X, 512, "proj0", [("xT_out", 2)])
            project(pe, 0, PB[1][:, :], COL_X + 512, 512, "proj1", [])
            project(pe, 0, PB[0][:, :], COL_GU, 512, "proj_gu", [("xbc0_out", 1)])
            project(pe, 0, PB[1][:, :], COL_GV, 512, "proj_gv", [("xbc1_out", 1)])
            project(pe, 0, dt_p, COL_DT, H, "dt_done", [("cols_out", 1)])
            project(pe, 0, PB[1][:, :], COL_Z, 512, "proj_z", [("gv_out", 1)])
            pe.wait_ge(s["ws_out"], 2)
            over_tiles(pe, lambda tn: pe_turn(pe, tn))

        def act_turn(act, tn):
            i, j, u = tn.i, tn.j, tn.u
            v = 1 - u
            if tn.end:
                act_end(act)
                return
            if tn.sample:
                act_sample_setup(act)
            for b in range(2):
                act.wait_ge(s["xbcT_full"], 2 * i + 1 + b)
                if tn.sample:
                    for k in range(4):
                        ins = nc.scalar.activation(xT_s[:, 4 * b + k, :, CW - 1:],
                                                   TB[b][:, k, :].rearrange("p (q l) -> p q l", q=SB), ACT.Copy)
                else:
                    act.wait_ge(s["halo_saved"], i + 1)
                    ins = nc.scalar.activation(xT[:, half(b), CW - 1:], TB[b][:, :, :], ACT.Copy)
                ins.then_inc(s["xbcT_out"], 1)
            if tn.prev:
                act_x2sq(act, i - 1, j - 1 + u, v)
            act.wait_ge(s["z_out"], i + 1)
            nc.scalar.activation(zz[u][:, :], zz[u][:, :], ACT.Silu).then_inc(s["zs_ready"], 1)
            if tn.next:
                act.wait_ge(s["proj0"], i + 2)
                if isinstance(i, int) and i == NP - 1:
                    act.wait_ge(convp_stored, 16)
                nc.scalar.activation(xbc[:, 0:512], PB[0][:, :], ACT.Copy).then_inc(s["xbc0_out"], 1)
            act.wait_ge(s["conv_done"], i + 1)
            nc.scalar.activation(xc[:, :, :], xc[:, :, :], ACT.Silu).then_inc(s["xc_ready"], 1)
            act.wait_ge(s["ein_ready"], i + 1)
            act.wait_ge(s["state_ready"], i + 1)
            nc.scalar.activation(e_out[:, :], e_in[:, :], ACT.Exp).then_inc(s["eout_ready"], 1)
            act.wait_ge(s["seg_done"], i + 1)
            nc.scalar.activation(dec[:, :, :], dec[:, :, :], ACT.Exp).then_inc(s["decay_ready"], 1)
            if tn.prev:
                act_h2T(act, i)
            act.wait_ge(s["xb_full"], 2 * i + 1)
            after(act, s["gated_ready"], i)
            nc.scalar.activation(xtok[:, :], flat(TB[0][:, :, :]), ACT.Copy).then_inc(s["xb_out"], 1)
            act.wait_ge(s["xb_full"], 2 * i + 2)
            after(act, s["states_done"], i)
            nc.scalar.activation(btok[:, :], flat(TB[1][:, 0:2, :]), ACT.Copy).then_inc(s["xb_out"], 1)
            if tn.next:
                act.wait_ge(s["proj1"], i + 2)
                nc.scalar.activation(xbc[:, 512:], PB[1][:, :], ACT.Copy).then_inc(s["xbc1_out"], 1)
            if tn.prev:
                act.wait_ge(s["gexin_ready"], i)
                nc.scalar.activation(gexo[:, :], gex[:, :], ACT.Exp).then_inc(s["gexout_ready"], 1)
            if tn.next2:
                act_xsq(act, j + 1, u)
            if tn.sample:
                act.wait_ge(s["smp_dec_full"], 1)
                nc.scalar.activation(st_dec, sd_p, ACT.Exp).then_inc(s["smp_dec_out"], 1)
            act.wait_ge(s["gated_ready"], i + 1)
            for g in range(G):
                c = slice(g * 256, (g + 1) * 256)
                ins = nc.scalar.activation(tmp[:, c], yb[:, c], ACT.Square, accum_out=sq[:, 2 + g:3 + g])
            ins.then_inc(s["ysq_ready"], 1)
            if tn.next:
                act.wait_ge(s["proj_gv"], i + 2)
                act.wait_ge(s["mixed_done"], i + 1)
                nc.scalar.activation(gv[:, :], PB[1][:, :], ACT.Gelu_apprx_tanh).then_inc(s["gv_out"], 1)
                act.wait_ge(s["proj_gu"], i + 2)
                nc.scalar.activation(gu[v][:, :], PB[0][:, :], ACT.Gelu_apprx_tanh).then_inc(s["gu_out"], 1)
            if tn.next2:
                act_xT(act, i + 2, u)
            if tn.next:
                act.wait_ge(s["proj_z"], i + 2)
                nc.scalar.activation(zz[v][:, :], PB[1][:, :], ACT.Copy).then_inc(s["z_out"], 1)
            for b in range(2):
                act.wait_ge(s["ycT_full"], 2 * i + 1 + b)
                after(act, s["logits_done"], i)
                nc.scalar.activation(tT[:, half(b), :], TB[b][:, :, :], ACT.Copy).then_inc(s["ycT_out"], 1)
            if tn.next:
                act.wait_ge(s["dtneg_ready"], i + 2)
                nc.scalar.activation(dtw[:, 2, :], dtw[:, 1, :], ACT.Exp).then_inc(s["dtexp_ready"], 1)
        def act_x2sq(act, i, j, u):
            act.wait_ge(s["x2_half"], 2 * (i + 1))
            after(act, h2_stored, 16 * i)
            after(act, s["h2T_full"], 2 * i)
            nc.scalar.activation(h2[:, :], x_res[u][:, :], ACT.Square, accum_out=sq[:, 1:2]).then_inc(s["x2sq_ready"], 1)

        def act_xsq(act, j, u):
            act.wait_ge(x_loaded[u], 16 * (j + 1))
            nc.scalar.activation(flat(hT[u][:, :, :]), x_in[u][:, :], ACT.Square, accum_out=sq[:, 0:1]).then_inc(s["xsq_ready"], 1)

        def act_xT(act, t, u):
            for b in range(2):
                act.wait_ge(s["xT_full"], 2 * t + 1 + b)
                nc.scalar.activation(hT[u][:, half(b), :], TB[b][:, :, :], ACT.Copy).then_inc(s["xT_out"], 1)

        def act_h2T(act, i):
            for b in range(2):
                act.wait_ge(s["h2T_full"], 2 * i - 1 + b)
                nc.scalar.activation(tT[:, half(b), :], TB[b][:, :, :], ACT.Copy).then_inc(s["h2T_out"], 1)

        def act_sample_setup(act):
            R = SB * (CW - 1)
            act.wait_ge(s["smp_cache_T"], 1)
            for b in range(2):
                for k in range(4):
                    ins = nc.scalar.activation(xT_s[:, 4 * b + k, :, 0:CW - 1],
                                               SS[:, b, k * R:(k + 1) * R].rearrange("p (q l) -> p q l", q=SB), ACT.Copy)
                ins.then_inc(s["smp_cache_out"], 1)
            for q in range(SB):
                act.wait_ge(s["smp_st_T"], q + 1)
                nc.scalar.activation(st_T[:, q, :], flat(TB[q % 2][:, :, :]), ACT.Copy).then_inc(s["smp_st_out"], 1)

        def act_end(act):
            act_x2sq(act, NP, NP // 2, NP % 2)
            act_h2T(act, NT)
            act.wait_ge(s["gexin_ready"], NT)
            nc.scalar.activation(gexo[:, :], gex[:, :], ACT.Exp).then_inc(s["gexout_ready"], 1)
            act.wait_ge(s["stateT_full"], 1)
            nc.scalar.activation(tmp[:, :], YB[:, :], ACT.Copy).then_inc(s["stateT_out"], 1)

        def act_phase1(act):
            act.wait_ge(const_loaded, 16 * N_CONST)
            nc.scalar.activation(aneg_b[:, :], alog_b, ACT.Exp).then_inc(s["eout_a"], 1)
            for u in range(2):
                if u == 1:
                    act.wait_ge(s["xr_ready"], 1)
                act_xsq(act, 0, u)
                act_xT(act, u, u)
            act.wait_ge(s["proj0"], 1)
            nc.scalar.activation(xbc[:, 0:512], PB[0][:, :], ACT.Copy).then_inc(s["xbc0_out"], 1)
            act.wait_ge(s["proj1"], 1)
            nc.scalar.activation(xbc[:, 512:], PB[1][:, :], ACT.Copy).then_inc(s["xbc1_out"], 1)
            act.wait_ge(s["proj_gu"], 1)
            nc.scalar.activation(gu[0][:, :], PB[0][:, :], ACT.Gelu_apprx_tanh).then_inc(s["gu_out"], 1)
            act.wait_ge(s["proj_gv"], 1)
            nc.scalar.activation(gv[:, :], PB[1][:, :], ACT.Gelu_apprx_tanh).then_inc(s["gv_out"], 1)
            act.wait_ge(s["dtneg_ready"], 1)
            nc.scalar.activation(dtw[:, 2, :], dtw[:, 1, :], ACT.Exp).then_inc(s["dtexp_ready"], 1)
            act.wait_ge(s["proj_z"], 1)
            nc.scalar.activation(zz[0][:, :], PB[1][:, :], ACT.Copy).then_inc(s["z_out"], 1)
            over_tiles(act, lambda tn: act_turn(act, tn))

        V = nc.vector

        def per_head(ap):
            return ap.rearrange("p (h a) -> p h a", a=1).broadcast_to([P, H, HD])

        def heads(ap):
            return ap.rearrange("p (h d) -> p h d", h=H)

        def dve_turn(dve, st, tn):
            i, j, u = tn.i, tn.j, tn.u
            v = 1 - u
            if tn.end:
                dve_h2(dve, NP, NP % 2)
                dve_route(dve, st, NT)
                dve_slots(dve, st, NT)
                return
            if tn.sample:
                for b in range(2):
                    dve.wait_ge(s["smp_ws_T"], b + 1)
                    V.tensor_tensor(wsT_s[:, half(b), :], TB[b][:, :, :], over(tri_s, 4), ALU.mult).then_inc(s["smp_ws_out"], 1)
            dve.wait_ge(s["xbcT_out"], 2 * (i + 1))
            tap = cols[:, R_CW:R_CW + CW * CB].rearrange("p (w b) -> p w b", w=CW)
            for w in range(CW - 1, -1, -1):
                for c in range(CB):
                    if tn.sample:
                        src, dst = xT_s[:, c, :, w:w + SL], xc[:, c, :].rearrange("p (q l) -> p q l", q=SB)
                    else:
                        src, dst = xT[:, c, w:w + P], xc[:, c, :]
                    if w == CW - 1:
                        ins = V.tensor_scalar(dst, src, tap[:, w, c:c + 1], cols[:, R_CBIAS + c:R_CBIAS + c + 1], ALU.mult, ALU.add)
                    else:
                        ins = V.scalar_tensor_tensor(out=dst, in0=src, scalar=tap[:, w, c:c + 1], in1=dst, op0=ALU.mult, op1=ALU.add)
                if w > 0:
                    st.link(ins)
                if w == CW - 1 and tn.prev:
                    dve_h2(dve, i - 1, v)
            ins.then_inc(s["conv_done"], 1)
            dve.wait_ge(s["conv_done"], i + 1)
            V.tensor_copy(xT[:, :, 0:CW - 1], xT[:, :, P:]).then_inc(s["halo_saved"], 1)
            dve.wait_ge(s["acs_done"], i + 1)
            st.link(V.tensor_copy(e_in[:, 0:2 * H], MB[:, H:3 * H]))
            V.tensor_tensor(e_in[:, 2 * H:], e_in[:, H:2 * H], e_in[:, 0:H], ALU.subtract).then_inc(s["ein_ready"], 1)
            dve.wait_ge(s["bcast_done"], i + 1)
            for h in range(H):
                a = e_in[:, h:h + 1]
                ins = V.tensor_scalar(dec[:, h, :], SS[:, h // 4, (h % 4) * P:(h % 4 + 1) * P], a, a, ALU.min, ALU.subtract)
            ins.then_inc(s["seg_done"], 1)
            dve.wait_ge(s["cb_done"], i + 1)
            V.tensor_tensor(cbm[:, :, :], cb_p.rearrange("p (g t) -> p g t", g=G),
                            over(tri_s if tn.sample else tri, G), ALU.mult).then_inc(s["cb_read"], 1)
            dve.wait_ge(s["cb_read"], i + 1)
            dve.wait_ge(s["decay_ready"], i + 1)
            for g in range(G):
                ins = V.tensor_tensor(dec[:, half(g), :], dec[:, half(g), :],
                                      cbm[:, g:g + 1, :].broadcast_to([P, 4, P]), ALU.mult)
            ins.then_inc(s["dec_ready"], 1)
            dve.wait_ge(s["xb_out"], 2 * (i + 1))
            dve.wait_ge(s["eout_ready"], i + 1)
            st.link(V.tensor_tensor(heads(xdt[:, :]), heads(xtok[:, :]), per_head(dt_t[:, :]), ALU.mult))
            V.tensor_tensor(heads(xw[:, :]), heads(xdt[:, :]), per_head(e_out[:, 2 * H:]), ALU.mult).then_inc(s["xw_ready"], 1)
            st.inc(V.tensor_tensor(heads(yb[:, :]), heads(xtok[:, :]), per_head(dsk_b), ALU.mult))
            if tn.sample:
                dve_sample_masks(dve, st)
            if tn.prev:
                dve_route(dve, st, i)
            if tn.next2:
                dve_scale_x(dve, i + 2, u)
            dve.wait_ge(s["mixed_done"], i + 1)
            b0 = R_BSS if tn.sample else R_BSP
            st.link(V.tensor_tensor(heads(tmp[:, :]), heads(PB[0][:, :]), per_head(cols[:, b0:b0 + H]), ALU.add))
            V.tensor_tensor(ycat[:, W:], tmp[:, :], gu[u][:, :], ALU.mult).then_inc(s["ycat_hi"], 1)
            dve.wait_ge(s["ydiag_done"], i + 1)
            dve.wait_ge(s["ycat_hi"], i + 1)
            st.inc(V.tensor_tensor(yb[:, :], yb[:, :], YB[:, :], ALU.add))
            dve.wait_ge(s["yoff_done"], i + 1)
            st.link(V.tensor_tensor(heads(tmp[:, :]), heads(SS[:, 0, :]), per_head(e_out[:, 0:H]), ALU.mult))
            st.link(V.tensor_tensor(yb[:, :], yb[:, :], tmp[:, :], ALU.add))
            dve.wait_ge(s["zs_ready"], i + 1)
            V.tensor_tensor(yb[:, :], yb[:, :], zz[u][:, :], ALU.mult).then_inc(s["gated_ready"], 1)
            if tn.sample:
                dve_sample_states(dve, st)
            else:
                dve.wait_ge(s["states_done"], i + 1)
                st.link(V.tensor_tensor(heads(state[:, :]), heads(state[:, :]), per_head(e_out[:, H:2 * H]), ALU.mult))
                V.tensor_tensor(state[:, :], state[:, :], SS[:, 1, :], ALU.add).then_inc(s["state_ready"], 1)
            if tn.prev:
                dve_slots(dve, st, i)
            dve.wait_ge(s["yr_ready"], i + 1)
            for g in range(G):
                c = slice(g * 256, (g + 1) * 256)
                ins = V.tensor_scalar(ycat[:, c], yb[:, c], rs[:, 2 + g:3 + g], None, ALU.mult)
            ins.then_inc(s["ycat_ready"], 1)
            if tn.next:
                dve_v(dve, st, i + 1)
                dve_dt(dve, st, i + 1)
            dve.wait_ge(res_loaded[u], 16 * (j + 1))
            for b in range(2):
                c = slice(b * 512, (b + 1) * 512)
                dve.wait_ge(s[f"out{b}"], i + 1)
                V.tensor_tensor(x_res[u][:, c], x_res[u][:, c], PB[b][:, :], ALU.add).then_inc(s["x2_half"], 1)
        def dve_h2(dve, i, u):
            dve.wait_ge(s["x2_half"], 2 * (i + 1))
            dve.wait_ge(s["x2r_ready"], i + 1)
            V.scalar_tensor_tensor(out=h2[:, :], in0=x_res[u][:, :], scalar=rs[:, 1:2], in1=g2_b[:, :],
                                   op0=ALU.mult, op1=ALU.mult).then_inc(s["h2_ready"], 1)

        def over(mask, n):
            return mask[:, :].rearrange("p (a t) -> p a t", a=1).broadcast_to([P, n, P])

        def dve_scale_x(dve, t, u):
            dve.wait_ge(s["xr_ready"], t + 1)
            V.tensor_scalar(x_in[u][:, :], x_in[u][:, :], rs[:, 0:1], None, ALU.mult).then_inc(s["x_scaled"], 1)

        def dve_v(dve, st, t):
            dve.wait_ge(s["gv_out"], t + 1)
            st.inc(V.bn_stats(bn6[:, :], gv[:, :]))
            st.wait()
            if not isinstance(t, int):
                V.memset(spare[:, 3:4], 0.0)
            V.bn_aggr(mv[:, :], bn6[:, :]).then_inc(s["bn_ready"], 1)
            dve.wait_ge(s["vr_ready"], t + 1)
            st.link(V.tensor_scalar(gv[:, :], gv[:, :], mv[:, 0:1], rs[:, 4:5], ALU.subtract, ALU.mult))
            st.link(V.tensor_tensor(gv[:, :], gv[:, :], lng_b[:, :], ALU.mult))
            V.tensor_tensor(gv[:, :], gv[:, :], lnb_b[:, :], ALU.add).then_inc(s["v_ready"], 1)

        def dve_dt(dve, st, t):
            dve.wait_ge(s["dt_done"], t + 1)
            V.tensor_tensor(dtw[:, 0, :], dt_p, dtb_b, ALU.add).then_inc(s["dt_read"], 1)
            dve.wait_ge(s["dt_read"], t + 1)
            V.scalar_tensor_tensor(out=dtw[:, 1, :], in0=dtw[:, 0, :], scalar=-1.0, in1=dtw[:, 0, :],
                                   op0=ALU.mult, op1=ALU.min).then_inc(s["dtneg_ready"], 1)
            dve.wait_ge(s["dtexp_ready"], t + 1)
            st.link(V.tensor_scalar(dtw[:, 3, :], dtw[:, 2, :], 2.0, None, ALU.add))
            V.reciprocal(dtw[:, 4, :], dtw[:, 3, :]).then_inc(s["dtrec_ready"], 1)

        def first_max(st, src, n, iota, best, key, work, onehot):
            st.link(V.tensor_reduce(best, src, AX.X, ALU.max))
            st.link(V.tensor_scalar(work, src, best, None, ALU.is_equal))
            st.link(V.tensor_tensor(work, work, iota, ALU.mult))
            st.link(V.tensor_reduce(key, work, AX.X, ALU.min))
            st.link(V.tensor_scalar(onehot, iota, key, None, ALU.is_equal))

        def dve_route(dve, st, i):
            dve.wait_ge(s["logits_done"], i)
            V.tensor_tensor(lgs[:, :], lg_p, rb_b[:, :], ALU.add).then_inc(s["lg_read"], 1)
            dve.wait_ge(s["lg_read"], i)
            gbest, gkey, b1, k1, b2, k2 = (rt[:, c:c + 1] for c in range(6))
            gone = rt[:, 12:16]
            first_max(st, lgs[:, 0:NG], NG, iota_g[:, :], gbest, gkey, eqt[:, 0:NG], gone)
            st.inc(V.tensor_scalar(gex[:, 0:NG], lgs[:, 0:NG], gbest, None, ALU.subtract))
            st.link(V.tensor_scalar(gone, gone, -1.0, BIG, ALU.add, ALU.mult))
            st.link(V.tensor_tensor(em[:, :].rearrange("p (g e) -> p g e", g=NG), lgs[:, NG:].rearrange("p (g e) -> p g e", g=NG),
                                    gone.rearrange("p (g a) -> p g a", a=1).broadcast_to([P, NG, EG]), ALU.add))
            first_max(st, em[:, :], NE, iota_e[:, :], b1, k1, eqt[:, :], oh[:, 0, :])
            st.link(V.scalar_tensor_tensor(out=em[:, :], in0=oh[:, 0, :], scalar=-4.0 * BIG, in1=em[:, :], op0=ALU.mult, op1=ALU.add))
            first_max(st, em[:, :], NE, iota_e[:, :], b2, k2, eqt[:, :], oh[:, 1, :])
            V.tensor_tensor(gex[:, NG:], b2, b1, ALU.subtract).then_inc(s["gexin_ready"], 1)
            V.tensor_tensor(oh[:, 2, :], oh[:, 0, :], oh[:, 1, :], ALU.add).then_inc(s["pick_ready"], 1)

        def dve_slots(dve, st, i):
            k1, k2 = rt[:, 3:4], rt[:, 5:6]
            ssum, den, w1, w2, p1, p2 = (rt[:, c:c + 1] for c in range(6, 12))
            dve.wait_ge(s["gexout_ready"], i)
            st.link(V.tensor_reduce(ssum, gexo[:, 0:NG], AX.X, ALU.add))
            st.link(V.tensor_scalar(den, gexo[:, NG:], 1.0, ssum, ALU.add, ALU.mult))
            st.link(V.reciprocal(w1, den))
            st.inc(V.tensor_tensor(w2, w1, gexo[:, NG:], ALU.mult))
            dve.wait_ge(s["rank_done"], i)
            st.link(V.tensor_tensor(rk[:, :], rk_p, carry[:, :], ALU.add))
            V.tensor_tensor(carry[:, :], carry[:, :], cnt_p, ALU.add).then_inc(s["rank_read"], 1)
            for k, p in ((0, p1), (1, p2)):
                st.link(V.tensor_tensor(eqt[:, :], oh[:, k, :], rk[:, :], ALU.mult))
                st.link(V.tensor_reduce(p, eqt[:, :], AX.X, ALU.add))
            sl = rt[:, 0:3]
            st.inc(V.scalar_tensor_tensor(out=rt[:, 0:1], in0=k1, scalar=float(T), in1=p1, op0=ALU.mult, op1=ALU.add))
            st.link(V.scalar_tensor_tensor(out=rt[:, 1:2], in0=k2, scalar=float(T), in1=p2, op0=ALU.mult, op1=ALU.add))
            after(dve, scattered, 32 * (i - 1))
            st.inc(V.tensor_scalar(slots[:, 0:2], rt[:, 0:2], float(NE * T), None, ALU.add))
            st.inc(V.tensor_copy(slots[:, 2:3], tok_id[:, :]))
            pk = picks[:, bass.ds(i - 1, 1), :].rearrange("p a c -> p (a c)") if not isinstance(i, int) else picks[:, i - 1, :]
            st.inc(V.tensor_copy(pk[:, 0:1], k1))
            st.inc(V.tensor_copy(pk[:, 1:2], k2))
            st.inc(V.tensor_copy(pk[:, 2:4], rt[:, 10:12]))
            st.inc(V.tensor_copy(pk[:, 4:6], rt[:, 8:10]))
            st.wait()
            V.tensor_scalar(tok_id[:, :], tok_id[:, :], float(P), None, ALU.add).then_inc(s["slots_ready"], 1)
            dve.wait_ge(s["slots_ready"], i)

        def dve_sample_masks(dve, st):
            dve.wait_ge(s["smp_zero"], 2)
            dve.wait_ge(s["xc_ready"], NT)
            for g in range(G):
                ins = V.tensor_copy(cmask[:, g, :].rearrange("p (q w) -> p q w", q=SB)[:, :, 0:SL],
                                    xc[:, 6 + g, :].rearrange("p (q l) -> p q l", q=SB))
            ins.then_inc(s["smp_masks"], 1)
            for g in range(G):
                ins = V.tensor_tensor(bmask[:, g, :, :],
                                      btok[:, g * N:(g + 1) * N].rearrange("p (a n) -> p a n", a=1).broadcast_to([P, SB, N]),
                                      row_s[:, :].rearrange("p (q a) -> p q a", a=1).broadcast_to([P, SB, N]), ALU.mult)
            ins.then_inc(s["smp_masks"], 1)
            V.tensor_copy(heads(adt_e), per_head(adt[:, :])).then_inc(s["smp_masks"], 1)

        def dve_sample_states(dve, st):
            dve.wait_ge(s["smp_dec_out"], 1)
            for n in range(8):
                b, w = n // 2, n % 2
                o = st_old[:, half(w), b, :]
                d = st_dec[:, b * SB + 4 * w:b * SB + 4 * w + 4].rearrange("p (q a) -> p q a", a=1).broadcast_to([P, 4, N])
                dve.wait_ge(s["states_done"], NP + 1 + n)
                st.link(V.tensor_tensor(o, o, d, ALU.mult))
                V.tensor_tensor(o, o, SS[:, 1, :].rearrange("p (q n) -> p q n", q=4), ALU.add).then_inc(s["smp_new"], 1)

        def dve_phase1(dve):
            st = Steps(dve, dve_step)
            V.memset(xT[:, :, 0:CW - 1], 0.0).then_inc(s["halo_saved"], 1)
            st.inc(V.memset(carry[:, :], 0.0))
            V.memset(state[:, :], 0.0).then_inc(s["state_ready"], 1)
            dve_scale_x(dve, 0, 0)
            dve_scale_x(dve, 1, 1)
            dve.wait_ge(s["eout_a"], 1)
            st.link(V.tensor_scalar(aneg_b[:, :], aneg_b[:, :], -1.0, None, ALU.mult))
            dve.wait_ge(s["cols_full"], 1)
            V.tensor_copy(cols[:, :], MB[:, 0:NROW]).then_inc(s["cols_out"], 1)
            dve.wait_ge(s["ws_full"], 1)
            for b in range(2):
                V.tensor_tensor(wsT[:, half(b), :], SS[:, b, :].rearrange("p (h t) -> p h t", h=4), over(tri, 4),
                                ALU.mult).then_inc(s["ws_out"], 1)
            dve.wait_ge(s["cols_out"], 1)
            for k in range(KD):
                if k % 4 == 0:
                    dve.wait_ge(win_loaded[k // 4], 16)
                ins = V.tensor_scalar(w_in_sb[:, k, :], w_in_sb[:, k, :], cols[:, R_G1 + k:R_G1 + k + 1], None, ALU.mult)
            ins.then_inc(s["w_scaled"], 1)
            dve.wait_ge(wout_loaded, 16)
            for k in range(W // P):
                ins = V.tensor_scalar(w_out_sb[:, k, :], w_out_sb[:, k, :], cols[:, R_SG + k:R_SG + k + 1], None, ALU.mult)
            ins.then_inc(s["w_scaled"], 1)
            dve_dt(dve, st, 0)
            dve_v(dve, st, 0)
            over_tiles(dve, lambda tn: dve_turn(dve, st, tn), st, DVE_TURN)
            return st

        def fence(n, k):
            if not isinstance(n, int):
                nc.gpsimd.tensor_tensor(spare[:, k:k + 1], neg_half[:, 0:1], neg_half[:, 0:1], ALU.mult)

        def root(pool, st, out, in_, scale, n):
            st.link(nc.gpsimd.tensor_scalar(out, in_, scale, EPS, ALU.mult, ALU.add))
            return nc.gpsimd.tensor_tensor(out, out, neg_half[:, 0:n], ALU.pow)

        def pool_turn(pool, st, tn):
            i, j, u = tn.i, tn.j, tn.u
            if tn.end:
                pool_scatter(pool, NT)
                return
            if tn.sample:
                pool.wait_ge(s["dt_done"], NT)
                nc.gpsimd.memset(cmask[:, :, :], 0.0).then_inc(s["smp_zero"], 1)
            if tn.next2:
                pool.wait_ge(s["xsq_ready"], i + 3)
                fence(i, 1)
                root(pool, st, rs[:, 0:1], sq[:, 0:1], 1.0 / D, 1).then_inc(s["xr_ready"], 1)
            pool.wait_ge(s["ysq_ready"], i + 1)
            fence(i, 1)
            root(pool, st, rs[:, 2:4], sq[:, 2:4], 1.0 / 256, 2).then_inc(s["yr_ready"], 1)
            if tn.prev:
                pool_scatter(pool, i)
            if tn.next:
                pool_v(pool, st, i + 1)
                pool_dt(pool, st, i + 1)
            if isinstance(i, int) and i == NP - 1:
                pool.wait_ge(s["dt_done"], NT)
                nc.gpsimd.memset(ws_nat[:, :, :], 0.0).then_inc(s["smp_zero"], 1)
            pool.wait_ge(s["x2sq_ready"], i + 1)
            fence(i, 1)
            root(pool, st, rs[:, 1:2], sq[:, 1:2], 1.0 / D, 1).then_inc(s["x2r_ready"], 1)

        def pool_v(pool, st, t):
            pool.wait_ge(s["bn_ready"], t + 1)
            fence(t, 1)
            root(pool, st, rs[:, 4:5], mv[:, 1:2], 1.0, 1).then_inc(s["vr_ready"], 1)

        def pool_dt(pool, st, t):
            g = nc.gpsimd
            pool.wait_ge(s["dtrec_ready"], t + 1)
            after(pool, s["xw_ready"], t)
            r, r2, a = dtw[:, 5, :], dtw[:, 6, :], dtw[:, 7, :]
            st.link(g.tensor_tensor(r, dtw[:, 2, :], dtw[:, 4, :], ALU.mult))
            st.link(g.tensor_tensor(r2, r, r, ALU.mult))
            st.link(g.tensor_scalar(a, r2, ARTANH[4], ARTANH[3], ALU.mult, ALU.add))
            for k in (2, 1, 0):
                st.link(g.tensor_tensor(a, a, r2, ALU.mult))
                st.link(g.tensor_scalar(a, a, ARTANH[k], None, ALU.add))
            st.inc(g.tensor_scalar(dtw[:, 3, :], dtw[:, 0, :], 0.0, None, ALU.max))
            st.link(g.tensor_tensor(a, a, r, ALU.mult))
            st.link(g.tensor_tensor(dt_t[:, :], a, dtw[:, 3, :], ALU.add))
            g.tensor_tensor(adt[:, :], dt_t[:, :], aneg_b[:, :], ALU.mult).then_inc(s["dt_ready"], 1)
            pool.wait_ge(s["dt_ready"], t + 1)
            after(pool, s["ydiag_done"], t)
            mask = tri_s if isinstance(t, int) and t == NP else tri
            g.tensor_tensor(dec[:, :, :], over(mask, H), adt[:, :].rearrange("p (h a) -> p h a", a=1).broadcast_to([P, H, P]),
                            ALU.mult).then_inc(s["trid_ready"], 1)

        def pool_scatter(pool, i):
            pool.wait_ge(s["slots_ready"], i)
            fence(i, 2)
            if isinstance(i, int) and i == 1:
                pool.wait_ge(slots_zeroed, 16 * 8)
            for k in range(2):
                nc.gpsimd.indirect_dma_start(out=slot_d[:, :], out_offset=bass.IndirectOffsetOnAxis(ap=slots[:, k:k + 1], axis=0),
                                             in_=slots[:, 2:3], in_offset=None).then_inc(scattered, 16)

        def pool_phase1(pool):
            g = nc.gpsimd
            st = Steps(pool, pool_step, fence)

            def select(out, in_, op, fill, base, pattern, mult):
                st.link(g.affine_select(out=out, in_=in_, compare_op=op, fill=fill, base=base, pattern=pattern,
                                        channel_multiplier=mult))
            st.inc(g.memset(neg_half[:], -0.5))
            st.inc(g.memset(ident[:], 0.0))
            st.inc(g.memset(ones[:], 1.0))
            st.inc(g.memset(row_s[:], 1.0))
            st.link(g.memset(slot_zero[:], 0))
            select(ident[:], ident[:], ALU.not_equal, 1.0, 0, [[-1, P]], 1)
            select(tri[:], ones[:], ALU.is_ge, 0.0, 0, [[1, P]], -1)
            select(stri[:], ones[:], ALU.is_gt, 0.0, 0, [[1, P]], -1)
            q_of = blk_s[:].rearrange("p (q l) -> p q l", q=SB)
            select(row_s[:], row_s[:], ALU.is_ge, 0.0, 0, [[-SL, SB]], 1)
            select(row_s[:], row_s[:], ALU.is_ge, 0.0, SL - 1, [[SL, SB]], -1)
            select(q_of, ones[:].rearrange("p (q l) -> p q l", q=SB), ALU.is_ge, 0.0, 0, [[-SL, SB], [0, SL]], 1)
            select(q_of, q_of, ALU.is_ge, 0.0, SL - 1, [[SL, SB], [0, SL]], -1)
            st.link(g.tensor_tensor(tri_s[:], tri[:], blk_s[:], ALU.mult))
            st.inc(g.iota(iota_i[:, 0:NG], pattern=[[1, NG]], base=-NG, channel_multiplier=0))
            st.inc(g.iota(iota_i[:, NG:NR], pattern=[[1, NE]], base=-NE, channel_multiplier=0))
            st.link(g.iota(iota_i[:, NR:NR + 1], pattern=[[1, 1]], base=0, channel_multiplier=1))
            st.inc(g.tensor_copy(iota_g[:], iota_i[:, 0:NG]))
            st.inc(g.tensor_copy(iota_e[:], iota_i[:, NG:NR]))
            st.inc(g.tensor_copy(tok0[:], iota_i[:, NR:NR + 1]))
            g.tensor_copy(tok_id[:], iota_i[:, NR:NR + 1]).then_inc(s["consts"], 1)
            for t in range(2):
                pool.wait_ge(s["xsq_ready"], t + 1)
                if t == 1:
                    pool.wait_ge(s["x_scaled"], 1)
                root(pool, st, rs[:, 0:1], sq[:, 0:1], 1.0 / D, 1).then_inc(s["xr_ready"], 1)
            pool_dt(pool, st, 0)
            pool_v(pool, st, 0)
            over_tiles(pool, lambda tn: pool_turn(pool, st, tn), st, POOL_TURN)
            return st

        def sp_turn(sp, tn):
            i, j, u = tn.i, tn.j, tn.u
            v = 1 - u
            if tn.next3:
                sp.wait_ge(s["xT_full"], 2 * (i + 2))
                sp.dma_start(x_in[v][:, :], input_tile(i + 3)).then_inc(x_loaded[v], 16)
            if tn.prev:
                sp.wait_ge(s["h2_ready"], i)
                sp.dma_start(at_tile(x2_tiles, i - 1), x_res[v][:, :]).then_inc(x2_stored, 16)
                sp.dma_start(at_tile(h2_tiles, i - 1), h2[:, :]).then_inc(h2_stored, 16)
            if tn.next:
                after(sp, x2_stored, 16 * i)
                sp.dma_start(x_res[v][:, :], input_tile(i + 1)).then_inc(res_loaded[v], 16)
            if tn.next:
                sp.dma_start(at_tile(ys_tiles, 2 * T // P + i), at_tile(x_tiles, i)).then_inc(ys_filled, 16)
            if isinstance(i, int) and i == NP - 1:
                sp.wait_ge(s["xbc1_out"], NP)
                sp.dma_start(conv_prompt[0, 0, :, :], xbc[P - CW + 1:, :]).then_inc(convp_stored, 16)
                sp.wait_ge(s["dt_done"], NT)
                sp.dma_start(cache_sb[0:SB * (CW - 1), :], cache_conv.rearrange("a q l c -> (a q l) c")).then_inc(smp_cache_loaded, 16)
                sp.dma_start(st_old, state_ssm.rearrange("a q (b h) d n -> (h d) (a q) b n", b=4)).then_inc(smp_st_loaded, 16)
                sp.wait_ge(s["smp_zero"], 1)
                for q in range(SB):
                    c = slice(q * SL, (q + 1) * SL)
                    sp.dma_start(ws_nat[c, :, c], w_spatial[0, :, 0:SL, 0:SL].rearrange("h t s -> t h s")).then_inc(smp_ws_loaded, 16)
            if tn.sample:
                sp.wait_ge(s["xbc1_out"], NT)
                for k in range(CW - 1):
                    sp.dma_start(conv_sample[0, :, k, :], xbc[SL - CW + 1 + k::SL, :]).then_inc(convs_stored, 16)
                sp.wait_ge(s["v_ready"], NT)
                sp.dma_start(gmlp_v_sample.rearrange("a q l c -> (a q l) c"), gv[:, :]).then_inc(vs_stored, 16)
            if tn.end:
                sp.wait_ge(s["smp_new"], 8)
                sp.dma_start(ssm_sample.rearrange("a q (b h) d n -> (h d) (a q) b n", b=4), st_old).then_inc(ssm_stored, 16)
                sp.wait_ge(s["stateT_out"], 1)
                sp.dma_start(ssm_prompt.rearrange("a q (b h) d n -> (h d) (a q b) n", b=4),
                             tmp[:, :].rearrange("p (b n) -> p b n", b=4)).then_inc(ssm_stored, 16)

        def sp_phase1(sp):
            for u in range(2):
                sp.dma_start(x_in[u][:, :], input_tile(u)).then_inc(x_loaded[u], 16)

            def row(dst, src):
                sp.dma_start(dst, src).then_inc(const_loaded, 16)
                count[0] += 1
            count = [0]
            row(rows[R_G1:R_G1 + KD, :], norm1_g.rearrange("a (k p) -> (a k) p", p=P))
            row(rows[R_CBIAS:R_CBIAS + CB, :], conv_b.rearrange("a (k p) -> (a k) p", p=P))
            row(rows[R_CW:R_BSP, :], conv_w.rearrange("a w (k p) -> (a w k) p", p=P))
            row(rows[R_BSP:R_SG, :], b_spatial[0, :, :])
            row(rows[R_SG:R_BSS, :], ssm_norm_g.rearrange("a (k p) -> (a k) p", p=P))
            for q in range(SB):
                row(rows[R_BSS:NROW, q * SL:(q + 1) * SL], b_spatial[0, :, 0:SL])
            for k, w in enumerate((dt_bias, a_log, d_skip)):
                row(small_b[:, k * H:(k + 1) * H], w.broadcast_to([P, H]))
            row(rb_b[:, 0:NG], b_rg.broadcast_to([P, NG]))
            row(rb_b[:, NG:], b_re.broadcast_to([P, NE]))
            row(g2_b[:, :], norm2_g.broadcast_to([P, D]))
            row(lng_b[:, :], ln_v_g.broadcast_to([P, W]))
            row(lnb_b[:, :], ln_v_b.broadcast_to([P, W]))
            row(wr_sb[:, :, 0:NG], w_rg[0, :, :].rearrange("(k p) n -> p k n", p=P))
            row(wr_sb[:, :, NG:], w_re[0, :, :].rearrange("(k p) n -> p k n", p=P))
            assert count[0] == N_CONST, count
            sp.dma_start(xc[:, :, :], w_spatial[0, :, :, :].rearrange("h t s -> t h s")).then_inc(ws_loaded, 16)
            w_rows = w_in[0, :, :].rearrange("(k p) n -> p k n", p=P)
            for k in range(2):
                sp.dma_start(w_in_sb[:, half(k), :], w_rows[:, half(k), :]).then_inc(win_loaded[k], 16)
            sp.dma_start(x_res[0][:, :], input_tile(0)).then_inc(res_loaded[0], 16)
            sp.dma_start(w_out_sb[:, :, :], w_out[0, :, :].rearrange("(k p) n -> p k n", p=P)).then_inc(wout_loaded, 16)
            sp.wait_ge(s["xT_full"], 2)
            sp.dma_start(x_in[0][:, :], input_tile(2)).then_inc(x_loaded[0], 16)
            sp.wait_ge(s["consts"], 1)
            for k in range(8):
                sp.dma_start(slot_d.rearrange("(c p n) a -> c p (n a)", c=8, p=P)[k, :, :], slot_zero[:, :]).then_inc(slots_zeroed, 16)
            over_tiles(sp, lambda tn: sp_turn(sp, tn))

        TAB_OFF, TAB_SLOT, TAB_WAIT = 0, 1, 2
        hTb = xdt[:, 0:2 * P].rearrange("p (k t) -> p k t", k=2)
        silu_g = [ycat[:, 0:DE], ycat[:, DE:2 * DE]]
        YBv = YB[:, 0:2 * P].rearrange("p (k t) -> p k t", k=2)
        SURE = 2 * T // P // 2

        def entry(eng, row, at, low, high):
            return eng.value_load(tab[0:1, row, bass.ds(at, 1)], min_val=low, max_val=high)

        def pairs_used(eng):
            return eng.value_load(misc[0:1, 0:1], min_val=SURE, max_val=NBLK // 2)

        def over_pairs(eng, pair):
            used = pairs_used(eng)
            pair(0)
            with eng.Fori(1, SURE) as j:
                pair(j)
            with eng.Fori(SURE, NBLK // 2) as j:
                with eng.If(j < used):
                    pair(j)
            return used

        def dve_tables(dve, st):
            nb, some, pend, pstart, nth = (eqt[:, :], em[:, :], oh[:, 0, :], oh[:, 1, :], oh[:, 2, :])
            ni = slots32[:, 0:NE]
            col = [rt[:, c:c + 1] for c in range(12)]
            block, ebase, kth, start, place, last = col[0:6]
            st.link(V.tensor_scalar(ni, carry[:, :], float(P - 1), None, ALU.add))
            st.link(V.tensor_scalar(ni, ni, 7, None, ALU.logical_shift_right))
            st.link(V.tensor_copy(nb, ni))
            st.inc(V.tensor_scalar(some, nb, 1.0, None, ALU.min))
            st.link(V.tensor_tensor_scan(out=pend, data0=ones[:, 0:NE], data1=nb, initial=0.0, op0=ALU.mult, op1=ALU.add))
            st.link(V.memset(some[:, 0:1], 1.0))
            st.inc(V.tensor_tensor(pstart, pend, nb, ALU.subtract))
            st.link(V.tensor_tensor_scan(out=nth, data0=ones[:, 0:NE], data1=some, initial=0.0, op0=ALU.mult, op1=ALU.add))
            cmp = rk[:, :]
            st.link(V.tensor_scalar(cmp, pend, tok0[:, :], None, ALU.is_le))
            st.inc(V.tensor_reduce(ebase, cmp, AX.X, ALU.add))
            st.link(V.tensor_tensor(cmp, cmp, some, ALU.mult))
            st.inc(V.tensor_reduce(kth, cmp, AX.X, ALU.add))
            st.link(V.tensor_scalar(last, nth[:, NE - 1:NE], -1.0, None, ALU.add))
            st.inc(V.tensor_tensor(kth, kth, last, ALU.min))
            st.link(V.tensor_scalar(ebase, ebase, float(NE - 1), float(-NE), ALU.min, ALU.add))
            st.link(V.tensor_scalar(cmp, iota_e[:, :], ebase, None, ALU.is_equal))
            st.link(V.tensor_tensor(cmp, cmp, pstart, ALU.mult))
            st.link(V.tensor_reduce(start, cmp, AX.X, ALU.add))
            st.link(V.tensor_tensor(place, tok0[:, :], start, ALU.subtract))
            st.link(V.tensor_scalar(place, place, float(T // P - 1), float(P), ALU.min, ALU.mult))
            st.inc(V.scalar_tensor_tensor(out=place, in0=ebase, scalar=float(T), in1=place, op0=ALU.mult, op1=ALU.add))
            st.link(V.tensor_copy(ni[:, 0:1], kth))
            st.link(V.tensor_scalar(ni[:, 0:1], ni[:, 0:1], 1, None, ALU.bitwise_and))
            st.inc(V.tensor_scalar(tcol[:, 0:1], place, float(NE * T), None, ALU.add))
            st.inc(V.tensor_scalar(tcol[:, 1:2], ni[:, 0:1], float(WSLOT), None, ALU.mult))
            st.inc(V.tensor_scalar(tcol[:, 2:3], kth, 1.0, 48.0, ALU.add, ALU.mult))
            st.link(V.tensor_scalar(cmp, nth, tok0[:, :], None, ALU.is_le))
            st.link(V.tensor_reduce(start, cmp, AX.X, ALU.add))
            st.link(V.tensor_scalar(tcol[:, 3:4], start, float(NE - 1), None, ALU.min))
            st.inc(V.tensor_scalar(last, tok0[:, :], 1.0, None, ALU.add))
            st.wait()
            st.link(V.tensor_scalar(cmp, nth, last, None, ALU.is_le))
            st.link(V.tensor_tensor(cmp, cmp, pend, ALU.mult))
            st.link(V.tensor_reduce(start, cmp, AX.X, ALU.max))
            V.tensor_scalar(tcol[:, 4:5], start, 1.0, None, ALU.add).then_inc(s["tab_cols"], 1)
            st.inc(V.tensor_copy(misc[:, 1:2], nth[:, NE - 1:NE]))
            st.link(V.tensor_scalar(misc[:, 0:1], pend[:, NE - 1:NE], 1.0, None, ALU.add))
            st.link(V.tensor_scalar(misc[:, 0:1], misc[:, 0:1], 1, None, ALU.logical_shift_right))
            dve.wait_ge(s["tab_rows"], 1)
            V.tensor_copy(tab[0:1, :, :], MB[0:1, :].rearrange("p (a b) -> p a b", a=4)).then_inc(s["tab_half"], 1)
            dve.wait_ge(s["tab_rows"], 2)
            V.tensor_copy(pend_i[0:1, :], MB[0:1, 0:P]).then_inc(s["tables"], 1)

        def dve_rows_of_picks(dve, st):
            pstart = oh[:, 1, :]
            shape2 = [P, 2 * NT, NE]

            def over_t(x):
                return x.rearrange("p (a e) -> p a e", a=1).broadcast_to(shape2)
            pk = flat(pickk[:, :, :])
            st.link(V.tensor_copy(pickk[:, :, :], picks[:, :, 0:2]))
            st.link(V.tensor_tensor(pos_t, over_t(iota_e[:, :]), pk.rearrange("p (t a) -> p t a", a=1).broadcast_to(shape2), ALU.is_equal))
            st.link(V.tensor_tensor(pos_t, pos_t, over_t(pstart), ALU.mult))
            st.link(V.tensor_reduce(pk, pos_t, AX.X, ALU.add))
            st.link(V.scalar_tensor_tensor(out=rowpos[:, :, :], in0=pickk[:, :, :], scalar=float(P), in1=picks[:, :, 2:4],
                                           op0=ALU.mult, op1=ALU.add))

        def sp_phase2(sp):
            def load(e, slot):
                w = SLOT[slot]
                gup = w[:, 0:KD * 2 * DE].rearrange("p (k n) -> p k n", k=KD)
                dn = w[:, KD * 2 * DE:].rearrange("p (k n) -> p k n", k=2)

                def of(x):
                    return x[0, e, :, :] if isinstance(e, int) else x[0, bass.ds(e, 1), :, :].rearrange("a k n -> (a k) n")
                sp.dma_start(gup[:, :, 0:DE], of(w_gate).rearrange("(k p) n -> p k n", p=P)).then_inc(w_loaded, 16)
                sp.dma_start(gup[:, :, DE:], of(w_up).rearrange("(k p) n -> p k n", p=P)).then_inc(w_loaded, 16)
                sp.dma_start(dn, of(w_down).rearrange("(k p) n -> p k n", p=P)).then_inc(w_loaded, 16)

            sp.wait_ge(ssm_stored, 32)
            sp.wait_ge(s["smp_new"], 8)
            load(0, 0)
            sp.wait_ge(s["tables"], 1)
            sp.wait_ge(w_loaded, 48)
            experts = sp.value_load(misc[0:1, 1:2], min_val=1, max_val=NE)
            with sp.If(1 < experts):
                load(entry(sp, 3, 1, 0, NE - 1), 1)
            with sp.Fori(1, NE // 2) as m:
                for c in range(2):
                    k = 2 * m + c
                    with sp.If(k < experts):
                        expert = entry(sp, 3, k, 0, NE - 1)
                        before = sp.value_load(pend_i[0:1, bass.ds(k - 2, 1)], min_val=1, max_val=NBLK + 1)
                        sp.wait_ge(w_loaded, 48 * k)
                        sp.wait_ge(s["dn_full"], before)
                        load(expert, c)

        def pool_phase2(pool):
            pool.wait_ge(s["tables"], 1)
            pool.wait_ge(scattered, 32 * NT)
            pool.wait_ge(h2_stored, 16 * NT)

            def gather(p):
                offs = [entry(pool, TAB_OFF, 2 * p + u, 0, NE * T - P) for u in range(2)]
                for u in range(2):
                    after(pool, gathered[u], 16 * p)
                    pool.dma_start(idx[u][:, :], slot_d[bass.ds(offs[u], P), :]).then_inc(idx_loaded[u], 16)
                for u in range(2):
                    b = 2 * p + u
                    pool.wait_ge(idx_loaded[u], 16 * (p + 1))
                    after(pool, s["gx_T"], 2 * (b - 1))
                    after(pool, s["fenced"], b)
                    nc.gpsimd.tensor_tensor(spare[:, 1:2], neg_half[:, 0:1], neg_half[:, 0:1], ALU.mult).then_inc(s["fenced"], 1)
                    nc.gpsimd.indirect_dma_start(out=x_in[u][:, :], out_offset=None, in_=h2_d[:, :],
                                                 in_offset=bass.IndirectOffsetOnAxis(ap=idx[u][:, 0:1], axis=0)).then_inc(gathered[u], 16)
            gather(0)
            return over_pairs(pool, lambda j: gather(j + 1))

        def pe_rows(pe, b, u, j):
            pe.wait_ge(gathered[u], 16 * (j + 1))
            for k in range(2):
                after(pe, s[f"gx_out{k}"], b)
                for c in range(4):
                    mm = nc.tensor.transpose(TB[k][:, c, :], x_in[u][:, (4 * k + c) * P:(4 * k + c + 1) * P], ident[:])
                mm.then_inc(s["gx_T"], 1)

        def pe_gate_up(pe, b, u):
            slot = entry(pe, TAB_SLOT, b, 0, WSLOT)
            ready = entry(pe, TAB_WAIT, b, 48, 48 * NE)
            pe.wait_ge(w_loaded, ready)
            for k in range(2):
                pe.wait_ge(s[f"gx_out{k}"], b + 1)
            after(pe, s["hb_ready"], b - 1)
            for k in range(KD):
                mm = nc.tensor.matmul(PB[u][:, :], hT[u][:, k, :], arena[:, bass.ds(slot + k * 2 * DE, 2 * DE)],
                                      start=k == 0, stop=k == KD - 1)
            mm.then_inc(s["gu_full"], 1)

        def pe_table_rows(pe):
            pe.wait_ge(s["tab_cols"], 1)
            pe.wait_ge(s["rank_read"], NT)
            for c in range(4):
                mm = nc.tensor.transpose(MB[0:1, c * P:(c + 1) * P], tcol[:, c:c + 1], ident[:])
            mm.then_inc(s["tab_rows"], 1)
            pe.wait_ge(s["tab_half"], 1)
            nc.tensor.transpose(MB[0:1, 0:P], tcol[:, 4:5], ident[:]).then_inc(s["tab_rows"], 1)

        def pe_phase2(pe):
            pe_table_rows(pe)
            pe.wait_ge(s["stateT_out"], 1)
            pe.wait_ge(s["tables"], 1)
            pe.wait_ge(s["h2T_out"], 2 * NT)
            pe.wait_ge(s["h2_ready"], NT)

            def pair(j):
                for u in range(2):
                    b = 2 * j + u
                    nj, nu = (j, 1) if u == 0 else (j + 1, 0)
                    pe_gate_up(pe, 2 * nj + nu, nu)
                    pe.wait_ge(s["hb_ready"], b + 1)
                    after(pe, s["hbT_out"], b)
                    for k in range(2):
                        mm = nc.tensor.transpose(YBv[:, k, :], hb2[u][:, k * P:(k + 1) * P], ident[:])
                    mm.then_inc(s["hbT_full"], 1)
                    pe_rows(pe, b + 2, u, j + 1)
                    slot = entry(pe, TAB_SLOT, b, 0, WSLOT)
                    pe.wait_ge(s["hbT_out"], b + 1)
                    for n in range(2):
                        after(pe, s[f"dn_out{n}"], b)
                        for k in range(2):
                            mm = nc.tensor.matmul(SS[:, n, :], hTb[:, k, :],
                                                  arena[:, bass.ds(slot + KD * 2 * DE + k * D + n * 512, 512)],
                                                  start=k == 0, stop=k == 1)
                    mm.then_inc(s["dn_full"], 1)
            pe_rows(pe, 0, 0, 0)
            pe_rows(pe, 1, 1, 0)
            pe_gate_up(pe, 0, 0)
            over_pairs(pe, pair)

        def act_phase2(act):
            act.wait_ge(x2_stored, 16 * NT)
            act.wait_ge(ys_filled, 16 * NP)
            act.wait_ge(s["tables"], 1)

            def rows0(b, u):
                act.wait_ge(s["gx_T"], 2 * b + 1)
                after(act, s["gu_full"], b - 1)
                nc.scalar.activation(hT[u][:, half(0), :], TB[0][:, :, :], ACT.Copy).then_inc(s["gx_out0"], 1)

            def silu(b, u):
                act.wait_ge(s["gu_full"], b + 1)
                after(act, s["hb_ready"], b - 1)
                nc.scalar.activation(silu_g[u], PB[u][:, 0:DE], ACT.Silu).then_inc(s["silu_out"], 1)

            def pair(j):
                for u in range(2):
                    b = 2 * j + u
                    act.wait_ge(s["hbT_full"], b + 1)
                    after(act, s["dn_full"], b + 1)
                    nc.scalar.activation(hTb, YBv, ACT.Copy).then_inc(s["hbT_out"], 1)
                    silu(b + 1, 1 - u)
                    rows0(b + 2, u)
                    act.wait_ge(s["dn_full"], b + 2)
                    after(act, ys_stored[u], 16 * j)
                    nc.scalar.activation(x_res[u][:, 0:512], SS[:, 0, :], ACT.Copy).then_inc(s["dn_out0"], 1)
                    act.wait_ge(s["dn_out1"], b + 1)
                    act.wait_ge(s["dn_out0"], b + 1)
                    act.dma_start(at_tile(ys_tiles, b), x_res[u][:, :]).then_inc(ys_stored[u], 16)
            rows0(0, 0)
            rows0(1, 1)
            silu(0, 0)
            return over_pairs(act, pair)

        def dve_phase2(dve):
            def rows1(b, u):
                dve.wait_ge(s["gx_T"], 2 * b + 2)
                after(dve, s["gu_full"], b - 1)
                V.tensor_copy(hT[u][:, half(1), :], TB[1][:, :, :]).then_inc(s["gx_out1"], 1)

            def gate(b, u):
                dve.wait_ge(s["silu_out"], b + 1)
                after(dve, s["hbT_full"], b - 1)
                V.tensor_tensor(hb2[u], silu_g[u], PB[u][:, DE:], ALU.mult).then_inc(s["hb_ready"], 1)

            def pair(j):
                for u in range(2):
                    b = 2 * j + u
                    gate(b + 1, 1 - u)
                    rows1(b + 2, u)
                    dve.wait_ge(s["dn_full"], b + 2)
                    after(dve, ys_stored[u], 16 * j)
                    V.tensor_copy(x_res[u][:, 512:], SS[:, 1, :]).then_inc(s["dn_out1"], 1)
            dve.wait_ge(x2_stored, 16 * NT)
            dve.wait_ge(s["tables"], 1)
            rows1(0, 0)
            rows1(1, 1)
            gate(0, 0)
            return over_pairs(dve, pair)

        LAST = NP // FB

        def over_out(eng, turn):
            for r in range(FB):
                turn(0, r)
            with eng.Fori(1, LAST - 1) as q:
                for r in range(FB):
                    turn(q, r)
            for t in range(NP - FB, NT):
                turn(t // FB, t % FB)

        def ahead(q, r, n):
            q, r = q + (r + n) // FB, (r + n) % FB
            if isinstance(q, int) and FB * q + r > NP:
                return None
            return q, r

        def whole(eng, used):
            eng.wait_ge(s["gx_T"], 4 * used + 4)
            eng.wait_ge(s["dn_full"], 2 * used + 1)

        def sp_phase3(sp):
            whole(sp, pairs_used(sp))
            sp.dma_start(gf_b, final_norm_g.rearrange("(a n) -> a n", a=1).broadcast_to([P, D])).then_inc(gf_loaded, 16)

            def load(q, r):
                sp.dma_start(x_row[r], at_tile(x2_tiles, FB * q + r)).then_inc(fx_loaded[r], 16)
            for r in range(FB):
                load(0, r)

            def turn(q, r):
                t = FB * q + r
                sp.wait_ge(s["fin_out"], t + 1)
                known = isinstance(t, int)
                out = y_sample.rearrange("b l d -> (b l) d") if known and t == NP else at_tile(y_tiles, t)
                sp.dma_start(out, fin_o[r % 2]).then_inc(fy_stored[r % 2], 16)
                if not isinstance(q, int) or ahead(q, r, FB):
                    load(q + 1, r)
            over_out(sp, turn)
            for u in range(2):
                sp.wait_ge(fy_stored[u], 16 * (NP // 2 + 1 - u))
            for sm, n in ((convp_stored, 1), (convs_stored, CW - 1), (vs_stored, 1), (ssm_stored, 2), (x2_stored, NT), (h2_stored, NT)):
                sp.wait_ge(sm, 16 * n)

        def pool_phase3(pool, used):
            whole(pool, used)
            for u in range(2):
                pool.wait_ge(gathered[u], 16 * used + 16)
                pool.wait_ge(ys_stored[u], 16 * used)
            fence(used, 3)

            def gather(q, r):
                t = FB * q + r
                pool.wait_ge(s["fin_idx"], t + 1)
                after(pool, s["fin_add"], t - FB + 1)
                fence(t, 2)
                for k in range(2):
                    nc.gpsimd.indirect_dma_start(out=y_row[r][k], out_offset=None, in_=ys_d[:, :],
                                                 in_offset=bass.IndirectOffsetOnAxis(ap=fidx[r][:, k:k + 1], axis=0)).then_inc(fy_gathered[r], 16)

            def turn(q, r):
                t = FB * q + r
                nxt = ahead(q, r, FB - 1)
                if nxt:
                    gather(*nxt)
                o = r % 2
                pool.wait_ge(s["fin_sq"], t + 1)
                fence(t, 1)
                nc.gpsimd.tensor_scalar(rs[:, o:o + 1], sq[:, o:o + 1], 1.0 / D, EPS, ALU.mult, ALU.add).then_inc(pool_fin, 1)
                pool.wait_ge(pool_fin, t + 1)
                nc.gpsimd.tensor_tensor(rs[:, o:o + 1], rs[:, o:o + 1], neg_half[:, 0:1], ALU.pow).then_inc(s["fin_r"], 1)
            for r in range(FB - 1):
                gather(0, r)
            over_out(pool, turn)

        def act_phase3(act, used):
            def turn(q, r):
                t = FB * q + r
                act.wait_ge(s["fin_add"], t + 1)
                after(act, s["fin_r"], t - 1)
                nc.scalar.activation(fin_s, x_row[r], ACT.Square, accum_out=sq[:, r % 2:r % 2 + 1]).then_inc(s["fin_sq"], 1)
                act.wait_ge(s["fin_sq"], t + 1)
            over_out(act, turn)

        def dve_phase3(dve, used):
            def prepare(q, r):
                t = FB * q + r
                known = isinstance(t, int)
                src = rowpos[:, t, :] if known else rowpos[:, bass.ds(t, 1), :].rearrange("p a c -> p (a c)")
                V.tensor_copy(fidx[r], src).then_inc(s["fin_idx"], 1)
                w = picks[:, t, 4:6] if known else picks[:, bass.ds(t, 1), 4:6].rearrange("p a c -> p (a c)")
                V.tensor_copy(wts[r], w).then_inc(fin_w, 1)

            def turn(q, r):
                t = FB * q + r
                dve.wait_ge(fin_w, t + 1)
                dve.wait_ge(fx_loaded[r], 16 * (q + 1))
                dve.wait_ge(fy_gathered[r], 32 * (q + 1))
                V.scalar_tensor_tensor(out=x_row[r], in0=y_row[r][0], scalar=wts[r][:, 0:1], in1=x_row[r],
                                       op0=ALU.mult, op1=ALU.add).then_inc(fin_one, 1)
                if not (isinstance(t, int) and t == 0):
                    scale(*ahead(q - 1, r, FB - 1))
                dve.wait_ge(fin_one, t + 1)
                V.scalar_tensor_tensor(out=x_row[r], in0=y_row[r][1], scalar=wts[r][:, 1:2], in1=x_row[r],
                                       op0=ALU.mult, op1=ALU.add).then_inc(s["fin_add"], 1)
                dve.wait_ge(s["fin_add"], t + 1)
                if not isinstance(q, int) or ahead(q, r, FB):
                    prepare(q + 1, r)

            def scale(q, r):
                t = FB * q + r
                o = r % 2
                dve.wait_ge(s["fin_r"], t + 1)
                count = 2 * q + r // 2
                after(dve, fy_stored[o], 16 * count)
                V.scalar_tensor_tensor(out=fin_o[o], in0=x_row[r], scalar=rs[:, o:o + 1], in1=gf_b,
                                       op0=ALU.mult, op1=ALU.mult).then_inc(s["fin_out"], 1)
            dve.wait_ge(gf_loaded, 16)
            for r in range(FB):
                prepare(0, r)
            over_out(dve, turn)
            scale(LAST, 0)

        block = ctx.enter_context(nc.Block())

        @block.tensor
        def _(pe):
            pe_phase1(pe)
            pe_phase2(pe)

        @block.scalar
        def _(act):
            act_phase1(act)
            act_phase3(act, act_phase2(act))

        @block.vector
        def _(dve):
            st = dve_phase1(dve)
            dve_tables(dve, st)
            dve_rows_of_picks(dve, st)
            dve_phase3(dve, dve_phase2(dve))

        @block.gpsimd
        def _(pool):
            st = pool_phase1(pool)
            pool_phase3(pool, pool_phase2(pool))

        @block.sync
        def _(sp):
            sp_phase1(sp)
            sp_phase2(sp)
            sp_phase3(sp)


_INS = ["x_prompt", "x_sample", "cache_conv", "state_ssm", "norm1_g", "w_in", "conv_w", "conv_b", "dt_bias", "a_log",
        "d_skip", "ssm_norm_g", "ln_v_g", "ln_v_b", "w_spatial", "b_spatial", "w_out", "norm2_g",
        "w_router_group", "b_router_group", "w_router_expert", "b_router_expert", "w_gate", "w_up", "w_down",
        "final_norm_g"]
_OUTS = [(1, SEQ, D), (SB, SL, D), (1, 1, CW - 1, CD), (1, 1, H, HD, N), (1, SB, CW - 1, CD), (1, SB, H, HD, N),
         (1, SB, SL, W)]


def kernel(**inputs):
    import numpy as _np
    import concourse.bacc as _bacc
    from concourse.bass_utils import run_bass_kernel_spmd as _run

    nc = _bacc.Bacc("TRN2", target_bir_lowering=False, num_devices=1)
    arrays, args = {}, []
    for name in _INS:
        a = _np.ascontiguousarray(inputs[name])
        arrays[f"in_{name}"] = a
        args.append(nc.dram_tensor(f"in_{name}", a.shape, mybir.dt.from_np(a.dtype), kind="ExternalInput").ap())
    for i, shape in enumerate(_OUTS):
        args.append(nc.dram_tensor(f"out_{i}", shape, F32, kind="ExternalOutput").ap())
    build(nc, *args)
    r = _run(nc, [arrays], core_ids=[0])
    return tuple(r.results[0][f"out_{i}"] for i in range(len(_OUTS)))
```

```python
from contextlib import ExitStack

import concourse.bass as bass
from concourse import mybir

F32 = mybir.dt.float32
I32 = mybir.dt.int32
ALU = mybir.AluOpType
ACT = mybir.ActivationFunctionType
AX = mybir.AxisListType

P = 128
D = 1024
KD = D // P
SEQ = 4096
NP = SEQ // P
NT = NP + 1
T = NT * P
SB, SL = 8, 16
H, HD = 8, 64
G, N = 2, 128
W = H * HD
CD = W + 2 * G * N
CB = CD // P
CW = 4
INP = W + CD + H + 2 * W
COL_Z, COL_X, COL_DT, COL_GU, COL_GV = 0, W, W + CD, W + CD + H, W + CD + H + W
NG, EG = 4, 8
NE = NG * EG
DE = 256
NR = NG + NE
R_G1, R_CBIAS, R_CW = 0, KD, KD + CB
R_BSP = R_CW + CW * CB
R_SG = R_BSP + H
R_BSS = R_SG + W // P
NROW = R_BSS + H
N_ROWS = 6
N_CONST = 3 + 2 + 3 + 2 + 1
W_GROUPS = ((COL_X, 512), (COL_X + 512, 512 + H), (COL_GU, 512), (COL_GV, 512), (COL_Z, 512))
NINIT = NE * T // P // 8
NBLK = 2 * T // P + NE
EPS = 1e-6
ARTANH = (2.000000007681758, 0.6666632164140268, 0.40024595229739224, 0.27965157758356346, 0.28157778304302755)
BIG = 1e30


class Steps:

    def __init__(self, eng, sem, fence=lambda n, k: None):
        self.eng, self.sem, self.base, self.n, self.fence = eng, sem, 0, 0, fence

    def inc(self, ins):
        self.n += 1
        ins.then_inc(self.sem, 1)

    def wait(self):
        self.eng.wait_ge(self.sem, self.base + self.n)
        self.fence(self.base, 0)

    def link(self, ins):
        self.inc(ins)
        self.wait()

    def loop_begin(self, per_turn):
        self.before, self.per_turn = self.base + self.n, per_turn

    def loop_at(self, turn):
        self.base, self.n = turn * self.per_turn + self.before, 0

    def loop_end(self, turns):
        assert self.n == self.per_turn, (self.n, self.per_turn)
        self.base, self.n = self.before + turns * self.per_turn, 0


def after(eng, sem, n):
    if isinstance(n, int) and n <= 0:
        return
    eng.wait_ge(sem, n)


DVE_TURN, POOL_TURN = 100, 32


def build(nc, x_prompt, x_sample, cache_conv, state_ssm, norm1_g, w_in, conv_w, conv_b, dt_bias, a_log,
          d_skip, ssm_norm_g, ln_v_g, ln_v_b, w_spatial, b_spatial, w_out, norm2_g,
          w_rg, b_rg, w_re, b_re, w_gate, w_up, w_down, final_norm_g,
          y_prompt, y_sample, conv_prompt, ssm_prompt, conv_sample, ssm_sample, gmlp_v_sample):
    ctx = ExitStack()
    with ctx:
        def sb(name, shape, dt=F32):
            return ctx.enter_context(nc.sbuf_tensor(name, shape, dt))

        def ps(name, shape):
            return ctx.enter_context(nc.psum_tensor(name, shape, F32))

        def sem(name):
            return ctx.enter_context(nc.semaphore(name))

        x2_d = nc.dram_tensor("x2_rows", [T + P, D], F32).ap()
        h2_d = nc.dram_tensor("h2_rows", [T + P, D], F32).ap()
        slot_d = nc.dram_tensor("slot_tokens", [NE * T + P, 2], I32).ap()

        W_IN = KD * INP
        ARENA = W_IN + KD * D
        arena = sb("arena", [P, ARENA])
        w_in_sb = arena[:, 0:W_IN].rearrange("p (k n) -> p k n", k=KD)
        w_out_sb = arena[:, W_IN:].rearrange("p (k n) -> p k n", k=KD)

        ident = sb("ident", [P, P])
        tri = sb("tri", [P, P])
        stri = sb("stri", [P, P])
        tri_s = sb("tri_s", [P, P])
        blk_s = sb("blk_s", [P, P])
        ones = sb("ones", [P, P])
        row_s = sb("row_s", [P, SB])
        iota_g = sb("iota_g", [P, NG])
        iota_e = sb("iota_e", [P, NE])
        neg_half = sb("neg_half", [P, 2])
        tok_id = sb("tok_id", [P, 1])
        g2_b = sb("g2_b", [P, D])
        lng_b = sb("lng_b", [P, W])
        lnb_b = sb("lnb_b", [P, W])
        small_b = sb("small_b", [P, 3 * H])
        dtb_b, alog_b, dsk_b = (small_b[:, k * H:(k + 1) * H] for k in range(3))
        aneg_b = sb("aneg_b", [P, H])
        rb_b = sb("rb_b", [P, NR])
        wr_sb = sb("wr_sb", [P, KD, NR])
        wsT = sb("wsT", [P, H, P])
        slot_init = sb("slot_init", [P, NINIT, 2], I32)
        cols = sb("cols", [P, NROW])

        x_in = [sb(f"x_in{u}", [P, D]) for u in range(2)]
        x_res = [sb(f"x_res{u}", [P, D]) for u in range(2)]
        hT = [sb(f"hT{u}", [P, KD, P]) for u in range(2)]
        xbc = sb("xbc", [P, CD])
        xT = sb("xT", [P, CB, P + CW - 1])
        xc = sb("xc", [P, CB, P])
        xtok = sb("xtok", [P, W])
        btok = sb("btok", [P, G * N])
        gu = [sb("gu", [P, W])] * 2
        zz = [sb("zz", [P, W])] * 2
        gv = sb("gv", [P, W])
        dec = sb("dec", [P, H, P])
        cbm = sb("cbm", [P, G, P])
        xdt = sb("xdt", [P, W])
        xw = sb("xw", [P, W])
        state = sb("state", [P, W])
        yb = sb("yb", [P, W])
        tmp = sb("tmp", [P, W])
        ycat = sb("ycat", [P, D])
        tT = sb("tT", [P, KD, P])
        h2 = sb("h2", [P, D])
        rows = h2[0:NROW, 0:P]
        iota_i = ycat[:, 0:NR + 1].bitcast(I32)
        place_i = ycat[:, 64:64 + NINIT].bitcast(I32)
        slots32 = ycat[:, 0:NE].bitcast(I32)
        dt_t = sb("dt_t", [P, H])
        adt = sb("adt", [P, H])
        dtw = sb("dtw", [P, 8, H])
        e_in = sb("e_in", [P, 3 * H])
        e_out = sb("e_out", [P, 3 * H])
        bn6 = sb("bn6", [P, 6])
        mv = sb("mv", [P, 2])
        sq = sb("sq", [P, 4])
        rs = sb("rs", [P, 8])
        lgs = sb("lgs", [P, NR])
        rt = sb("rt", [P, 16])
        gex = sb("gex", [P, NG + 1])
        gexo = sb("gexo", [P, NG + 1])
        eqt = sb("eqt", [P, NE])
        em = sb("em", [P, NE])
        oh = sb("oh", [P, 3, NE])
        rk = sb("rk", [P, NE])
        carry = sb("carry", [P, NE])
        slots = sb("slots", [P, 6], I32)
        slots_f = slots[:, :].bitcast(F32)
        spare = sb("spare", [P, 4])

        pend_i = sb("pend_i", [P, P], I32)
        tab = sb("tab", [P, 4, P], I32)
        misc = sb("misc", [P, 2], I32)
        tcol = sb("tcol", [P, 5])
        tok0 = sb("tok0", [P, 1])
        idx = [sb(f"idx{n}", [P, 2], I32) for n in range(4)]
        hb2 = [gv[:, 0:DE], gv[:, DE:2 * DE]]

        PB = [ps(f"PB{u}", [P, 512]) for u in range(2)]
        TB = [ps(f"TB{u}", [P, 4, P]) for u in range(2)]
        SS = ps("SS", [P, 2, 512])
        YB = ps("YB", [P, 512])
        MB = ps("MB", [P, 512])
        dt_p, acs_p, tot_p = MB[:, 0:H], MB[:, H:2 * H], MB[:, 2 * H:3 * H]
        cb_p = MB[:, 32:32 + G * P]
        lg_p, rk_p, cnt_p = MB[:, 288:288 + NR], MB[:, 324:324 + NE], MB[:, 356:356 + NE]
        sd_p = MB[:, 400:400 + 4 * SB]


        names = """consts w_scaled eout_a cols_full cols_out ws_full ws_out
            xsq_ready xr_ready x_scaled xT_full xT_out
            proj0 proj1 proj_gv proj_gu proj_z xbc0_out xbc1_out gv_out gu_out z_out
            xbcT_full xbcT_out halo_saved conv_done zs_ready xc_ready cb_done xb_full xb_out
            dt_done dt_read lg_read cb_read rank_read dtneg_ready dtexp_ready dtrec_ready dt_ready trid_ready acs_done bcast_done
            ein_ready eout_ready seg_done decay_ready dec_ready xw_ready
            mixed_done bn_ready vr_ready v_ready ycat_hi
            ydiag_done yoff_done states_done state_ready gated_ready ysq_ready yr_ready ycat_ready
            ycT_full ycT_out out0 out1 x2_half x2sq_ready x2r_ready h2_ready
            h2T_full h2T_out logits_done gexin_ready gexout_ready pick_ready rank_done slots_ready
            smp_zero smp_cache_T smp_cache_out smp_ws_T smp_ws_out smp_st_T smp_st_out smp_masks smp_dec_full
            smp_dec_out smp_new stateT_full stateT_out
            tab_cols tab_rows tab_half fenced tables gx_T gx_out0 gx_out1 gu_full silu_out hb_ready hbT_full hbT_out
            dn_full dn_out0 dn_out1 fin_sq fin_r fin_out""".split()
        s = {n: sem(n) for n in names}
        x_loaded = [sem(f"x_loaded{u}") for u in range(2)]
        res_loaded = [sem(f"res_loaded{u}") for u in range(2)]
        win_loaded = [sem(f"win_loaded{k}") for k in range(len(W_GROUPS))]
        rows_loaded, const_loaded, wout_loaded = sem("rows_loaded"), sem("const_loaded"), sem("wout_loaded")
        lists_set, scattered = sem("lists_set"), sem("scattered")
        x2_stored, h2_stored = sem("x2_stored"), sem("h2_stored")
        convp_stored, convs_stored, ssm_stored = (sem(n) for n in ("convp_stored", "convs_stored", "ssm_stored"))
        smp_loaded = sem("smp_loaded")
        w_loaded, wd_loaded = sem("w_loaded"), sem("wd_loaded")
        idx_loaded = [sem(f"idx_loaded{n}") for n in range(4)]
        gathered = [sem(f"gathered{u}") for u in range(2)]
        added = sem("added")
        fx_loaded = [sem(f"fx_loaded{r}") for r in range(4)]
        fy_stored = [sem(f"fy_stored{u}") for u in range(2)]
        gf_loaded, pool_fin, slots_set = (sem(n) for n in ("gf_loaded", "pool_fin", "slots_set"))
        dve_step, pool_step = sem("dve_step"), sem("pool_step")

        x_tiles = x_prompt.rearrange("a (t p) d -> (a t) p d", p=P)
        y_tiles = y_prompt.rearrange("a (t p) d -> (a t) p d", p=P)
        x2_tiles = x2_d.rearrange("(t p) d -> t p d", p=P)
        h2_tiles = h2_d.rearrange("(t p) d -> t p d", p=P)

        def at_tile(tiles, t):
            if isinstance(t, int):
                return tiles[t, :, :]
            return tiles[bass.ds(t, 1), :, :].rearrange("a p d -> (a p) d")

        def input_tile(t):
            if isinstance(t, int) and t == NP:
                return x_sample.rearrange("b l d -> (b l) d")
            return at_tile(x_tiles, t)

        used = [0]

        def take(n):
            used[0] += n
            assert used[0] <= ARENA, used[0]
            return arena[:, used[0] - n:used[0]]

        CMW = SB * (P + SL)
        st_old = take(SB * W).rearrange("p (q b n) -> p q b n", q=SB, b=4)
        st_T = take(SB * W).rearrange("p (q w) -> p q w", q=SB)
        cmask = take(G * CMW).rearrange("p (g w) -> p g w", g=G)
        bmask = take(G * SB * N).rearrange("p (g q n) -> p g q n", g=G, q=SB)
        wsT_s = take(H * P).rearrange("p (h t) -> p h t", h=H)
        ws_nat = take(H * P).rearrange("p (h t) -> p h t", h=H)
        xT_s = take(CB * SB * (SL + CW - 1)).rearrange("p (b q l) -> p b q l", b=CB, q=SB)
        cache_sb = take(CD)
        adt_e = take(W)
        st_dec = take(4 * SB)
        used[0] = 0
        WSLOT = KD * 2 * DE + 2 * D
        SLOT_AT = [W_IN, 0]
        SLOT = [arena[:, a:a + WSLOT] for a in SLOT_AT]
        take(WSLOT)
        FB = 4
        x_row = [take(D) for _ in range(FB)]
        gf_b = take(D)
        fin_o = [take(D) for _ in range(2)]
        fin_s = take(D)

        def half(b):
            return slice(4 * b, 4 * b + 4)

        def flat(ap):
            return ap.rearrange("p a b -> p (a b)")

        class Turn:

            def __init__(self, j, u):
                self.j, self.u = j, u
                self.i = 2 * j + u
                n = self.i if isinstance(self.i, int) else None
                self.first, self.sample, self.end = n == 0, n == NP, n == NT
                self.prev = not self.first
                self.next, self.next2, self.next3 = (n is None or n + k <= NP for k in (1, 2, 3))

        def over_tiles(eng, turn, steps=None, per_turn=0):
            turn(Turn(0, 0))
            turn(Turn(0, 1))
            last = NP // 2 - 2
            if steps:
                steps.loop_begin(per_turn)
            with eng.Fori(1, last) as j:
                if steps:
                    steps.loop_at(j - 1)
                turn(Turn(j, 0))
                turn(Turn(j, 1))
            if steps:
                steps.loop_end(last - 1)
            for i in range(2 * last, NT + 1):
                turn(Turn(i // 2, i % 2))

        def transpose8(pe, src, waits, done):
            for b in range(2):
                for sm, n in waits(b):
                    after(pe, s[sm], n)
                for k in range(4):
                    mm = nc.tensor.transpose(TB[b][:, k, :], src(4 * b + k), ident[:])
                mm.then_inc(s[done], 1)

        def block_of(t):
            return lambda c: t[:, c * P:(c + 1) * P]

        def project(pe, u, out, col, n, done, waits):
            for sm, v in waits:
                pe.wait_ge(s[sm], v)
            for k in range(KD):
                mm = nc.tensor.matmul(out, hT[u][:, k, :], w_in_sb[:, k, col:col + n], start=k == 0, stop=k == KD - 1)
            mm.then_inc(s[done], 1)

        def pe_turn(pe, tn):
            i, j, u = tn.i, tn.j, tn.u
            v = 1 - u
            if tn.end:
                pe_end(pe, tn)
                return
            if tn.sample:
                pe_sample_setup(pe)
            before = (lambda b: [("xT_out", 3 + b)]) if tn.first else \
                (lambda b: [("smp_st_out", SB - 1 + b)]) if tn.sample else (lambda b: [("ycT_out", 2 * i - 1 + b)])
            transpose8(pe, block_of(xbc), lambda b: [(f"xbc{b}_out", i + 1)] + before(b), "xbcT_full")
            cum, tot = (tri_s, blk_s) if tn.sample else (tri, ones)
            pe.wait_ge(s["dt_ready"], i + 1)
            pe.wait_ge(s["dt_read"], i + 1)
            nc.tensor.matmul(acs_p, cum[:], adt[:], start=True, stop=True)
            nc.tensor.matmul(tot_p, tot[:], adt[:], start=True, stop=True).then_inc(s["acs_done"], 1)
            pe.wait_ge(s["trid_ready"], i + 1)
            pe.wait_ge(s["state_ready"], i + 1)
            if tn.sample:
                pe.wait_ge(s["smp_cache_out"], 2)
            for b in range(2):
                mm = nc.tensor.matmul(SS[:, b, :], tot[:], flat(dec[:, half(b), :]), start=True, stop=True)
            mm.then_inc(s["bcast_done"], 1)
            if tn.next:
                project(pe, v, PB[0][:, :], COL_X, 512, "proj0",
                        [("xT_out", 2 * (i + 2)), ("gu_out", 1) if tn.first else ("x2_half", 2 * i - 1)])
            if tn.prev:
                pe.wait_ge(s["h2_ready"], i)
                transpose8(pe, block_of(h2), lambda b: [("xbcT_out", 2 * i + 1 + b)], "h2T_full")
            if tn.next:
                project(pe, v, PB[1][:, :], COL_X + 512, 512, "proj1",
                        [("z_out", 1) if tn.first else ("x2_half", 2 * i)])
            pe.wait_ge(s["xc_ready"], i + 1)
            after(pe, s["dec_ready"], i)
            pe.wait_ge(s["ein_ready"], i + 1)
            for g in range(G):
                mm = nc.tensor.matmul(cb_p[:, g * P:(g + 1) * P], xc[:, 4 + g, :], xc[:, 6 + g, :], start=True, stop=True)
            mm.then_inc(s["cb_done"], 1)
            for b in range(2):
                pe.wait_ge(*((s["xbcT_out"], 1 + b) if tn.first else (s["h2T_out"], 2 * i - 1 + b)))
                for k in range(4 - 2 * b):
                    mm = nc.tensor.transpose(TB[b][:, k, :], xc[:, 4 * b + k, :], ident[:])
                mm.then_inc(s["xb_full"], 1)
            if tn.prev:
                pe_router(pe, i)
            pe.wait_ge(s["v_ready"], i + 1)
            pe.wait_ge(*((s["xbc0_out"], i + 2) if tn.next else (s["x2_half"], 2 * i - 1)))
            if tn.first:
                pe.wait_ge(s["ws_out"], 2)
            ws = wsT_s if tn.sample else wsT
            for h in range(H):
                c = slice(h * HD, (h + 1) * HD)
                mm = nc.tensor.matmul(PB[0][:, c], ws[:, h, :], gv[:, c], start=True, stop=True)
            mm.then_inc(s["mixed_done"], 1)
            pe.wait_ge(s["dec_ready"], i + 1)
            pe.wait_ge(s["xw_ready"], i + 1)
            after(pe, s["gated_ready"], i)
            for h in range(H):
                c = slice(h * HD, (h + 1) * HD)
                mm = nc.tensor.matmul(YB[:, c], dec[:, h, :], xdt[:, c], start=True, stop=True)
            mm.then_inc(s["ydiag_done"], 1)
            if tn.sample:
                pe_sample_states(pe)
            else:
                for g in range(G):
                    c = slice(g * 256, (g + 1) * 256)
                    mm = nc.tensor.matmul(SS[:, 0, c], xc[:, 6 + g, :], state[:, c], start=True, stop=True)
                mm.then_inc(s["yoff_done"], 1)
                for g in range(G):
                    c = slice(g * 256, (g + 1) * 256)
                    mm = nc.tensor.matmul(SS[:, 1, c], btok[:, g * N:(g + 1) * N], xw[:, c], start=True, stop=True)
                mm.then_inc(s["states_done"], 1)
            if tn.next:
                project(pe, v, PB[1][:, :], COL_GV, 512, "proj_gv", [("xbc1_out", i + 2)])
            if tn.prev:
                pe_rank(pe, i, tn.sample)
            if tn.next:
                project(pe, v, PB[0][:, :], COL_GU, 512, "proj_gu", [("ycat_hi", i + 1)])
            if tn.next2:
                pe.wait_ge(s["x_scaled"], i + 3)
                transpose8(pe, block_of(x_in[u]), lambda b: [("xb_out", 2 * i + 1 + b)], "xT_full")
            if tn.next:
                project(pe, v, PB[1][:, :], COL_Z, 512, "proj_z", [("gv_out", i + 2)])
            pe.wait_ge(s["ycat_ready"], i + 1)
            transpose8(pe, block_of(ycat),
                       lambda b: [("xT_out", 2 * i + 5 + b) if tn.next2 else ("xb_out", 2 * i + 1 + b)], "ycT_full")
            if tn.next:
                project(pe, v, dt_p, COL_DT, H, "dt_done", [("cb_read", 1) if tn.first else ("rank_read", i)])
            pe.wait_ge(s["ycT_out"], 2 * (i + 1))
            if tn.first:
                pe.wait_ge(s["w_scaled"], len(W_GROUPS) + 1)
            for b in range(2):
                if tn.next:
                    pe.wait_ge(s[("gu_out", "z_out")[b]], i + 2)
                else:
                    pe.wait_ge(*((s["ycat_hi"], i + 1) if b == 0 else (s["x2_half"], 2 * i)))
                for k in range(KD):
                    mm = nc.tensor.matmul(PB[b][:, :], tT[:, k, :], w_out_sb[:, k, b * 512:(b + 1) * 512],
                                          start=k == 0, stop=k == KD - 1)
                mm.then_inc(s[f"out{b}"], 1)

        def pe_router(pe, i):
            pe.wait_ge(s["h2T_out"], 2 * i)
            pe.wait_ge(*((s["rank_read"], NP) if isinstance(i, int) and i == NT else (s["cb_read"], i + 1)))
            for k in range(KD):
                mm = nc.tensor.matmul(lg_p, tT[:, k, :], wr_sb[:, k, :], start=k == 0, stop=k == KD - 1)
            mm.then_inc(s["logits_done"], 1)

        def pe_rank(pe, i, after_decay=False):
            pe.wait_ge(s["pick_ready"], i)
            if after_decay:
                pe.wait_ge(s["smp_dec_out"], 1)
            nc.tensor.matmul(rk_p, stri[:], oh[:, 2, :], start=True, stop=True)
            nc.tensor.matmul(cnt_p, ones[:], oh[:, 2, :], start=True, stop=True).then_inc(s["rank_done"], 1)

        def pe_sample_setup(pe):
            pe.wait_ge(smp_loaded, 16 * (SB + 2))
            pe.wait_ge(s["state_ready"], NP + 1)
            R = SB * (CW - 1)
            for c in range(CB):
                mm = nc.tensor.transpose(SS[:, c // 4, (c % 4) * R:(c % 4 + 1) * R], cache_sb[0:R, c * P:(c + 1) * P],
                                         ident[0:R, 0:R])
            mm.then_inc(s["smp_cache_T"], 1)
            transpose8(pe, lambda c: ws_nat[:, c, :], lambda b: [("ycT_out", 2 * NP - 1 + b)], "smp_ws_T")
            for q in range(SB):
                pe.wait_ge(*((s["smp_ws_out"], q + 1) if q < 2 else (s["smp_st_out"], q - 1)))
                for k in range(4):
                    mm = nc.tensor.transpose(TB[q % 2][:, k, :], st_old[:, q, k, :], ident[:])
                mm.then_inc(s["smp_st_T"], 1)

        def pe_sample_states(pe):
            pe.wait_ge(s["smp_masks"], 3)
            pe.wait_ge(s["smp_st_out"], SB)
            pe.wait_ge(s["seg_done"], NP + 1)
            for g in range(G):
                for q in range(SB):
                    mm = nc.tensor.matmul(SS[:, 0, g * 256:(g + 1) * 256], cmask[:, g, q * P:(q + 1) * P],
                                          st_T[:, q, g * 256:(g + 1) * 256], start=q == 0, stop=q == SB - 1)
            mm.then_inc(s["yoff_done"], 1)
            pe.wait_ge(s["lg_read"], NP)
            for b in range(4):
                mm = nc.tensor.matmul(sd_p[:, b * SB:(b + 1) * SB], adt_e[:, b * P:(b + 1) * P], row_s[:], start=True, stop=True)
            mm.then_inc(s["smp_dec_full"], 1)

        def pe_end(pe, tn):
            pe.wait_ge(s["h2_ready"], NT)
            transpose8(pe, block_of(h2), lambda b: [("ycT_out", 2 * NT - 1 + b)], "h2T_full")
            pe_router(pe, NT)
            pe_rank(pe, NT)
            for k in range(4):
                mm = nc.tensor.transpose(YB[:, k * P:(k + 1) * P], state[:, k * P:(k + 1) * P], ident[:])
                if k == 0:
                    mm.then_inc(s["dn_full"], 1)
                if k == 1:
                    mm.then_inc(s["gu_full"], 1)
            mm.then_inc(s["stateT_full"], 1)

        def pe_phase1(pe):
            pe.wait_ge(s["consts"], 1)
            pe.wait_ge(s["x_scaled"], 1)
            transpose8(pe, block_of(x_in[0]), lambda b: [], "xT_full")
            pe.wait_ge(rows_loaded, 16 * N_ROWS)
            nc.tensor.transpose(MB[:, 0:NROW], rows[0:NROW, :], ident[0:NROW, 0:NROW]).then_inc(s["cols_full"], 1)
            pe.wait_ge(s["x_scaled"], 2)
            transpose8(pe, block_of(x_in[1]), lambda b: [("xT_out", 1 + b)], "xT_full")
            project(pe, 0, PB[0][:, :], COL_X, 512, "proj0", [("xT_out", 2), ("w_scaled", 1)])
            project(pe, 0, PB[1][:, :], COL_X + 512, 512, "proj1", [("w_scaled", 2)])
            project(pe, 0, PB[0][:, :], COL_GU, 512, "proj_gu", [("xbc0_out", 1), ("w_scaled", 3)])
            project(pe, 0, PB[1][:, :], COL_GV, 512, "proj_gv", [("xbc1_out", 1), ("w_scaled", 4)])
            project(pe, 0, dt_p, COL_DT, H, "dt_done", [("cols_out", 1)])
            project(pe, 0, PB[1][:, :], COL_Z, 512, "proj_z", [("gv_out", 1), ("w_scaled", 5)])
            pe.wait_ge(const_loaded, 16 * N_CONST)
            for b in range(2):
                for k in range(4):
                    mm = nc.tensor.transpose(SS[:, b, k * P:(k + 1) * P], xc[:, 4 * b + k, :], ident[:])
            mm.then_inc(s["ws_full"], 1)
            pe.wait_ge(s["ws_out"], 2)
            over_tiles(pe, lambda tn: pe_turn(pe, tn))

        def act_turn(act, tn):
            i, j, u = tn.i, tn.j, tn.u
            v = 1 - u
            if tn.end:
                act_end(act)
                return
            if tn.sample:
                act_sample_setup(act)
            for b in range(2):
                act.wait_ge(s["xbcT_full"], 2 * i + 1 + b)
                if tn.sample:
                    for k in range(4):
                        ins = nc.scalar.activation(xT_s[:, 4 * b + k, :, CW - 1:],
                                                   TB[b][:, k, :].rearrange("p (q l) -> p q l", q=SB), ACT.Copy)
                else:
                    act.wait_ge(s["halo_saved"], i + 1)
                    ins = nc.scalar.activation(xT[:, half(b), CW - 1:], TB[b][:, :, :], ACT.Copy)
                ins.then_inc(s["xbcT_out"], 1)
            if tn.prev:
                act_x2sq(act, i - 1, j - 1 + u, v)
            act.wait_ge(s["z_out"], i + 1)
            nc.scalar.activation(zz[u][:, :], zz[u][:, :], ACT.Silu).then_inc(s["zs_ready"], 1)
            if tn.next:
                act.wait_ge(s["proj0"], i + 2)
                if isinstance(i, int) and i == NP - 1:
                    act.wait_ge(convp_stored, 16)
                nc.scalar.activation(xbc[:, 0:512], PB[0][:, :], ACT.Copy).then_inc(s["xbc0_out"], 1)
            act.wait_ge(s["conv_done"], i + 1)
            nc.scalar.activation(xc[:, :, :], xc[:, :, :], ACT.Silu).then_inc(s["xc_ready"], 1)
            act.wait_ge(s["ein_ready"], i + 1)
            act.wait_ge(s["state_ready"], i + 1)
            nc.scalar.activation(e_out[:, :], e_in[:, :], ACT.Exp).then_inc(s["eout_ready"], 1)
            act.wait_ge(s["seg_done"], i + 1)
            nc.scalar.activation(dec[:, :, :], dec[:, :, :], ACT.Exp).then_inc(s["decay_ready"], 1)
            if tn.prev:
                act_h2T(act, i)
            act.wait_ge(s["xb_full"], 2 * i + 1)
            after(act, s["gated_ready"], i)
            nc.scalar.activation(xtok[:, :], flat(TB[0][:, :, :]), ACT.Copy).then_inc(s["xb_out"], 1)
            act.wait_ge(s["xb_full"], 2 * i + 2)
            after(act, s["states_done"], i)
            nc.scalar.activation(btok[:, :], flat(TB[1][:, 0:2, :]), ACT.Copy).then_inc(s["xb_out"], 1)
            if tn.next:
                act.wait_ge(s["proj1"], i + 2)
                nc.scalar.activation(xbc[:, 512:], PB[1][:, :], ACT.Copy).then_inc(s["xbc1_out"], 1)
            if tn.prev:
                act.wait_ge(s["gexin_ready"], i)
                nc.scalar.activation(gexo[:, :], gex[:, :], ACT.Exp).then_inc(s["gexout_ready"], 1)
            if tn.next2:
                act_xsq(act, j + 1, u)
            if tn.sample:
                act.wait_ge(s["smp_dec_full"], 1)
                nc.scalar.activation(st_dec, sd_p, ACT.Exp).then_inc(s["smp_dec_out"], 1)
            act.wait_ge(s["gated_ready"], i + 1)
            for g in range(G):
                c = slice(g * 256, (g + 1) * 256)
                ins = nc.scalar.activation(tmp[:, c], yb[:, c], ACT.Square, accum_out=sq[:, 2 + g:3 + g])
            ins.then_inc(s["ysq_ready"], 1)
            if tn.next:
                act.wait_ge(s["proj_gv"], i + 2)
                act.wait_ge(s["mixed_done"], i + 1)
                nc.scalar.activation(gv[:, :], PB[1][:, :], ACT.Gelu_apprx_tanh).then_inc(s["gv_out"], 1)
                act.wait_ge(s["proj_gu"], i + 2)
                nc.scalar.activation(gu[v][:, :], PB[0][:, :], ACT.Gelu_apprx_tanh).then_inc(s["gu_out"], 1)
            if tn.next2:
                act_xT(act, i + 2, u)
            if tn.next:
                act.wait_ge(s["proj_z"], i + 2)
                nc.scalar.activation(zz[v][:, :], PB[1][:, :], ACT.Copy).then_inc(s["z_out"], 1)
            for b in range(2):
                act.wait_ge(s["ycT_full"], 2 * i + 1 + b)
                after(act, s["logits_done"], i)
                nc.scalar.activation(tT[:, half(b), :], TB[b][:, :, :], ACT.Copy).then_inc(s["ycT_out"], 1)
            if tn.next:
                act.wait_ge(s["dtneg_ready"], i + 2)
                nc.scalar.activation(dtw[:, 2, :], dtw[:, 1, :], ACT.Exp).then_inc(s["dtexp_ready"], 1)
        def act_x2sq(act, i, j, u):
            act.wait_ge(s["x2_half"], 2 * (i + 1))
            after(act, h2_stored, 16 * i)
            after(act, s["h2T_full"], 2 * i)
            nc.scalar.activation(h2[:, :], x_res[u][:, :], ACT.Square, accum_out=sq[:, 1:2]).then_inc(s["x2sq_ready"], 1)

        def act_xsq(act, j, u):
            act.wait_ge(x_loaded[u], 16 * (j + 1))
            nc.scalar.activation(flat(hT[u][:, :, :]), x_in[u][:, :], ACT.Square, accum_out=sq[:, 0:1]).then_inc(s["xsq_ready"], 1)

        def act_xT(act, t, u):
            for b in range(2):
                act.wait_ge(s["xT_full"], 2 * t + 1 + b)
                nc.scalar.activation(hT[u][:, half(b), :], TB[b][:, :, :], ACT.Copy).then_inc(s["xT_out"], 1)

        def act_h2T(act, i):
            for b in range(2):
                act.wait_ge(s["h2T_full"], 2 * i - 1 + b)
                nc.scalar.activation(tT[:, half(b), :], TB[b][:, :, :], ACT.Copy).then_inc(s["h2T_out"], 1)

        def act_sample_setup(act):
            R = SB * (CW - 1)
            act.wait_ge(s["smp_cache_T"], 1)
            for b in range(2):
                for k in range(4):
                    ins = nc.scalar.activation(xT_s[:, 4 * b + k, :, 0:CW - 1],
                                               SS[:, b, k * R:(k + 1) * R].rearrange("p (q l) -> p q l", q=SB), ACT.Copy)
                ins.then_inc(s["smp_cache_out"], 1)
            for q in range(SB):
                act.wait_ge(s["smp_st_T"], q + 1)
                nc.scalar.activation(st_T[:, q, :], flat(TB[q % 2][:, :, :]), ACT.Copy).then_inc(s["smp_st_out"], 1)

        def act_end(act):
            act_x2sq(act, NP, NP // 2, NP % 2)
            act_h2T(act, NT)
            act.wait_ge(s["gexin_ready"], NT)
            nc.scalar.activation(gexo[:, :], gex[:, :], ACT.Exp).then_inc(s["gexout_ready"], 1)
            act.wait_ge(s["stateT_full"], 1)
            nc.scalar.activation(tmp[:, :], YB[:, :], ACT.Copy).then_inc(s["stateT_out"], 1)

        def act_phase1(act):
            for u in range(2):
                if u == 1:
                    act.wait_ge(s["xr_ready"], 1)
                act_xsq(act, 0, u)
                act_xT(act, u, u)
            act.wait_ge(s["proj0"], 1)
            nc.scalar.activation(xbc[:, 0:512], PB[0][:, :], ACT.Copy).then_inc(s["xbc0_out"], 1)
            act.wait_ge(s["proj1"], 1)
            nc.scalar.activation(xbc[:, 512:], PB[1][:, :], ACT.Copy).then_inc(s["xbc1_out"], 1)
            act.wait_ge(s["proj_gu"], 1)
            nc.scalar.activation(gu[0][:, :], PB[0][:, :], ACT.Gelu_apprx_tanh).then_inc(s["gu_out"], 1)
            act.wait_ge(s["proj_gv"], 1)
            nc.scalar.activation(gv[:, :], PB[1][:, :], ACT.Gelu_apprx_tanh).then_inc(s["gv_out"], 1)
            act.wait_ge(const_loaded, 16 * N_CONST)
            nc.scalar.activation(aneg_b[:, :], alog_b, ACT.Exp).then_inc(s["eout_a"], 1)
            act.wait_ge(s["dtneg_ready"], 1)
            nc.scalar.activation(dtw[:, 2, :], dtw[:, 1, :], ACT.Exp).then_inc(s["dtexp_ready"], 1)
            act.wait_ge(s["proj_z"], 1)
            nc.scalar.activation(zz[0][:, :], PB[1][:, :], ACT.Copy).then_inc(s["z_out"], 1)
            over_tiles(act, lambda tn: act_turn(act, tn))

        V = nc.vector

        def per_head(ap):
            return ap.rearrange("p (h a) -> p h a", a=1).broadcast_to([P, H, HD])

        def heads(ap):
            return ap.rearrange("p (h d) -> p h d", h=H)

        def dve_turn(dve, st, tn):
            i, j, u = tn.i, tn.j, tn.u
            v = 1 - u
            if tn.end:
                dve_h2(dve, NP, NP % 2)
                dve_route(dve, st, NT)
                dve_slots(dve, st, NT)
                return
            if tn.sample:
                for b in range(2):
                    dve.wait_ge(s["smp_ws_T"], b + 1)
                    V.tensor_tensor(wsT_s[:, half(b), :], TB[b][:, :, :], over(tri_s, 4), ALU.mult).then_inc(s["smp_ws_out"], 1)
            dve.wait_ge(s["xbcT_out"], 2 * (i + 1))
            tap = cols[:, R_CW:R_CW + CW * CB].rearrange("p (w b) -> p w b", w=CW)
            for w in range(CW - 1, -1, -1):
                for c in range(CB):
                    if tn.sample:
                        src, dst = xT_s[:, c, :, w:w + SL], xc[:, c, :].rearrange("p (q l) -> p q l", q=SB)
                    else:
                        src, dst = xT[:, c, w:w + P], xc[:, c, :]
                    if w == CW - 1:
                        ins = V.tensor_scalar(dst, src, tap[:, w, c:c + 1], cols[:, R_CBIAS + c:R_CBIAS + c + 1], ALU.mult, ALU.add)
                    else:
                        ins = V.scalar_tensor_tensor(out=dst, in0=src, scalar=tap[:, w, c:c + 1], in1=dst, op0=ALU.mult, op1=ALU.add)
                if w > 0:
                    st.link(ins)
                if w == CW - 1 and tn.prev:
                    dve_h2(dve, i - 1, v)
            ins.then_inc(s["conv_done"], 1)
            dve.wait_ge(s["conv_done"], i + 1)
            V.tensor_copy(xT[:, :, 0:CW - 1], xT[:, :, P:]).then_inc(s["halo_saved"], 1)
            dve.wait_ge(s["acs_done"], i + 1)
            st.link(V.tensor_copy(e_in[:, 0:2 * H], MB[:, H:3 * H]))
            V.tensor_tensor(e_in[:, 2 * H:], e_in[:, H:2 * H], e_in[:, 0:H], ALU.subtract).then_inc(s["ein_ready"], 1)
            dve.wait_ge(s["bcast_done"], i + 1)
            for h in range(H):
                a = e_in[:, h:h + 1]
                ins = V.tensor_scalar(dec[:, h, :], SS[:, h // 4, (h % 4) * P:(h % 4 + 1) * P], a, a, ALU.min, ALU.subtract)
            ins.then_inc(s["seg_done"], 1)
            dve.wait_ge(s["cb_done"], i + 1)
            V.tensor_tensor(cbm[:, :, :], cb_p.rearrange("p (g t) -> p g t", g=G),
                            over(tri_s if tn.sample else tri, G), ALU.mult).then_inc(s["cb_read"], 1)
            dve.wait_ge(s["cb_read"], i + 1)
            dve.wait_ge(s["decay_ready"], i + 1)
            for g in range(G):
                ins = V.tensor_tensor(dec[:, half(g), :], dec[:, half(g), :],
                                      cbm[:, g:g + 1, :].broadcast_to([P, 4, P]), ALU.mult)
            ins.then_inc(s["dec_ready"], 1)
            dve.wait_ge(s["xb_out"], 2 * (i + 1))
            dve.wait_ge(s["eout_ready"], i + 1)
            st.link(V.tensor_tensor(heads(xdt[:, :]), heads(xtok[:, :]), per_head(dt_t[:, :]), ALU.mult))
            V.tensor_tensor(heads(xw[:, :]), heads(xdt[:, :]), per_head(e_out[:, 2 * H:]), ALU.mult).then_inc(s["xw_ready"], 1)
            st.inc(V.tensor_tensor(heads(yb[:, :]), heads(xtok[:, :]), per_head(dsk_b), ALU.mult))
            if tn.sample:
                dve_sample_masks(dve, st)
            if tn.prev:
                dve_route(dve, st, i)
            if tn.next2:
                dve_scale_x(dve, i + 2, u)
            dve.wait_ge(s["mixed_done"], i + 1)
            b0 = R_BSS if tn.sample else R_BSP
            st.link(V.tensor_tensor(heads(tmp[:, :]), heads(PB[0][:, :]), per_head(cols[:, b0:b0 + H]), ALU.add))
            V.tensor_tensor(ycat[:, W:], tmp[:, :], gu[u][:, :], ALU.mult).then_inc(s["ycat_hi"], 1)
            dve.wait_ge(s["ydiag_done"], i + 1)
            dve.wait_ge(s["ycat_hi"], i + 1)
            st.inc(V.tensor_tensor(yb[:, :], yb[:, :], YB[:, :], ALU.add))
            dve.wait_ge(s["yoff_done"], i + 1)
            st.link(V.tensor_tensor(heads(tmp[:, :]), heads(SS[:, 0, :]), per_head(e_out[:, 0:H]), ALU.mult))
            st.link(V.tensor_tensor(yb[:, :], yb[:, :], tmp[:, :], ALU.add))
            dve.wait_ge(s["zs_ready"], i + 1)
            V.tensor_tensor(yb[:, :], yb[:, :], zz[u][:, :], ALU.mult).then_inc(s["gated_ready"], 1)
            if not tn.sample:
                dve.wait_ge(s["states_done"], i + 1)
                st.link(V.tensor_tensor(heads(state[:, :]), heads(state[:, :]), per_head(e_out[:, H:2 * H]), ALU.mult))
                V.tensor_tensor(state[:, :], state[:, :], SS[:, 1, :], ALU.add).then_inc(s["state_ready"], 1)
            if tn.prev:
                dve_slots(dve, st, i)
            dve.wait_ge(s["yr_ready"], i + 1)
            for g in range(G):
                c = slice(g * 256, (g + 1) * 256)
                ins = V.tensor_scalar(ycat[:, c], yb[:, c], rs[:, 2 + g:3 + g], None, ALU.mult)
            ins.then_inc(s["ycat_ready"], 1)
            if tn.next:
                dve_v(dve, st, i + 1)
                dve_dt(dve, st, i + 1)
            dve.wait_ge(res_loaded[u], 16 * (j + 1))
            for b in range(2):
                c = slice(b * 512, (b + 1) * 512)
                dve.wait_ge(s[f"out{b}"], i + 1)
                V.tensor_tensor(x_res[u][:, c], x_res[u][:, c], PB[b][:, :], ALU.add).then_inc(s["x2_half"], 1)
        def dve_h2(dve, i, u):
            dve.wait_ge(s["x2_half"], 2 * (i + 1))
            dve.wait_ge(s["x2r_ready"], i + 1)
            V.scalar_tensor_tensor(out=h2[:, :], in0=x_res[u][:, :], scalar=rs[:, 1:2], in1=g2_b[:, :],
                                   op0=ALU.mult, op1=ALU.mult).then_inc(s["h2_ready"], 1)

        def over(mask, n):
            return mask[:, :].rearrange("p (a t) -> p a t", a=1).broadcast_to([P, n, P])

        def dve_scale_x(dve, t, u):
            dve.wait_ge(s["xr_ready"], t + 1)
            V.tensor_scalar(x_in[u][:, :], x_in[u][:, :], rs[:, 0:1], None, ALU.mult).then_inc(s["x_scaled"], 1)

        def dve_v(dve, st, t):
            dve.wait_ge(s["gv_out"], t + 1)
            st.inc(V.bn_stats(bn6[:, :], gv[:, :]))
            st.wait()
            if not isinstance(t, int):
                V.memset(spare[:, 3:4], 0.0)
            V.bn_aggr(mv[:, :], bn6[:, :]).then_inc(s["bn_ready"], 1)
            dve.wait_ge(s["vr_ready"], t + 1)
            st.link(V.tensor_scalar(gv[:, :], gv[:, :], mv[:, 0:1], rs[:, 4:5], ALU.subtract, ALU.mult))
            st.link(V.tensor_tensor(gv[:, :], gv[:, :], lng_b[:, :], ALU.mult))
            V.tensor_tensor(gv[:, :], gv[:, :], lnb_b[:, :], ALU.add).then_inc(s["v_ready"], 1)

        def dve_dt(dve, st, t):
            dve.wait_ge(s["dt_done"], t + 1)
            V.tensor_tensor(dtw[:, 0, :], dt_p, dtb_b, ALU.add).then_inc(s["dt_read"], 1)
            dve.wait_ge(s["dt_read"], t + 1)
            V.scalar_tensor_tensor(out=dtw[:, 1, :], in0=dtw[:, 0, :], scalar=-1.0, in1=dtw[:, 0, :],
                                   op0=ALU.mult, op1=ALU.min).then_inc(s["dtneg_ready"], 1)
            dve.wait_ge(s["dtexp_ready"], t + 1)
            st.link(V.tensor_scalar(dtw[:, 3, :], dtw[:, 2, :], 2.0, None, ALU.add))
            V.reciprocal(dtw[:, 4, :], dtw[:, 3, :]).then_inc(s["dtrec_ready"], 1)

        def first_max(st, src, n, iota, best, key, work, onehot):
            st.link(V.tensor_reduce(best, src, AX.X, ALU.max))
            st.link(V.tensor_scalar(work, src, best, None, ALU.is_equal))
            st.link(V.tensor_tensor(work, work, iota, ALU.mult))
            st.link(V.tensor_reduce(key, work, AX.X, ALU.min))
            st.link(V.tensor_scalar(onehot, iota, key, None, ALU.is_equal))

        def dve_route(dve, st, i):
            dve.wait_ge(s["logits_done"], i)
            V.tensor_tensor(lgs[:, :], lg_p, rb_b[:, :], ALU.add).then_inc(s["lg_read"], 1)
            dve.wait_ge(s["lg_read"], i)
            gbest, gkey, b1, k1, b2, k2 = (rt[:, c:c + 1] for c in range(6))
            gone = rt[:, 12:16]
            first_max(st, lgs[:, 0:NG], NG, iota_g[:, :], gbest, gkey, eqt[:, 0:NG], gone)
            st.inc(V.tensor_scalar(gex[:, 0:NG], lgs[:, 0:NG], gbest, None, ALU.subtract))
            st.link(V.tensor_scalar(gone, gone, -1.0, BIG, ALU.add, ALU.mult))
            st.link(V.tensor_tensor(em[:, :].rearrange("p (g e) -> p g e", g=NG), lgs[:, NG:].rearrange("p (g e) -> p g e", g=NG),
                                    gone.rearrange("p (g a) -> p g a", a=1).broadcast_to([P, NG, EG]), ALU.add))
            first_max(st, em[:, :], NE, iota_e[:, :], b1, k1, eqt[:, :], oh[:, 0, :])
            st.link(V.scalar_tensor_tensor(out=em[:, :], in0=oh[:, 0, :], scalar=-4.0 * BIG, in1=em[:, :], op0=ALU.mult, op1=ALU.add))
            first_max(st, em[:, :], NE, iota_e[:, :], b2, k2, eqt[:, :], oh[:, 1, :])
            V.tensor_tensor(gex[:, NG:], b2, b1, ALU.subtract).then_inc(s["gexin_ready"], 1)
            V.tensor_tensor(oh[:, 2, :], oh[:, 0, :], oh[:, 1, :], ALU.add).then_inc(s["pick_ready"], 1)

        def dve_slots(dve, st, i):
            k1, k2 = rt[:, 3:4], rt[:, 5:6]
            ssum, den, w1, w2, p1, p2 = (rt[:, c:c + 1] for c in range(6, 12))
            dve.wait_ge(s["gexout_ready"], i)
            st.link(V.tensor_reduce(ssum, gexo[:, 0:NG], AX.X, ALU.add))
            st.link(V.tensor_scalar(den, gexo[:, NG:], 1.0, ssum, ALU.add, ALU.mult))
            st.link(V.reciprocal(w1, den))
            st.inc(V.tensor_tensor(w2, w1, gexo[:, NG:], ALU.mult))
            dve.wait_ge(s["rank_done"], i)
            st.link(V.tensor_tensor(rk[:, :], rk_p, carry[:, :], ALU.add))
            V.tensor_tensor(carry[:, :], carry[:, :], cnt_p, ALU.add).then_inc(s["rank_read"], 1)
            for k, p in ((0, p1), (1, p2)):
                st.link(V.tensor_tensor(eqt[:, :], oh[:, k, :], rk[:, :], ALU.mult))
                st.link(V.tensor_reduce(p, eqt[:, :], AX.X, ALU.add))
            st.inc(V.scalar_tensor_tensor(out=rt[:, 0:1], in0=k1, scalar=float(T), in1=p1, op0=ALU.mult, op1=ALU.add))
            st.link(V.scalar_tensor_tensor(out=rt[:, 1:2], in0=k2, scalar=float(T), in1=p2, op0=ALU.mult, op1=ALU.add))
            after(dve, scattered, 32 * (i - 1))
            st.inc(V.tensor_scalar(slots[:, 0:2], rt[:, 0:2], float(NE * T), None, ALU.add))
            for k, weight in enumerate((w1, w2)):
                st.inc(V.tensor_copy(slots[:, 2 + 2 * k:3 + 2 * k], tok_id[:, :]))
                st.inc(V.tensor_copy(slots_f[:, 3 + 2 * k:4 + 2 * k], weight))
            st.wait()
            V.tensor_scalar(tok_id[:, :], tok_id[:, :], float(P), None, ALU.add).then_inc(s["slots_ready"], 1)
            dve.wait_ge(s["slots_ready"], i)

        def dve_sample_masks(dve, st):
            dve.wait_ge(s["smp_zero"], 2)
            dve.wait_ge(s["xc_ready"], NT)
            for g in range(G):
                ins = V.tensor_copy(cmask[:, g, :].rearrange("p (q w) -> p q w", q=SB)[:, :, 0:SL],
                                    xc[:, 6 + g, :].rearrange("p (q l) -> p q l", q=SB))
            ins.then_inc(s["smp_masks"], 1)
            for g in range(G):
                ins = V.tensor_tensor(bmask[:, g, :, :],
                                      btok[:, g * N:(g + 1) * N].rearrange("p (a n) -> p a n", a=1).broadcast_to([P, SB, N]),
                                      row_s[:, :].rearrange("p (q a) -> p q a", a=1).broadcast_to([P, SB, N]), ALU.mult)
            ins.then_inc(s["smp_masks"], 1)
            V.tensor_copy(heads(adt_e), per_head(adt[:, :])).then_inc(s["smp_masks"], 1)

        def dve_sample_states(dve, st):
            dve.wait_ge(s["smp_dec_out"], 1)
            for n in range(8):
                b, w = n // 2, n % 2
                o = st_old[:, half(w), b, :]
                d = st_dec[:, b * SB + 4 * w:b * SB + 4 * w + 4].rearrange("p (q a) -> p q a", a=1).broadcast_to([P, 4, N])
                dve.wait_ge(s["states_done"], NP + 1 + n)
                st.link(V.tensor_tensor(o, o, d, ALU.mult))
                V.tensor_tensor(o, o, SS[:, n % 2, :].rearrange("p (q n) -> p q n", q=4), ALU.add).then_inc(s["smp_new"], 1)

        def dve_phase1(dve):
            st = Steps(dve, dve_step)
            V.memset(xT[:, :, 0:CW - 1], 0.0).then_inc(s["halo_saved"], 1)
            st.inc(V.memset(carry[:, :], 0.0))
            V.memset(state[:, :], 0.0).then_inc(s["state_ready"], 1)
            dve_scale_x(dve, 0, 0)
            dve_scale_x(dve, 1, 1)
            dve.wait_ge(s["cols_full"], 1)
            V.tensor_copy(cols[:, :], MB[:, 0:NROW]).then_inc(s["cols_out"], 1)
            dve.wait_ge(s["consts"], 1)
            st.link(V.tensor_scalar(place_i, place_i, P - 1, None, ALU.bitwise_and))
            V.tensor_scalar(slot_init[:, :, 0], place_i, float(T), None, ALU.add).then_inc(slots_set, 1)
            dve.wait_ge(s["cols_out"], 1)
            for g, (c, n) in enumerate(W_GROUPS):
                dve.wait_ge(win_loaded[g], 16)
                for k in range(KD):
                    ins = V.tensor_scalar(w_in_sb[:, k, c:c + n], w_in_sb[:, k, c:c + n], cols[:, R_G1 + k:R_G1 + k + 1], None, ALU.mult)
                ins.then_inc(s["w_scaled"], 1)
            dve.wait_ge(s["eout_a"], 1)
            st.link(V.tensor_scalar(aneg_b[:, :], aneg_b[:, :], -1.0, None, ALU.mult))
            dve_dt(dve, st, 0)
            dve_v(dve, st, 0)
            dve.wait_ge(s["ws_full"], 1)
            for b in range(2):
                V.tensor_tensor(wsT[:, half(b), :], SS[:, b, :].rearrange("p (h t) -> p h t", h=4), over(tri, 4),
                                ALU.mult).then_inc(s["ws_out"], 1)
            dve.wait_ge(wout_loaded, 16)
            for k in range(W // P):
                ins = V.tensor_scalar(w_out_sb[:, k, :], w_out_sb[:, k, :], cols[:, R_SG + k:R_SG + k + 1], None, ALU.mult)
            ins.then_inc(s["w_scaled"], 1)
            over_tiles(dve, lambda tn: dve_turn(dve, st, tn), st, DVE_TURN)
            return st

        def fence(n, k):
            if not isinstance(n, int):
                nc.gpsimd.tensor_tensor(spare[:, k:k + 1], neg_half[:, 0:1], neg_half[:, 0:1], ALU.mult)

        def root(pool, st, out, in_, scale, n):
            st.link(nc.gpsimd.tensor_scalar(out, in_, scale, EPS, ALU.mult, ALU.add))
            return nc.gpsimd.tensor_tensor(out, out, neg_half[:, 0:n], ALU.pow)

        def pool_turn(pool, st, tn):
            i, j, u = tn.i, tn.j, tn.u
            if tn.end:
                pool_scatter(pool, NT)
                return
            if tn.sample:
                pool.wait_ge(s["dt_done"], NT)
                nc.gpsimd.memset(cmask[:, :, :], 0.0).then_inc(s["smp_zero"], 1)
            if tn.next2:
                pool.wait_ge(s["xsq_ready"], i + 3)
                fence(i, 1)
                root(pool, st, rs[:, 0:1], sq[:, 0:1], 1.0 / D, 1).then_inc(s["xr_ready"], 1)
            pool.wait_ge(s["ysq_ready"], i + 1)
            fence(i, 1)
            root(pool, st, rs[:, 2:4], sq[:, 2:4], 1.0 / 256, 2).then_inc(s["yr_ready"], 1)
            if tn.prev:
                pool_scatter(pool, i)
            if tn.next:
                pool_v(pool, st, i + 1)
                pool_dt(pool, st, i + 1)
            if isinstance(i, int) and i == NP - 1:
                pool.wait_ge(s["dt_done"], NT)
                nc.gpsimd.memset(ws_nat[:, :, :], 0.0).then_inc(s["smp_zero"], 1)
            pool.wait_ge(s["x2sq_ready"], i + 1)
            fence(i, 1)
            root(pool, st, rs[:, 1:2], sq[:, 1:2], 1.0 / D, 1).then_inc(s["x2r_ready"], 1)

        def pool_v(pool, st, t):
            pool.wait_ge(s["bn_ready"], t + 1)
            fence(t, 1)
            root(pool, st, rs[:, 4:5], mv[:, 1:2], 1.0, 1).then_inc(s["vr_ready"], 1)

        def pool_dt(pool, st, t):
            g = nc.gpsimd
            pool.wait_ge(s["dtrec_ready"], t + 1)
            after(pool, s["xw_ready"], t)
            r, r2, a = dtw[:, 5, :], dtw[:, 6, :], dtw[:, 7, :]
            st.link(g.tensor_tensor(r, dtw[:, 2, :], dtw[:, 4, :], ALU.mult))
            st.link(g.tensor_tensor(r2, r, r, ALU.mult))
            st.link(g.tensor_scalar(a, r2, ARTANH[4], ARTANH[3], ALU.mult, ALU.add))
            for k in (2, 1, 0):
                st.link(g.tensor_tensor(a, a, r2, ALU.mult))
                st.link(g.tensor_scalar(a, a, ARTANH[k], None, ALU.add))
            st.inc(g.tensor_scalar(dtw[:, 3, :], dtw[:, 0, :], 0.0, None, ALU.max))
            st.link(g.tensor_tensor(a, a, r, ALU.mult))
            st.link(g.tensor_tensor(dt_t[:, :], a, dtw[:, 3, :], ALU.add))
            g.tensor_tensor(adt[:, :], dt_t[:, :], aneg_b[:, :], ALU.mult).then_inc(s["dt_ready"], 1)
            pool.wait_ge(s["dt_ready"], t + 1)
            after(pool, s["ydiag_done"], t)
            mask = tri_s if isinstance(t, int) and t == NP else tri
            g.tensor_tensor(dec[:, :, :], over(mask, H), adt[:, :].rearrange("p (h a) -> p h a", a=1).broadcast_to([P, H, P]),
                            ALU.mult).then_inc(s["trid_ready"], 1)

        def pool_scatter(pool, i):
            pool.wait_ge(s["slots_ready"], i)
            fence(i, 2)
            if isinstance(i, int) and i == 1:
                pool.wait_ge(lists_set, 16 * 9)
            for k in range(2):
                nc.gpsimd.indirect_dma_start(out=slot_d[:, :], out_offset=bass.IndirectOffsetOnAxis(ap=slots[:, k:k + 1], axis=0),
                                             in_=slots[:, 2 + 2 * k:4 + 2 * k], in_offset=None).then_inc(scattered, 16)

        def pool_phase1(pool):
            g = nc.gpsimd
            st = Steps(pool, pool_step, fence)

            def select(out, in_, op, fill, base, pattern, mult):
                st.link(g.affine_select(out=out, in_=in_, compare_op=op, fill=fill, base=base, pattern=pattern,
                                        channel_multiplier=mult))
            st.inc(g.memset(neg_half[:], -0.5))
            st.inc(g.memset(ident[:], 0.0))
            st.inc(g.memset(ones[:], 1.0))
            st.inc(g.memset(row_s[:], 1.0))
            st.link(g.memset(slot_init[:], 0))
            select(ident[:], ident[:], ALU.not_equal, 1.0, 0, [[-1, P]], 1)
            select(tri[:], ones[:], ALU.is_ge, 0.0, 0, [[1, P]], -1)
            select(stri[:], ones[:], ALU.is_gt, 0.0, 0, [[1, P]], -1)
            q_of = blk_s[:].rearrange("p (q l) -> p q l", q=SB)
            select(row_s[:], row_s[:], ALU.is_ge, 0.0, 0, [[-SL, SB]], 1)
            select(row_s[:], row_s[:], ALU.is_ge, 0.0, SL - 1, [[SL, SB]], -1)
            select(q_of, ones[:].rearrange("p (q l) -> p q l", q=SB), ALU.is_ge, 0.0, 0, [[-SL, SB], [0, SL]], 1)
            select(q_of, q_of, ALU.is_ge, 0.0, SL - 1, [[SL, SB], [0, SL]], -1)
            st.link(g.tensor_tensor(tri_s[:], tri[:], blk_s[:], ALU.mult))
            st.inc(g.iota(iota_i[:, 0:NG], pattern=[[1, NG]], base=-NG, channel_multiplier=0))
            st.inc(g.iota(iota_i[:, NG:NR], pattern=[[1, NE]], base=-NE, channel_multiplier=0))
            st.inc(g.iota(place_i, pattern=[[1, NINIT]], base=0, channel_multiplier=NINIT % P))
            st.link(g.iota(iota_i[:, NR:NR + 1], pattern=[[1, 1]], base=0, channel_multiplier=1))
            st.inc(g.tensor_copy(iota_g[:], iota_i[:, 0:NG]))
            st.inc(g.tensor_copy(iota_e[:], iota_i[:, NG:NR]))
            st.inc(g.tensor_copy(tok0[:], iota_i[:, NR:NR + 1]))
            g.tensor_copy(tok_id[:], iota_i[:, NR:NR + 1]).then_inc(s["consts"], 1)
            for t in range(2):
                pool.wait_ge(s["xsq_ready"], t + 1)
                if t == 1:
                    pool.wait_ge(s["x_scaled"], 1)
                root(pool, st, rs[:, 0:1], sq[:, 0:1], 1.0 / D, 1).then_inc(s["xr_ready"], 1)
            pool_dt(pool, st, 0)
            pool_v(pool, st, 0)
            over_tiles(pool, lambda tn: pool_turn(pool, st, tn), st, POOL_TURN)
            return st

        def sp_turn(sp, tn):
            i, j, u = tn.i, tn.j, tn.u
            v = 1 - u
            if tn.next3:
                sp.wait_ge(s["xT_full"], 2 * (i + 2))
                sp.dma_start(x_in[v][:, :], input_tile(i + 3)).then_inc(x_loaded[v], 16)
            if tn.prev:
                sp.wait_ge(s["h2_ready"], i)
                sp.dma_start(at_tile(x2_tiles, i - 1), x_res[v][:, :]).then_inc(x2_stored, 16)
                sp.dma_start(at_tile(h2_tiles, i - 1), h2[:, :]).then_inc(h2_stored, 16)
            if tn.end:
                sp.dma_start(at_tile(x2_tiles, NT), x_res[v][:, :]).then_inc(x2_stored, 16)
                sp.dma_start(at_tile(h2_tiles, NT), h2[:, :]).then_inc(h2_stored, 16)
            if tn.next:
                after(sp, x2_stored, 16 * i)
                sp.dma_start(x_res[v][:, :], input_tile(i + 1)).then_inc(res_loaded[v], 16)
            if isinstance(i, int) and i == NP - 1:
                sp.wait_ge(s["xbc1_out"], NP)
                sp.dma_start(conv_prompt[0, 0, :, :], xbc[P - CW + 1:, :]).then_inc(convp_stored, 16)
                sp.wait_ge(s["dt_done"], NT)
                sp.dma_start(cache_sb[0:SB * (CW - 1), :], cache_conv.rearrange("a q l c -> (a q l) c")).then_inc(smp_loaded, 16)
                sp.dma_start(st_old, state_ssm.rearrange("a q (b h) d n -> (h d) (a q) b n", b=4)).then_inc(smp_loaded, 16)
                sp.wait_ge(s["smp_zero"], 1)
                for q in range(SB):
                    c = slice(q * SL, (q + 1) * SL)
                    sp.dma_start(ws_nat[c, :, c], w_spatial[0, :, 0:SL, 0:SL].rearrange("h t s -> t h s")).then_inc(smp_loaded, 16)
            if tn.sample:
                sp.wait_ge(s["xbc1_out"], NT)
                for k in range(CW - 1):
                    sp.dma_start(conv_sample[0, :, k, :], xbc[SL - CW + 1 + k::SL, :]).then_inc(convs_stored, 16)
                sp.wait_ge(s["v_ready"], NT)
                sp.dma_start(gmlp_v_sample.rearrange("a q l c -> (a q l) c"), gv[:, :]).then_inc(convs_stored, 16)

        def store_states(sp):
            sp.wait_ge(s["smp_new"], 8)
            sp.dma_start(ssm_sample.rearrange("a q (b h) d n -> (h d) (a q) b n", b=4), st_old).then_inc(ssm_stored, 16)
            sp.wait_ge(s["stateT_out"], 1)
            sp.dma_start(ssm_prompt.rearrange("a q (b h) d n -> (h d) (a q b) n", b=4),
                         tmp[:, :].rearrange("p (b n) -> p b n", b=4)).then_inc(ssm_stored, 16)

        def sp_phase1(sp):
            for u in range(2):
                sp.dma_start(x_in[u][:, :], input_tile(u)).then_inc(x_loaded[u], 16)

            def small(dst, src, loaded=const_loaded):
                sp.dma_start(dst, src).then_inc(loaded, 16)
                count[loaded] += 1
            count = {rows_loaded: 0, const_loaded: 0}
            small(rows[R_G1:R_G1 + KD, :], norm1_g.rearrange("a (k p) -> (a k) p", p=P), rows_loaded)
            small(rows[R_CBIAS:R_CBIAS + CB, :], conv_b.rearrange("a (k p) -> (a k) p", p=P), rows_loaded)
            small(rows[R_CW:R_BSP, :], conv_w.rearrange("a w (k p) -> (a w k) p", p=P), rows_loaded)
            small(rows[R_BSP:R_SG, :], b_spatial[0, :, :], rows_loaded)
            small(rows[R_SG:R_BSS, :], ssm_norm_g.rearrange("a (k p) -> (a k) p", p=P), rows_loaded)
            small(rows[R_BSS:NROW, :].rearrange("h (q l) -> h q l", q=SB),
                  b_spatial[0, :, 0:SL].rearrange("h (a l) -> h a l", a=1).broadcast_to([H, SB, SL]), rows_loaded)
            w_rows = w_in[0, :, :].rearrange("(k p) n -> p k n", p=P)
            for k, (c, n) in enumerate(W_GROUPS):
                sp.dma_start(w_in_sb[:, :, c:c + n], w_rows[:, :, c:c + n]).then_inc(win_loaded[k], 16)
                if k == 0:
                    for q, w in enumerate((dt_bias, a_log, d_skip)):
                        small(small_b[:, q * H:(q + 1) * H], w.broadcast_to([P, H]))
                    small(rb_b[:, 0:NG], b_rg.broadcast_to([P, NG]))
                    small(rb_b[:, NG:], b_re.broadcast_to([P, NE]))
                    small(g2_b[:, :], norm2_g.broadcast_to([P, D]))
                    small(lng_b[:, :], ln_v_g.broadcast_to([P, W]))
                    small(lnb_b[:, :], ln_v_b.broadcast_to([P, W]))
                    small(wr_sb[:, :, 0:NG], w_rg[0, :, :].rearrange("(k p) n -> p k n", p=P))
                    small(wr_sb[:, :, NG:], w_re[0, :, :].rearrange("(k p) n -> p k n", p=P))
            small(xc[:, :, :], w_spatial[0, :, :, :].rearrange("h t s -> t h s"))
            assert (count[rows_loaded], count[const_loaded]) == (N_ROWS, N_CONST), count
            sp.dma_start(x_res[0][:, :], input_tile(0)).then_inc(res_loaded[0], 16)
            sp.dma_start(w_out_sb[:, :, :], w_out[0, :, :].rearrange("(k p) n -> p k n", p=P)).then_inc(wout_loaded, 16)
            sp.wait_ge(s["xT_full"], 2)
            sp.dma_start(x_in[0][:, :], input_tile(2)).then_inc(x_loaded[0], 16)
            sp.wait_ge(slots_set, 1)
            for k in range(8):
                part = slot_d[0:NE * T, :].rearrange("(c p n) a -> c p (n a)", c=8, p=P)[k, :, :]
                sp.dma_start(part, flat(slot_init[:, :, :])).then_inc(lists_set, 16)
            sp.dma_start(slot_d[NE * T:, :].rearrange("(a n) b -> a (n b)", a=1), flat(slot_init[0:1, 0:P, :])).then_inc(lists_set, 16)
            over_tiles(sp, lambda tn: sp_turn(sp, tn))

        TAB_OFF, TAB_SLOT, TAB_NTH = 0, 1, 2
        hTb = xdt[:, 0:2 * P].rearrange("p (k t) -> p k t", k=2)
        silu_g = [ycat[:, 0:DE], ycat[:, DE:2 * DE]]
        YBv = YB[:, 0:2 * P].rearrange("p (k t) -> p k t", k=2)
        SURE = 2 * T // P // 2

        def entry(eng, row, at, low, high):
            return eng.value_load(tab[0:1, row, bass.ds(at, 1)], min_val=low, max_val=high)

        def pairs_used(eng):
            return eng.value_load(misc[0:1, 0:1], min_val=SURE, max_val=NBLK // 2)

        def weight_of(n):
            return idx[n][:, 1:2].bitcast(F32)

        def over_pairs(eng, pair):
            used = pairs_used(eng)
            assert SURE % 2 and NBLK // 2 % 2
            pair(0, 0)
            with eng.Fori(0, SURE // 2) as q:
                pair(q, 1)
                pair(q + 1, 0)
            with eng.Fori(SURE // 2, NBLK // 4) as q:
                with eng.If(2 * q + 1 < used):
                    pair(q, 1)
                with eng.If(2 * q + 2 < used):
                    pair(q + 1, 0)
            return used

        def dve_tables(dve, st):
            nb, some, pend, pstart, nth = (eqt[:, :], em[:, :], oh[:, 0, :], oh[:, 1, :], oh[:, 2, :])
            ni = slots32[:, 0:NE]
            col = [rt[:, c:c + 1] for c in range(12)]
            block, ebase, kth, start, place, last = col[0:6]
            st.link(V.tensor_scalar(ni, carry[:, :], float(P - 1), None, ALU.add))
            st.link(V.tensor_scalar(ni, ni, 7, None, ALU.logical_shift_right))
            st.link(V.tensor_copy(nb, ni))
            st.inc(V.tensor_scalar(some, nb, 1.0, None, ALU.min))
            st.link(V.tensor_tensor_scan(out=pend, data0=ones[:, 0:NE], data1=nb, initial=0.0, op0=ALU.mult, op1=ALU.add))
            st.link(V.memset(some[:, 0:1], 1.0))
            st.inc(V.tensor_tensor(pstart, pend, nb, ALU.subtract))
            st.link(V.tensor_tensor_scan(out=nth, data0=ones[:, 0:NE], data1=some, initial=0.0, op0=ALU.mult, op1=ALU.add))
            cmp = rk[:, :]
            st.link(V.tensor_scalar(cmp, pend, tok0[:, :], None, ALU.is_le))
            st.inc(V.tensor_reduce(ebase, cmp, AX.X, ALU.add))
            st.link(V.tensor_tensor(cmp, cmp, some, ALU.mult))
            st.inc(V.tensor_reduce(kth, cmp, AX.X, ALU.add))
            st.link(V.tensor_scalar(last, nth[:, NE - 1:NE], -1.0, None, ALU.add))
            st.inc(V.tensor_tensor(kth, kth, last, ALU.min))
            st.link(V.tensor_scalar(ebase, ebase, float(NE - 1), float(-NE), ALU.min, ALU.add))
            st.link(V.tensor_scalar(cmp, iota_e[:, :], ebase, None, ALU.is_equal))
            st.link(V.tensor_tensor(cmp, cmp, pstart, ALU.mult))
            st.link(V.tensor_reduce(start, cmp, AX.X, ALU.add))
            st.link(V.tensor_tensor(place, tok0[:, :], start, ALU.subtract))
            st.link(V.tensor_scalar(place, place, float(T // P), float(P), ALU.min, ALU.mult))
            st.inc(V.scalar_tensor_tensor(out=place, in0=ebase, scalar=float(T), in1=place, op0=ALU.mult, op1=ALU.add))
            st.link(V.tensor_copy(ni[:, 0:1], kth))
            st.link(V.tensor_scalar(ni[:, 0:1], ni[:, 0:1], 1, None, ALU.bitwise_and))
            st.inc(V.tensor_scalar(tcol[:, 0:1], place, float(NE * T), None, ALU.add))
            st.inc(V.tensor_scalar(tcol[:, 1:2], ni[:, 0:1], float(SLOT_AT[1] - SLOT_AT[0]), float(SLOT_AT[0]), ALU.mult, ALU.add))
            st.inc(V.tensor_scalar(tcol[:, 2:3], kth, 1.0, None, ALU.add))
            st.link(V.tensor_scalar(cmp, nth, tok0[:, :], None, ALU.is_le))
            st.link(V.tensor_reduce(start, cmp, AX.X, ALU.add))
            st.link(V.tensor_scalar(tcol[:, 3:4], start, float(NE - 1), None, ALU.min))
            st.inc(V.tensor_scalar(last, tok0[:, :], 1.0, None, ALU.add))
            st.wait()
            st.link(V.tensor_scalar(cmp, nth, last, None, ALU.is_le))
            st.link(V.tensor_tensor(cmp, cmp, pend, ALU.mult))
            st.link(V.tensor_reduce(start, cmp, AX.X, ALU.max))
            V.tensor_scalar(tcol[:, 4:5], start, 1.0, None, ALU.add).then_inc(s["tab_cols"], 1)
            st.inc(V.tensor_copy(misc[:, 1:2], nth[:, NE - 1:NE]))
            st.link(V.tensor_scalar(misc[:, 0:1], pend[:, NE - 1:NE], 1.0, None, ALU.add))
            st.link(V.tensor_scalar(misc[:, 0:1], misc[:, 0:1], 1, None, ALU.logical_shift_right))
            dve.wait_ge(s["tab_rows"], 1)
            V.tensor_copy(tab[0:1, :, :], MB[0:1, :].rearrange("p (a b) -> p a b", a=4)).then_inc(s["tab_half"], 1)
            dve.wait_ge(s["tab_rows"], 2)
            V.tensor_copy(pend_i[0:1, :], MB[0:1, 0:P]).then_inc(s["tables"], 1)

        def load_row(sp, q, r):
            sp.dma_start(x_row[r], at_tile(x2_tiles, FB * q + r)).then_inc(fx_loaded[r], 16)

        def sp_phase2(sp):
            def of(x, e):
                return x[0, e, :, :] if isinstance(e, int) else x[0, bass.ds(e, 1), :, :].rearrange("a k n -> (a k) n")

            def load_gate_up(e, slot):
                gup = SLOT[slot][:, 0:KD * 2 * DE].rearrange("p (k n) -> p k n", k=KD)
                sp.dma_start(gup[:, :, 0:DE], of(w_gate, e).rearrange("(k p) n -> p k n", p=P)).then_inc(w_loaded, 16)
                sp.dma_start(gup[:, :, DE:], of(w_up, e).rearrange("(k p) n -> p k n", p=P)).then_inc(w_loaded, 16)

            def load_down(e, slot):
                dn = SLOT[slot][:, KD * 2 * DE:].rearrange("p (k n) -> p k n", k=2)
                sp.dma_start(dn, of(w_down, e).rearrange("(k p) n -> p k n", p=P)).then_inc(wd_loaded, 16)

            sp.wait_ge(s["x2_half"], 2 * NT)
            load_gate_up(0, 0)
            load_down(0, 0)
            store_states(sp)
            sp.wait_ge(s["tables"], 1)
            sp.wait_ge(w_loaded, 32)
            sp.wait_ge(wd_loaded, 16)
            sp.wait_ge(ssm_stored, 32)
            experts = sp.value_load(misc[0:1, 1:2], min_val=1, max_val=NE)
            with sp.If(1 < experts):
                second = entry(sp, 3, 1, 0, NE - 1)
                load_gate_up(second, 1)
                load_down(second, 1)
            sp.dma_start(gf_b, final_norm_g.rearrange("(a n) -> a n", a=1).broadcast_to([P, D])).then_inc(gf_loaded, 16)
            with sp.Fori(1, NE // 2) as m:
                for c in range(2):
                    k = 2 * m + c
                    with sp.If(k < experts):
                        expert = entry(sp, 3, k, 0, NE - 1)
                        before = sp.value_load(pend_i[0:1, bass.ds(k - 2, 1)], min_val=1, max_val=NBLK + 1)
                        sp.wait_ge(w_loaded, 32 * k)
                        sp.wait_ge(s["gu_full"], before)
                        load_gate_up(expert, c)
                        sp.wait_ge(wd_loaded, 16 * k)
                        sp.wait_ge(s["dn_full"], before)
                        load_down(expert, c)

        def pool_phase2(pool):
            pool.wait_ge(s["tables"], 1)
            pool.wait_ge(scattered, 32 * NT)
            pool.wait_ge(h2_stored, 16 * (NT + 1))

            def carry_waits(n):
                after(pool, s["fenced"], n)
                nc.gpsimd.tensor_tensor(spare[:, 1:2], neg_half[:, 0:1], neg_half[:, 0:1], ALU.mult).then_inc(s["fenced"], 1)

            def gather(q, n, fences):
                b, u = 4 * q + n, n % 2
                off = entry(pool, TAB_OFF, b, 0, NE * T)
                after(pool, added, 16 * (b - 3))
                pool.dma_start(idx[n][:, :], slot_d[bass.ds(off, P), :]).then_inc(idx_loaded[n], 16)
                pool.wait_ge(idx_loaded[n], 16 * (q + 1))
                after(pool, s["gx_T"], 2 * (b - 1))
                carry_waits(fences)
                nc.gpsimd.indirect_dma_start(out=x_in[u][:, :], out_offset=None, in_=h2_d[:, :],
                                             in_offset=bass.IndirectOffsetOnAxis(ap=idx[n][:, 0:1], axis=0)).then_inc(gathered[u], 16)

            def pair(q, w):
                for u in range(2):
                    n = 2 * w + u
                    b = 4 * q + n
                    gather(q + (n + 3) // 4, (n + 3) % 4, 2 * b + 3)
                    after(pool, added, 16 * b)
                    for k in range(2):
                        pool.wait_ge(s[f"dn_out{k}"], b + 1)
                    carry_waits(2 * b + 4)
                    nc.gpsimd.indirect_dma_start(out=x2_d[:, :], in_=x_res[u][:, :], in_offset=None, compute_op=ALU.add,
                                                 out_offset=bass.IndirectOffsetOnAxis(ap=idx[n][:, 0:1], axis=0)).then_inc(added, 16)
            for n in range(3):
                gather(0, n, n)
            return over_pairs(pool, pair)

        def pe_rows(pe, b, u, j):
            pe.wait_ge(gathered[u], 16 * (j + 1))
            for k in range(2):
                after(pe, s[f"gx_out{k}"], b)
                for c in range(4):
                    mm = nc.tensor.transpose(TB[k][:, c, :], x_in[u][:, (4 * k + c) * P:(4 * k + c + 1) * P], ident[:])
                mm.then_inc(s["gx_T"], 1)

        def pe_gate_up(pe, b, u):
            slot = entry(pe, TAB_SLOT, b, 0, W_IN)
            pe.wait_ge(w_loaded, entry(pe, TAB_NTH, b, 1, NE) * 32)
            for k in range(2):
                pe.wait_ge(s[f"gx_out{k}"], b + 1)
            after(pe, s["hb_ready"], b - 1)
            for k in range(KD):
                mm = nc.tensor.matmul(PB[u][:, :], hT[u][:, k, :], arena[:, bass.ds(slot + k * 2 * DE, 2 * DE)],
                                      start=k == 0, stop=k == KD - 1)
            mm.then_inc(s["gu_full"], 1)

        def pe_table_rows(pe):
            pe.wait_ge(s["tab_cols"], 1)
            pe.wait_ge(s["rank_read"], NT)
            for c in range(4):
                mm = nc.tensor.transpose(MB[0:1, c * P:(c + 1) * P], tcol[:, c:c + 1], ident[:])
            mm.then_inc(s["tab_rows"], 1)
            pe.wait_ge(s["tab_half"], 1)
            nc.tensor.transpose(MB[0:1, 0:P], tcol[:, 4:5], ident[:]).then_inc(s["tab_rows"], 1)

        def pe_phase2(pe):
            pe_table_rows(pe)
            pe.wait_ge(s["smp_masks"], 3)
            for n in range(8):
                after(pe, s["smp_new"], n - 1)
                nc.tensor.matmul(SS[:, n % 2, :], xw[:, (n // 2) * P:(n // 2 + 1) * P],
                                 flat(bmask[:, n // 4, half(n % 2), :]), start=True, stop=True).then_inc(s["states_done"], 1)
            pe.wait_ge(s["stateT_out"], 1)
            pe.wait_ge(s["tables"], 1)
            pe.wait_ge(s["h2T_out"], 2 * NT)
            pe.wait_ge(s["h2_ready"], NT)

            def pair(q, w):
                j = 2 * q + w
                for u in range(2):
                    b = 2 * j + u
                    nj, nu = (j, 1) if u == 0 else (j + 1, 0)
                    pe_gate_up(pe, 2 * nj + nu, nu)
                    pe.wait_ge(s["hb_ready"], b + 1)
                    after(pe, s["hbT_out"], b)
                    for k in range(2):
                        mm = nc.tensor.transpose(YBv[:, k, :], hb2[u][:, k * P:(k + 1) * P], ident[:])
                    mm.then_inc(s["hbT_full"], 1)
                    pe_rows(pe, b + 2, u, j + 1)
                    slot = entry(pe, TAB_SLOT, b, 0, W_IN)
                    pe.wait_ge(wd_loaded, entry(pe, TAB_NTH, b, 1, NE) * 16)
                    pe.wait_ge(s["hbT_out"], b + 1)
                    for n in range(2):
                        after(pe, s[f"dn_out{n}"], b)
                        for k in range(2):
                            mm = nc.tensor.matmul(SS[:, n, :], hTb[:, k, :],
                                                  arena[:, bass.ds(slot + KD * 2 * DE + k * D + n * 512, 512)],
                                                  start=k == 0, stop=k == 1)
                    mm.then_inc(s["dn_full"], 1)
            pe_rows(pe, 0, 0, 0)
            pe_rows(pe, 1, 1, 0)
            pe_gate_up(pe, 0, 0)
            over_pairs(pe, pair)

        def act_phase2(act):
            act.wait_ge(x2_stored, 16 * (NT + 1))
            act.wait_ge(s["tables"], 1)

            def rows0(b, u):
                act.wait_ge(s["gx_T"], 2 * b + 1)
                after(act, s["gu_full"], b)
                nc.scalar.activation(hT[u][:, half(0), :], TB[0][:, :, :], ACT.Copy).then_inc(s["gx_out0"], 1)

            def silu(b, u):
                act.wait_ge(s["gu_full"], b + 2)
                after(act, s["hb_ready"], b - 1)
                nc.scalar.activation(silu_g[u], PB[u][:, 0:DE], ACT.Silu).then_inc(s["silu_out"], 1)

            def pair(q, w):
                j = 2 * q + w
                for u in range(2):
                    b = 2 * j + u
                    act.wait_ge(s["hbT_full"], b + 1)
                    after(act, s["dn_full"], b + 1)
                    nc.scalar.activation(hTb, YBv, ACT.Copy).then_inc(s["hbT_out"], 1)
                    silu(b + 1, 1 - u)
                    rows0(b + 2, u)
                    act.wait_ge(s["dn_full"], b + 2)
                    after(act, added, 16 * (b - 1))
                    nc.scalar.activation(x_res[u][:, 0:512], SS[:, 0, :], ACT.Copy,
                                         scale=weight_of(2 * w + u)).then_inc(s["dn_out0"], 1)
            rows0(0, 0)
            rows0(1, 1)
            silu(0, 0)
            return over_pairs(act, pair)

        def dve_phase2(dve, st):
            def rows1(b, u):
                dve.wait_ge(s["gx_T"], 2 * b + 2)
                after(dve, s["gu_full"], b)
                V.tensor_copy(hT[u][:, half(1), :], TB[1][:, :, :]).then_inc(s["gx_out1"], 1)

            def gate(b, u):
                dve.wait_ge(s["silu_out"], b + 1)
                after(dve, s["hbT_full"], b - 1)
                V.tensor_tensor(hb2[u], silu_g[u], PB[u][:, DE:], ALU.mult).then_inc(s["hb_ready"], 1)

            def pair(q, w):
                j = 2 * q + w
                for u in range(2):
                    b = 2 * j + u
                    gate(b + 1, 1 - u)
                    rows1(b + 2, u)
                    dve.wait_ge(s["dn_full"], b + 2)
                    after(dve, added, 16 * (b - 1))
                    V.tensor_scalar(x_res[u][:, 512:], SS[:, 1, :], weight_of(2 * w + u), None, ALU.mult).then_inc(s["dn_out1"], 1)
            dve.wait_ge(x2_stored, 16 * (NT + 1))
            dve.wait_ge(s["tables"], 1)
            rows1(0, 0)
            rows1(1, 1)
            gate(0, 0)
            return over_pairs(dve, pair)

        LAST = NP // FB

        def over_out(eng, turn):
            for r in range(FB):
                turn(0, r)
            with eng.Fori(1, LAST - 1) as q:
                for r in range(FB):
                    turn(q, r)
            for t in range(NP - FB, NT):
                turn(t // FB, t % FB)

        def whole(eng, used):
            eng.wait_ge(s["gx_T"], 4 * used + 4)
            eng.wait_ge(s["dn_full"], 2 * used + 1)

        def sp_phase3(sp):
            used = pairs_used(sp)
            sp.wait_ge(added, 32 * used)
            whole(sp, used)
            for r in range(FB):
                load_row(sp, 0, r)

            def turn(q, r):
                t = FB * q + r
                sp.wait_ge(s["fin_out"], t + 1)
                known = isinstance(t, int)
                out = y_sample.rearrange("b l d -> (b l) d") if known and t == NP else at_tile(y_tiles, t)
                sp.dma_start(out, fin_o[r % 2]).then_inc(fy_stored[r % 2], 16)
                if not known or t + FB <= NP:
                    load_row(sp, q + 1, r)
            over_out(sp, turn)
            for u in range(2):
                sp.wait_ge(fy_stored[u], 16 * (NP // 2 + 1 - u))
            for sm, n in ((convp_stored, 1), (convs_stored, CW), (ssm_stored, 2), (x2_stored, NT + 1), (h2_stored, NT + 1)):
                sp.wait_ge(sm, 16 * n)

        def pool_phase3(pool, used):
            for u in range(2):
                pool.wait_ge(gathered[u], 16 * used + 16 * (2 - u))

            def turn(q, r):
                t = FB * q + r
                o = r % 2
                pool.wait_ge(s["fin_sq"], t + 1)
                after(pool, s["fin_out"], t - 1)
                fence(t, 2)
                nc.gpsimd.tensor_scalar(rs[:, o:o + 1], sq[:, o:o + 1], 1.0 / D, EPS, ALU.mult, ALU.add).then_inc(pool_fin, 1)
                pool.wait_ge(pool_fin, t + 1)
                nc.gpsimd.tensor_tensor(rs[:, o:o + 1], rs[:, o:o + 1], neg_half[:, 0:1], ALU.pow).then_inc(s["fin_r"], 1)
            fence(used, 3)
            over_out(pool, turn)

        def act_phase3(act, used):
            def turn(q, r):
                t = FB * q + r
                act.wait_ge(fx_loaded[r], 16 * (q + 1))
                after(act, s["fin_r"], t - 1)
                after(act, s["fin_sq"], t)
                nc.scalar.activation(fin_s, x_row[r], ACT.Square, accum_out=sq[:, r % 2:r % 2 + 1]).then_inc(s["fin_sq"], 1)
            over_out(act, turn)

        def dve_phase3(dve, used):
            def turn(q, r):
                t = FB * q + r
                o = r % 2
                dve.wait_ge(fx_loaded[r], 16 * (q + 1))
                dve.wait_ge(s["fin_r"], t + 1)
                after(dve, fy_stored[o], 16 * (2 * q + r // 2))
                V.scalar_tensor_tensor(out=fin_o[o], in0=x_row[r], scalar=rs[:, o:o + 1], in1=gf_b,
                                       op0=ALU.mult, op1=ALU.mult).then_inc(s["fin_out"], 1)
            dve.wait_ge(gf_loaded, 16)
            over_out(dve, turn)

        block = ctx.enter_context(nc.Block())

        @block.tensor
        def _(pe):
            pe_phase1(pe)
            pe_phase2(pe)

        @block.scalar
        def _(act):
            act_phase1(act)
            act_phase3(act, act_phase2(act))

        @block.vector
        def _(dve):
            st = dve_phase1(dve)
            dve_tables(dve, st)
            dve_sample_states(dve, st)
            dve_phase3(dve, dve_phase2(dve, st))

        @block.gpsimd
        def _(pool):
            st = pool_phase1(pool)
            pool_phase3(pool, pool_phase2(pool))

        @block.sync
        def _(sp):
            sp_phase1(sp)
            sp_phase2(sp)
            sp_phase3(sp)


_INS = ["x_prompt", "x_sample", "cache_conv", "state_ssm", "norm1_g", "w_in", "conv_w", "conv_b", "dt_bias", "a_log",
        "d_skip", "ssm_norm_g", "ln_v_g", "ln_v_b", "w_spatial", "b_spatial", "w_out", "norm2_g",
        "w_router_group", "b_router_group", "w_router_expert", "b_router_expert", "w_gate", "w_up", "w_down",
        "final_norm_g"]
_OUTS = [(1, SEQ, D), (SB, SL, D), (1, 1, CW - 1, CD), (1, 1, H, HD, N), (1, SB, CW - 1, CD), (1, SB, H, HD, N),
         (1, SB, SL, W)]


def kernel(**inputs):
    import numpy as _np
    import concourse.bacc as _bacc
    from concourse.bass_utils import run_bass_kernel_spmd as _run

    nc = _bacc.Bacc("TRN2", target_bir_lowering=False, num_devices=1)
    arrays, args = {}, []
    for name in _INS:
        a = _np.ascontiguousarray(inputs[name])
        arrays[f"in_{name}"] = a
        args.append(nc.dram_tensor(f"in_{name}", a.shape, mybir.dt.from_np(a.dtype), kind="ExternalInput").ap())
    for i, shape in enumerate(_OUTS):
        args.append(nc.dram_tensor(f"out_{i}", shape, F32, kind="ExternalOutput").ap())
    build(nc, *args)
    r = _run(nc, [arrays], core_ids=[0])
    return tuple(r.results[0][f"out_{i}"] for i in range(len(_OUTS)))
```
